# Optimizing a Trainium2 kernel written in Bass

```python
import jax, jax.numpy as jnp
from jax import lax
import numpy as np

D_MODEL = 1024
BATCH = 1
SEQ = 512
DEPTH = 1

N_MEM = 256
A_HEADS = 8
A_HEAD_DIM = 64
A_WIDTH = A_HEADS * A_HEAD_DIM
IDX_HEADS = 8
IDX_DIM = 64
TOPK_MAX = 256
Q_BLOCK = 128
CONV_WIDTH = 512
CONV_K = 3
X_HEADS = 4
X_HEAD_DIM = D_MODEL // X_HEADS
D_FF = 2816
ROPE_THETA = 10000.0
EPS = 1e-6

SPLITS = (A_WIDTH, A_HEAD_DIM, A_HEAD_DIM, IDX_HEADS * IDX_DIM, IDX_DIM, IDX_HEADS,
          CONV_WIDTH, CONV_WIDTH, CONV_WIDTH, D_MODEL, D_MODEL)
IN_WIDTH = (A_WIDTH + 2 * A_HEAD_DIM + IDX_HEADS * IDX_DIM + IDX_DIM + IDX_HEADS
            + 3 * CONV_WIDTH + 2 * D_MODEL)


def rms_norm(x, g):
    xf = x.astype(jnp.float32)
    y = xf * lax.rsqrt(jnp.mean(xf * xf, axis=-1, keepdims=True) + EPS)
    return (y * g.astype(jnp.float32)).astype(x.dtype)

def rope_tables(seq_len, dim):
    pos = jnp.arange(seq_len, dtype=jnp.float32)
    inv = ROPE_THETA ** (-jnp.arange(0, dim, 2, dtype=jnp.float32) / dim)
    ang = pos[:, None] * inv[None, :]
    return jnp.cos(ang), jnp.sin(ang)

def apply_rope(x, cos, sin):
    xf = x.astype(jnp.float32)
    half = xf.shape[-1] // 2
    x1, x2 = xf[..., :half], xf[..., half:]
    c = cos[None, :, None, :]
    s = sin[None, :, None, :]
    return jnp.concatenate([x1 * c - x2 * s, x2 * c + x1 * s], axis=-1).astype(x.dtype)

def swiglu(x, w1, w3, w2):
    return (jax.nn.silu(x @ w1) * (x @ w3)) @ w2

def dsa_attention(q, k, v, q_idx, k_idx, w_idx):
    b, seq_len, n_heads, head_dim = q.shape
    k_top = min(TOPK_MAX, seq_len // 4)
    n_blocks = seq_len // Q_BLOCK
    key_pos = jnp.arange(seq_len)
    idx_scale = IDX_DIM ** -0.5
    attn_scale = head_dim ** -0.5

    def to_blocks(a):
        return a.reshape((b, n_blocks, Q_BLOCK) + a.shape[2:]).swapaxes(0, 1)

    def block(args):
        qb, qib, wb, t0 = args
        qpos = t0 + jnp.arange(Q_BLOCK)
        raw = jnp.einsum('bqhd,bsd->bqhs', qib, k_idx).astype(jnp.float32) * idx_scale
        score = jnp.einsum('bqhs,bqh->bqs', jax.nn.relu(raw), wb.astype(jnp.float32))
        causal = key_pos[None, :] <= qpos[:, None]
        score = jnp.where(causal[None], score, -jnp.inf)
        _, sel = lax.top_k(score, k_top)
        k_sel = jax.vmap(lambda kb, ib: kb[ib])(k, sel)
        v_sel = jax.vmap(lambda vb, ib: vb[ib])(v, sel)
        logits = jnp.einsum('bqhd,bqkd->bqhk', qb, k_sel).astype(jnp.float32) * attn_scale
        valid = (sel <= qpos[None, :, None])[:, :, None, :]
        logits = jnp.where(valid, logits, -jnp.inf)
        p = jax.nn.softmax(logits, axis=-1)
        return jnp.einsum('bqhk,bqkd->bqhd', p.astype(v.dtype), v_sel)

    outs = lax.map(block, (to_blocks(q), to_blocks(q_idx), to_blocks(w_idx),
                           jnp.arange(n_blocks) * Q_BLOCK))
    return outs.swapaxes(0, 1).reshape(b, seq_len, n_heads * head_dim)

def short_conv_causal(z, conv_w):
    c = z.shape[-1]
    kern = conv_w.reshape(CONV_K, 1, c).astype(z.dtype)
    return lax.conv_general_dilated(z, kern, window_strides=(1,), padding=[(CONV_K - 1, 0)],
                                    dimension_numbers=('NWC', 'WIO', 'NWC'),
                                    feature_group_count=c)

def memory_cross_attention(h, mem_n, w_q, w_kv, w_o):
    b, s, _ = h.shape
    m = mem_n.shape[1]
    q = (h @ w_q).reshape(b, s, X_HEADS, X_HEAD_DIM)
    kv = (mem_n @ w_kv).reshape(b, m, 2, X_HEADS, X_HEAD_DIM)
    k, v = kv[:, :, 0], kv[:, :, 1]
    logits = jnp.einsum('bshd,bmhd->bhsm', q, k).astype(jnp.float32) * (X_HEAD_DIM ** -0.5)
    p = jax.nn.softmax(logits, axis=-1)
    o = jnp.einsum('bhsm,bmhd->bshd', p.astype(v.dtype), v)
    return o.reshape(b, s, D_MODEL) @ w_o

def first_inputs(seed: int = 0) -> dict:
    key = jax.random.key(seed)
    ks = iter(jax.random.split(key, 32))

    def w(shape, fan_in):
        return jax.random.normal(next(ks), (DEPTH,) + shape, jnp.float32) * fan_in ** -0.5

    def gain(n):
        return 1.0 + 0.05 * jax.random.normal(next(ks), (DEPTH, n), jnp.float32)

    x = jax.random.normal(next(ks), (BATCH, SEQ, D_MODEL), jnp.float32)
    mem = jax.random.normal(next(ks), (BATCH, N_MEM, D_MODEL), jnp.float32)
    return {
        "x": x,
        "mem": mem,
        "ffn1_pre_g": gain(D_MODEL),
        "ffn1_post_g": gain(D_MODEL),
        "ffn1_w1": w((D_MODEL, D_FF), D_MODEL),
        "ffn1_w3": w((D_MODEL, D_FF), D_MODEL),
        "ffn1_w2": w((D_FF, D_MODEL), D_FF),
        "mix_pre_g": gain(D_MODEL),
        "mix_post_g": gain(D_MODEL),
        "w_in": w((D_MODEL, IN_WIDTH), D_MODEL),
        "conv_w": w((CONV_K, CONV_WIDTH), CONV_K),
        "w_a_out": w((A_WIDTH, D_MODEL), A_WIDTH),
        "w_b_out": w((CONV_WIDTH, D_MODEL), CONV_WIDTH),
        "w_out": w((D_MODEL, D_MODEL), D_MODEL),
        "mem_g": gain(D_MODEL),
        "xattn_pre_g": gain(D_MODEL),
        "xattn_post_g": gain(D_MODEL),
        "xattn_w_q": w((D_MODEL, D_MODEL), D_MODEL),
        "xattn_w_kv": w((D_MODEL, 2 * D_MODEL), D_MODEL),
        "xattn_w_o": w((D_MODEL, D_MODEL), D_MODEL),
        "ffn2_pre_g": gain(D_MODEL),
        "ffn2_post_g": gain(D_MODEL),
        "ffn2_w1": w((D_MODEL, D_FF), D_MODEL),
        "ffn2_w3": w((D_MODEL, D_FF), D_MODEL),
        "ffn2_w2": w((D_FF, D_MODEL), D_FF),
    }

def first_block(x, mem, ffn1_pre_g, ffn1_post_g, ffn1_w1, ffn1_w3, ffn1_w2,
              mix_pre_g, mix_post_g, w_in, conv_w, w_a_out, w_b_out, w_out,
              mem_g, xattn_pre_g, xattn_post_g, xattn_w_q, xattn_w_kv, xattn_w_o,
              ffn2_pre_g, ffn2_post_g, ffn2_w1, ffn2_w3, ffn2_w2):
    b, seq_len, _ = x.shape
    cos_a, sin_a = rope_tables(seq_len, A_HEAD_DIM)
    cos_i, sin_i = rope_tables(seq_len, IDX_DIM)
    split_points = np.cumsum(np.array(SPLITS))[:-1].tolist()
    h = x
    for l in range(DEPTH):
        f = swiglu(rms_norm(h, ffn1_pre_g[l]), ffn1_w1[l], ffn1_w3[l], ffn1_w2[l])
        h = h + 0.5 * rms_norm(f, ffn1_post_g[l])

        u = rms_norm(h, mix_pre_g[l])
        proj = u @ w_in[l]
        (q_a, k_a, v_a, q_i, k_i, w_i, gate_b, gate_c, conv_in,
         g_a, g_b) = jnp.split(proj, split_points, axis=-1)

        q_a = apply_rope(q_a.reshape(b, seq_len, A_HEADS, A_HEAD_DIM), cos_a, sin_a)
        k_a = apply_rope(k_a[:, :, None, :], cos_a, sin_a)[:, :, 0]
        q_i = apply_rope(q_i.reshape(b, seq_len, IDX_HEADS, IDX_DIM), cos_i, sin_i)
        k_i = apply_rope(k_i[:, :, None, :], cos_i, sin_i)[:, :, 0]
        w_i = w_i * (IDX_HEADS ** -0.5)
        y_a = dsa_attention(q_a, k_a, v_a, q_i, k_i, w_i) @ w_a_out[l]

        z = short_conv_causal(gate_c * conv_in, conv_w[l])
        y_b = (gate_b * z) @ w_b_out[l]

        merged = jax.nn.sigmoid(g_a) * y_a + jax.nn.sigmoid(g_b) * y_b
        h = h + rms_norm(merged @ w_out[l], mix_post_g[l])

        c = memory_cross_attention(rms_norm(h, xattn_pre_g[l]), rms_norm(mem, mem_g[l]),
                                   xattn_w_q[l], xattn_w_kv[l], xattn_w_o[l])
        h = h + rms_norm(c, xattn_post_g[l])

        f = swiglu(rms_norm(h, ffn2_pre_g[l]), ffn2_w1[l], ffn2_w3[l], ffn2_w2[l])
        h = h + 0.5 * rms_norm(f, ffn2_post_g[l])
    return h


GRID_W = 64
H_A = 8
QK_NOPE = 64
QK_ROPE = 32
V_DIM_A = 64
Q_LORA = 256
KV_LORA = 128
H_B = 8
KV_B = 2
HD_B = 64
D_FF_2 = 4 * D_MODEL
PLE_DIM = 256
IN_SPLITS = [Q_LORA, KV_LORA + QK_ROPE, H_B * HD_B, KV_B * HD_B, KV_B * HD_B, D_MODEL, D_MODEL]
D_IN = sum(IN_SPLITS)


def rmsnorm(x, g):
    xf = x.astype(jnp.float32)
    y = xf * lax.rsqrt(jnp.mean(xf * xf, axis=-1, keepdims=True) + EPS)
    return (y * g.astype(jnp.float32)).astype(x.dtype)

def rope_angles(pos, dim):
    inv = ROPE_THETA ** (-jnp.arange(0, dim, 2, dtype=jnp.float32) / dim)
    return pos.astype(jnp.float32)[:, None] * inv[None, :]

def apply_rope_2(x, ang):
    cos = jnp.cos(ang)[None, :, None, :].astype(x.dtype)
    sin = jnp.sin(ang)[None, :, None, :].astype(x.dtype)
    x1, x2 = jnp.split(x, 2, axis=-1)
    return jnp.concatenate([x1 * cos - x2 * sin, x1 * sin + x2 * cos], axis=-1)

def blocked_attention(q, k, v):
    B, S, Hk, G, dk = q.shape
    nb = S // Q_BLOCK
    qb = q.reshape(B, nb, Q_BLOCK, Hk, G, dk).transpose(1, 0, 2, 3, 4, 5)

    def one_block(qblk):
        s = jnp.einsum("bqhgd,bkhd->bhgqk", qblk, k).astype(jnp.float32)
        pr = jax.nn.softmax(s, axis=-1).astype(v.dtype)
        return jnp.einsum("bhgqk,bkhd->bqhgd", pr, v)

    o = lax.map(one_block, qb)
    return o.transpose(1, 0, 2, 3, 4, 5).reshape(B, S, Hk * G, v.shape[-1])

def second_inputs(seed: int = 0) -> dict:
    key = jax.random.key(seed)
    ks = jax.random.split(key, 24)
    f32 = jnp.float32

    def w(k, shape, fan_in):
        return jax.random.normal(k, shape, f32) * (fan_in ** -0.5)

    def gain(k, shape):
        return 1.0 + 0.05 * jax.random.normal(k, shape, f32)

    L = DEPTH
    return {
        "x": jax.random.normal(ks[0], (BATCH, SEQ, D_MODEL), f32),
        "p": jax.random.normal(ks[1], (DEPTH, BATCH, SEQ, PLE_DIM), f32),
        "g_mix": gain(ks[2], (L, D_MODEL)),
        "w_in": w(ks[3], (L, D_MODEL, D_IN), D_MODEL),
        "g_qa": gain(ks[4], (L, Q_LORA)),
        "w_qb": w(ks[5], (L, Q_LORA, H_A * (QK_NOPE + QK_ROPE)), Q_LORA),
        "g_kva": gain(ks[6], (L, KV_LORA)),
        "w_kvb": w(ks[7], (L, KV_LORA, H_A * (QK_NOPE + V_DIM_A)), KV_LORA),
        "g_qn": gain(ks[8], (L, HD_B)),
        "g_kn": gain(ks[9], (L, HD_B)),
        "w_oa": w(ks[10], (L, H_A * V_DIM_A, D_MODEL), H_A * V_DIM_A),
        "w_ob": w(ks[11], (L, H_B * HD_B, D_MODEL), H_B * HD_B),
        "w_o": w(ks[12], (L, D_MODEL, D_MODEL), D_MODEL),
        "g_mlp": gain(ks[13], (L, D_MODEL)),
        "w_up": w(ks[14], (L, D_MODEL, D_FF_2), D_MODEL),
        "w_down": w(ks[15], (L, D_FF_2, D_MODEL), D_FF_2),
        "g_ple": gain(ks[16], (L, D_MODEL)),
        "w_ple_gate": w(ks[17], (L, D_MODEL, D_MODEL), D_MODEL),
        "w_ple": w(ks[18], (L, PLE_DIM, D_MODEL), PLE_DIM),
        "g_final": gain(ks[19], (D_MODEL,)),
    }

def second_block(x, p, g_mix, w_in, g_qa, w_qb, g_kva, w_kvb, g_qn, g_kn, w_oa, w_ob, w_o,
              g_mlp, w_up, w_down, g_ple, w_ple_gate, w_ple, g_final):
    B, S, D = x.shape
    ROWS = S // GRID_W
    t = jnp.arange(S)
    row = jnp.broadcast_to(jnp.arange(ROWS)[:, None], (ROWS, GRID_W)).reshape(-1)
    col = jnp.broadcast_to(jnp.arange(GRID_W)[None, :], (ROWS, GRID_W)).reshape(-1)
    ang_1d = rope_angles(t, QK_ROPE)
    ang_row = rope_angles(row, HD_B // 2)
    ang_col = rope_angles(col, HD_B // 2)
    split_idx = list(np.cumsum(IN_SPLITS)[:-1])
    scale_a = (QK_NOPE + QK_ROPE) ** -0.5
    scale_b = HD_B ** -0.5

    for i in range(DEPTH):
        h = rmsnorm(x, g_mix[i])
        z = jnp.einsum("bsd,de->bse", h, w_in[i])
        q_lat, kv_lat, qb, kb, vb, gate_a, gate_b = jnp.split(z, split_idx, axis=-1)

        cq = rmsnorm(q_lat, g_qa[i])
        qa = jnp.einsum("bsr,re->bse", cq, w_qb[i]).reshape(B, S, H_A, QK_NOPE + QK_ROPE)
        qa_nope, qa_rope = jnp.split(qa, [QK_NOPE], axis=-1)
        qa_rope = apply_rope_2(qa_rope, ang_1d)
        c_kv, k_pe = jnp.split(kv_lat, [KV_LORA], axis=-1)
        c_kv = rmsnorm(c_kv, g_kva[i])
        k_pe = apply_rope_2(k_pe[:, :, None, :], ang_1d)
        kva = jnp.einsum("bsr,re->bse", c_kv, w_kvb[i]).reshape(B, S, H_A, QK_NOPE + V_DIM_A)
        ka_nope, va = jnp.split(kva, [QK_NOPE], axis=-1)
        qa_full = (jnp.concatenate([qa_nope, qa_rope], axis=-1) * scale_a)[:, :, :, None, :]
        ka_full = jnp.concatenate([ka_nope, jnp.broadcast_to(k_pe, (B, S, H_A, QK_ROPE))], axis=-1)
        oa = blocked_attention(qa_full, ka_full, va).reshape(B, S, H_A * V_DIM_A)
        ya = jnp.einsum("bse,ed->bsd", oa, w_oa[i])

        qb = rmsnorm(qb.reshape(B, S, H_B, HD_B), g_qn[i])
        kb = rmsnorm(kb.reshape(B, S, KV_B, HD_B), g_kn[i])
        vb = vb.reshape(B, S, KV_B, HD_B)
        qr, qc = jnp.split(qb, 2, axis=-1)
        qb = jnp.concatenate([apply_rope_2(qr, ang_row), apply_rope_2(qc, ang_col)], axis=-1)
        kr, kc = jnp.split(kb, 2, axis=-1)
        kb = jnp.concatenate([apply_rope_2(kr, ang_row), apply_rope_2(kc, ang_col)], axis=-1)
        qb = (qb * scale_b).reshape(B, S, KV_B, H_B // KV_B, HD_B)
        ob = blocked_attention(qb, kb, vb).reshape(B, S, H_B * HD_B)
        yb = jnp.einsum("bse,ed->bsd", ob, w_ob[i])

        merged = jax.nn.sigmoid(gate_a) * ya + jax.nn.sigmoid(gate_b) * yb
        x = x + jnp.einsum("bsd,de->bse", merged, w_o[i])

        h2 = rmsnorm(x, g_mlp[i])
        u = jax.nn.relu(jnp.einsum("bsd,df->bsf", h2, w_up[i]))
        x = x + jnp.einsum("bsf,fd->bsd", u * u, w_down[i])

        h3 = rmsnorm(x, g_ple[i])
        gate = jax.nn.sigmoid(jnp.einsum("bsd,de->bse", h3, w_ple_gate[i]))
        x = x + gate * jnp.einsum("bsk,kd->bsd", p[i], w_ple[i])

    return rmsnorm(x, g_final)


def setup_inputs(seed=0):
    out = dict(first_inputs(seed))
    for name, value in second_inputs(seed + 1).items():
        if name != "x":
            out[name + "_2"] = value
    return out


def reference(
    x, mem, ffn1_pre_g, ffn1_post_g, ffn1_w1, ffn1_w3, ffn1_w2, mix_pre_g, mix_post_g, w_in,
    conv_w, w_a_out, w_b_out, w_out, mem_g, xattn_pre_g, xattn_post_g, xattn_w_q, xattn_w_kv,
    xattn_w_o, ffn2_pre_g, ffn2_post_g, ffn2_w1, ffn2_w3, ffn2_w2, p_2, g_mix_2, w_in_2, g_qa_2,
    w_qb_2, g_kva_2, w_kvb_2, g_qn_2, g_kn_2, w_oa_2, w_ob_2, w_o_2, g_mlp_2, w_up_2, w_down_2,
    g_ple_2, w_ple_gate_2, w_ple_2, g_final_2,
):
    x = first_block(
        x, mem, ffn1_pre_g, ffn1_post_g, ffn1_w1, ffn1_w3, ffn1_w2, mix_pre_g, mix_post_g, w_in,
        conv_w, w_a_out, w_b_out, w_out, mem_g, xattn_pre_g, xattn_post_g, xattn_w_q,
        xattn_w_kv, xattn_w_o, ffn2_pre_g, ffn2_post_g, ffn2_w1, ffn2_w3, ffn2_w2,
    )
    return second_block(
        x, p_2, g_mix_2, w_in_2, g_qa_2, w_qb_2, g_kva_2, w_kvb_2, g_qn_2, g_kn_2, w_oa_2,
        w_ob_2, w_o_2, g_mlp_2, w_up_2, w_down_2, g_ple_2, w_ple_gate_2, w_ple_2, g_final_2,
    )


_drawn_inputs = setup_inputs


def setup_inputs(seed=0):
    import zlib

    import numpy as np

    out = dict(_drawn_inputs(seed))
    spreads = {}
    factors = {'ffn2_pre_g': 3.014,
     'ffn2_post_g': 4.015,
     'g_mix_2': 7.441,
     'g_qa_2': 8.0,
     'g_kva_2': 8.0,
     'g_qn_2': 8.0,
     'g_kn_2': 8.0,
     'g_ple_2': 200.0,
     'g_mlp_2': 6.025,
     'p_2': 3.69,
     'w_ple_gate_2': 5.183,
     'w_ple_2': 3.689}
    for name, (base, spread) in spreads.items():
        noise = np.random.default_rng([zlib.crc32(name.encode()), seed]).standard_normal(out[name].shape)
        drawn = base * np.exp(spread * noise) if base else spread * noise
        out[name] = __import__('jax').numpy.asarray(drawn.astype(out[name].dtype))
    for name, factor in factors.items():
        out[name] = (out[name] * factor).astype(out[name].dtype)
    return out
```

```python
from contextlib import ExitStack

import numpy as np

import concourse.bass as bass
from concourse import mybir

F32 = mybir.dt.float32
F32R = mybir.dt.float32r
I32 = mybir.dt.int32
ALU = mybir.AluOpType
ACT = mybir.ActivationFunctionType
AX = mybir.AxisListType

P = 128
T = 512
TB = T // P
D = 1024
KC = D // P
N_MEM = 256
MB = N_MEM // P
FF = 2816 // P
FF_A, FF_B = 16, 6
FF2 = 4096 // P
FF2_HALF = FF2 // 2
HEADS = 8
HD = 64
TOP_K = 128
LAT_Q, LAT_KV, ROPE_D, NOPE = 256, 128, 32, 64
QW = NOPE + ROPE_D
XH, XD = 4, 256
PLE = 256
EPS = 1e-6
RSQRT_SEED = float(0x5F3759DF)
NEWTON_STEPS = 3
RING = 4
LOOKAHEAD = 3
UNIT = 1024
REPLACED = -(2.0 ** 127)
NOT_CAUSAL = -(2.0 ** 126)
MASKED = -(2.0 ** 100)

C_QA, C_KA, C_VA, C_QI, C_KI, C_WI = 0, 512, 576, 640, 1152, 1216
C_GB, C_GC, C_CI, C_GA, C_GBB = 1224, 1736, 2248, 2760, 3784
Z_QL, Z_KVL, Z_KPE, Z_QB, Z_KB, Z_VB, Z_GA, Z_GB = 0, 256, 384, 416, 928, 1056, 1184, 2208

GAINS = ["ffn1_pre_g", "ffn1_post_g", "mix_pre_g", "mix_post_g", "mem_g", "xattn_pre_g", "xattn_post_g",
         "ffn2_pre_g", "ffn2_post_g", "g_mix_2", "g_mlp_2", "g_ple_2", "g_final_2"]
G_QA_ROW = len(GAINS) * KC
G_KVA_ROW = G_QA_ROW + LAT_Q // P
CONV_ROW = G_KVA_ROW + 1
G_QN_ROW = CONV_ROW + 3 * 4
G_KN_ROW = G_QN_ROW + 1
GAIN_ROWS = G_KN_ROW + 1

STEPS = [("ffn1_up_a", 2 * FF_A), ("ffn1_down_a", 2 * KC), ("ffn1_up_b", 2 * FF_B), ("ffn1_down_b", KC),
         ("conv", 12), ("merge_conv", 12), ("index", 5), ("values", 1), ("queries", 5), ("gate_a", 8),
         ("attn_out", 4), ("mix_out", 8),
         ("mem_k", 8), ("mem_v", 8), ("x_q", 8), ("x_out", 8),
         ("ffn2_up_a", 2 * FF_A), ("ffn2_down_a", 2 * KC), ("ffn2_up_b", 2 * FF_B), ("ffn2_down_b", KC),
         ("grouped", 7), ("latent", 4), ("latent_heads", 4), ("merge", 24), ("out", 8),
         ("mlp_up_a", FF2_HALF), ("mlp_down_a", FF2_HALF), ("mlp_up_b", FF2_HALF), ("mlp_down_b", FF2_HALF),
         ("ple", 2), ("ple_gate", 8)]
FIRST = {}
UNITS = 0
for _name, _n in STEPS:
    FIRST[_name] = UNITS
    UNITS += _n
assert UNITS % RING == 0
TWO_PART = [FIRST["index"] + 4, FIRST["values"], FIRST["queries"] + 4, FIRST["grouped"] + 4, FIRST["grouped"] + 5,
            *[FIRST["latent_heads"] + c for c in range(4)]]


def shape_constants():
    i = np.arange(P)
    ident = np.eye(P, dtype=np.float32)

    def rotation(half):
        m = np.zeros((P, P), np.float32)
        first = (i % (2 * half)) < half
        m[i[first] + half, i[first]] = -1.0
        m[i[~first] - half, i[~first]] = 1.0
        return m

    causal = np.where(i[None, :] <= i[:, None], 0.0, 1.0).astype(np.float32)
    heads = np.zeros((P, P), np.float32)
    heads[:HD, 0] = 1.0
    heads[HD:, 1] = 1.0
    mats = np.concatenate([ident, np.ones((P, P), np.float32), rotation(32), rotation(16), causal, heads], 1)

    def angles(pos, dim):
        inv = (10000.0 ** (-(np.arange(0, dim, 2, dtype=np.float32) / np.float32(dim)).astype(np.float64)))
        return pos.astype(np.float32)[:, None] * inv.astype(np.float32)[None, :]

    def tables(ang_rows):
        ang = np.stack(ang_rows).astype(np.float64)
        return np.cos(ang).astype(np.float32), np.sin(ang).astype(np.float32)

    t = np.arange(T)
    a64 = angles(t, 64)
    main = tables([a64[:, p % 32] for p in range(P)])
    a32 = angles(t, ROPE_D)
    lat = tables([a32[:, p % 16] if NOPE <= p < QW else np.zeros(T) for p in range(P)])
    row, col = angles(t // 64, 32), angles(t % 64, 32)
    grid = tables([(row if p % 64 < 32 else col)[:, p % 16] for p in range(P)])
    return mats, np.concatenate([np.stack(x, 1) for x in (main, lat, grid)], 1).reshape(P, 3, 2, T)


GROUPED_ORDER = (4, 5, 0, 1, 2, 3)
IDX_SUM = [n // HEADS * (HEADS + 1) + n % HEADS + 1 for n in range(3 * HEADS)]
CONST_DMAS = 1 + len(GAINS) + 3 + 4


class NormSems:

    def __init__(self, sem):
        self.squares = sem("norm_squares")
        self.summed = sem("norm_summed")
        self.newton = sem("norm_newton")
        self.expand = sem("norm_expand")
        self.spread = sem("norm_spread")
        self.scale = sem("norm_scale")


class Norm:

    def __init__(self, before, chunks, copies, expands=1):
        self.chunks, self.copies, self.expands = chunks, copies, expands
        self.chunk0 = before.chunk0 + before.chunks if before else 0
        self.expand0 = before.expand0 + before.expands if before else 0
        self.scale0 = before.scale0 + before.copies if before else 0
        self.newton0 = before.newton0 + 2 + 3 * NEWTON_STEPS if before else 0


class Split:

    def __init__(self, sem, name):
        self.hi = sem(name + "_hi")
        self.lo = sem(name + "_lo")


class Entry:

    def __init__(self, split, n):
        self.hi, self.lo, self.first = split.hi, split.lo, n * KC


class FfnSems:

    def __init__(self, sem):
        self.gate = sem("ffn_gate")
        self.silu = sem("ffn_silu")
        self.up = sem("ffn_up")
        self.prod = sem("ffn_prod")
        self.hid = Split(sem, "ffn_hid")
        self.part = sem("ffn_part")
        self.full = sem("ffn_full")


class Ffn:

    def __init__(self, n):
        self.hid0, self.out0 = n * FF, n * KC


class Residual:

    def __init__(self, term, h, n):
        self.term = term
        self.h = h
        self.first = n * KC


class Rope:
    def __init__(self, sem, name):
        self.x = sem(name + "_x")
        self.cos = sem(name + "_cos")
        self.rot = sem(name + "_rot")
        self.sin = sem(name + "_sin")
        self.sum = sem(name + "_sum")
        self.out = Split(sem, name + "_out")


class AttentionSems:

    def __init__(self, sem):
        self.logits = sem("att_logits")
        self.top = sem("att_top")
        self.exp = sem("att_exp")
        self.inv = sem("att_inv")
        self.probs = sem("att_probs")
        self.turned = sem("att_turned")
        self.pt = Split(sem, "att_pt")
        self.pv = sem("att_pv")
        self.out = Split(sem, "att_out")


class Attention:

    def __init__(self, block0, piece0):
        self.block0, self.half0, self.piece0 = block0, block0 // 2, piece0


def build(nc, dram, out):
    base = -(-nc.sbuf_base // 32) * 32
    place = [base]

    def fixed(name, shape, dt):
        words = int(np.prod(shape[1:]))
        t = nc.alloc_sbuf_tensor_at(name, shape, dt, offset=place[0])
        place[0] += -(-words * 4 // 32) * 32
        return t

    mats = fixed("mats", [P, 6, P], F32)
    ident, ones, rot32, rot16, after_query, head_sel = (mats[:, n, :] for n in range(6))
    gains = fixed("gains", [P, P], F32)
    tab = fixed("rope_tab", [P, 2, T], F32)
    scale = fixed("scale", [P, T], F32)
    n_x = fixed("newton_x", [P, 48], F32)
    n_y = fixed("newton_y", [P, 48], F32)
    n_t = fixed("newton_t", [P, 48], F32)
    top = fixed("top", [P, 4], F32)
    sums = fixed("sums", [P, 4], F32)
    invs = fixed("invs", [P, 4], F32)
    w_idx = fixed("w_idx", [P, TB, HEADS], F32)
    best8 = fixed("best8", [P, 8], F32)
    mem_sq = fixed("mem_sq", [P, MB], F32)
    h = fixed("h", [P, KC, T], F32)
    mem_rows = nc.alloc_sbuf_tensor_at("mem_rows", [P, MB, D], F32, offset=place[0] + 4 * T * 4)
    xh = fixed("xh", [P, KC, T], F32R)
    mem_squares = nc.alloc_sbuf_tensor_at("mem_squares", [P, D], F32, offset=place[0] + 4 * T * 4)
    xl = fixed("xl", [P, KC, T], F32R)
    raw = fixed("ring_raw", [P, RING, UNIT], F32)
    wh = fixed("ring_hi", [P, RING, UNIT], F32R)
    wl = fixed("ring_lo", [P, RING, UNIT], F32R)
    arena = place[0]
    K = 1024

    def at(name, kib, shape, dt):
        offset = arena + int(kib * K)
        assert offset + int(np.prod(shape[1:])) * 4 <= nc.sbuf_usable_end, name
        return nc.alloc_sbuf_tensor_at(name, shape, dt, offset=offset)

    f = at("f", 0, [P, KC, T], F32)
    squares = at("squares", 80, [P, 2, T], F32)
    wa = at("work_a", 84, [P, 2, T], F32)
    wb = at("work_b", 88, [P, 2, T], F32)
    expand = at("expand", 92, [P, TB, P], F32)
    probs = at("probs", 94, [P, 3, T], F32)
    x_rows = at("x_rows", 16, [P, TB, D], F32)
    gain_rows = at("gain_rows", 32, [P, P], F32)
    hid_h = at("hid_h", 16, [P, FF2_HALF, T], F32R)
    hid_l = at("hid_l", 48, [P, FF2_HALF, T], F32R)
    cz_h = at("cz_h", 16, [P, 4, T], F32R)
    cz_l = at("cz_l", 24, [P, 4, T], F32R)
    c_gb = at("c_gb", 32, [P, 2, T], F32)
    c_gc = at("c_gc", 36, [P, 2, T], F32)
    c_y = at("c_y", 40, [P, 2, T + 8], F32)
    c_z = at("c_z", 45, [P, 2, T], F32)
    mixed = at("mixed", 0, [P, KC, T], F32)
    qa_h = at("qa_h", 16, [P, 4, T], F32R)
    qa_l = at("qa_l", 24, [P, 4, T], F32R)
    qi_h = at("qi_h", 32, [P, 4, T], F32R)
    qi_l = at("qi_l", 40, [P, 4, T], F32R)
    a_pt_h = at("a_pt_h", 32, [P, 2, 4, 256], F32R)
    a_pt_l = at("a_pt_l", 40, [P, 2, 4, 256], F32R)
    ka_h = at("ka_h", 48, [P, T], F32R)
    ka_l = at("ka_l", 50, [P, T], F32R)
    ki_h = at("ki_h", 52, [P, T], F32R)
    ki_l = at("ki_l", 54, [P, T], F32R)
    va_h = at("va_h", 56, [P, TB, 192], F32R)
    va_l = at("va_l", 59, [P, TB, 192], F32R)
    v_rows = at("v_rows", 94, [P, TB, HD], F32)
    mask = at("mask", 62, [P, TB * (TB + 1) // 2 * P], F32)
    gate_a = at("gate_a", 67, [P, KC, T], F32)
    mg_h = at("mg_h", 16, [P, KC, T], F32R)
    mg_l = at("mg_l", 32, [P, KC, T], F32R)
    memt_h = at("memt_h", 48, [P, KC, N_MEM], F32R)
    memt_l = at("memt_l", 56, [P, KC, N_MEM], F32R)
    mk_h = at("mk_h", 32, [P, KC, N_MEM], F32R)
    mk_l = at("mk_l", 40, [P, KC, N_MEM], F32R)
    mv_h = at("mv_h", 16, [P, MB, D], F32R)
    mv_l = at("mv_l", 24, [P, MB, D], F32R)
    xq_h = at("xq_h", 0, [P, KC, T], F32R)
    xq_l = at("xq_l", 48, [P, KC, T], F32R)
    x_pt_h = at("x_pt_h", 64, [P, 2, MB, 256], F32R)
    x_pt_l = at("x_pt_l", 68, [P, 2, MB, 256], F32R)
    go_h = at("go_h", 0, [P, 4, T], F32R)
    go_l = at("go_l", 8, [P, 4, T], F32R)
    gq_h = at("gq_h", 16, [P, 4, T], F32R)
    gq_l = at("gq_l", 24, [P, 4, T], F32R)
    gk_h = at("gk_h", 32, [P, 2, T], F32R)
    gk_l = at("gk_l", 36, [P, 2, T], F32R)
    gv_h = at("gv_h", 40, [P, 2, TB, 192], F32R)
    gv_l = at("gv_l", 46, [P, 2, TB, 192], F32R)
    g_pt_h = at("g_pt_h", 52, [P, 2, 4, 256], F32R)
    g_pt_l = at("g_pt_l", 60, [P, 2, 4, 256], F32R)
    g_x = at("g_x", 68, [P, 6, T], F32)
    g_v = at("g_v", 94, [P, TB, P], F32)
    cq_h = at("cq_h", 16, [P, 2, T], F32R)
    cq_l = at("cq_l", 20, [P, 2, T], F32R)
    ck_h = at("ck_h", 24, [P, T], F32R)
    ck_l = at("ck_l", 26, [P, T], F32R)
    lq_h = at("lq_h", 28, [P, 2, T], F32R)
    lq_l = at("lq_l", 32, [P, 2, T], F32R)
    lk_h = at("lk_h", 36, [P, 2, T], F32R)
    lk_l = at("lk_l", 40, [P, 2, T], F32R)
    lv_h = at("lv_h", 44, [P, TB, 192], F32R)
    lv_l = at("lv_l", 47, [P, TB, 192], F32R)
    l_pt_h = at("l_pt_h", 50, [P, 2, 4, 256], F32R)
    l_pt_l = at("l_pt_l", 58, [P, 2, 4, 256], F32R)
    l_x = at("l_x", 66, [P, 4, T], F32)
    l_q = at("l_q", 84, [P, 2, T], F32)
    lo_h = at("lo_h", 66, [P, 4, T], F32R)
    lo_l = at("lo_l", 74, [P, 4, T], F32R)
    p_rows = at("p_rows", 0, [P, TB, PLE], F32)
    pt_h = at("pt_h", 4, [P, 2, T], F32R)
    pt_l = at("pt_l", 8, [P, 2, T], F32R)
    ple = at("ple", 16, [P, KC, T], F32)
    normed = at("normed", 0, [P, KC, T], F32)
    out_rows = at("out_rows", 32, [P, TB, D], F32)

    def mask_of(b):
        lo = b * (b + 1) // 2 * P
        return mask[:, lo:lo + (b + 1) * P]

    def gain(name, k):
        row = GAINS.index(name) * KC + k
        return gains[:, row:row + 1]

    def gain_row(row):
        return gains[:, row:row + 1]

    with ExitStack() as ctx:
        def sem(name):
            return ctx.enter_context(nc.semaphore(name))

        bank = [ctx.enter_context(nc.psum_tensor(f"bank{n}", [P, T], F32)) for n in range(8)]
        SPREAD, SUMS = 6, 7

        raw_in = [sem(f"raw_in{s}") for s in range(RING)]
        hi_ready = sem("hi_ready")
        lo_ready = sem("lo_ready")
        unit_used = sem("unit_used")
        const_in = sem("const_in")
        x_in = sem("x_in")
        mem_in = sem("mem_in")
        p_in = sem("p_in")
        tab_in = sem("tab_in")
        out_sent = sem("out_sent")
        gains_turned = sem("gains_turned")
        gains_kept = sem("gains_kept")
        x_turned = sem("x_turned")
        x_kept = sem("x_kept")
        norm = NormSems(sem)
        n_ffn1 = Norm(None, KC, 1)
        n_ffn1p = Norm(n_ffn1, KC, 0)
        n_mix = Norm(n_ffn1p, KC, 1)
        n_mixp = Norm(n_mix, KC, 0)
        n_xq = Norm(n_mixp, KC, 1)
        n_xp = Norm(n_xq, KC, 0)
        n_ffn2 = Norm(n_xp, KC, 1)
        n_ffn2p = Norm(n_ffn2, KC, 0)
        n_mix2 = Norm(n_ffn2p, KC, 1)
        n_heads = Norm(n_mix2, 6, 0, expands=6)
        n_cq = Norm(n_heads, LAT_Q // P, 0)
        n_ckv = Norm(n_cq, 1, 0)
        n_mlp = Norm(n_ckv, KC, 1)
        n_ple = Norm(n_mlp, KC, 1)
        n_end = Norm(n_ple, KC, 0)
        n_mem = sem("n_mem")
        entry = Split(sem, "entry")
        x_ffn1, x_mix, x_x, x_ffn2, x_mix2, x_mlp, x_ple = (Entry(entry, n) for n in range(7))
        ffn = FfnSems(sem)
        ffn1, ffn2 = Ffn(0), Ffn(1)
        normed_term, h_added = sem("normed_term"), sem("h_added")
        r_ffn1, r_mix, r_x, r_ffn2 = (Residual(normed_term, h_added, n) for n in range(4))
        conv_step = sem("conv_step")
        conv_tap = sem("conv_tap")
        conv_out = Split(sem, "conv_out")
        mc_gate, mc_sig, mc_sum = sem("mc_gate"), sem("mc_sig"), sem("mc_sum")
        rope = Rope(sem, "rope")
        v_scaled, v_split = sem("v_scaled"), Split(sem, "v_split")
        v_zero = sem("v_zero")
        idx_raw, idx_relu, idx_sum = sem("idx_raw"), sem("idx_relu"), sem("idx_sum")
        taken = sem("taken")
        masked = sem("masked")
        ga_scaled, ga_sig = sem("ga_scaled"), sem("ga_sig")
        att = AttentionSems(sem)
        HB = HEADS * TB
        a_main, a_mem = Attention(0, 0), Attention(HB, HEADS)
        a_grp = Attention(HB + XH * TB, HEADS + 4 * XH)
        a_lat = Attention(2 * HB + XH * TB, 2 * HEADS + 4 * XH)
        ma_term, ma_sum, merged = sem("ma_term"), sem("ma_sum"), Split(sem, "merged")
        mo_full = sem("mo_full")
        mem_sum, mem_normed, mem_turned = sem("mem_sum"), sem("mem_normed"), sem("mem_turned")
        memt, mk, mv = Split(sem, "memt"), Split(sem, "mk"), Split(sem, "mv")
        xq_scaled, xq = sem("xq_scaled"), Split(sem, "xq")
        xo_full = sem("xo_full")
        gx, gx_normed = Rope(sem, "gx"), sem("gx_normed")
        gv_scaled, gv = sem("gv_scaled"), Split(sem, "gv")
        lx, l_normed, l_lat = sem("lx"), sem("l_normed"), Split(sem, "l_lat")
        kpe = Rope(sem, "kpe")
        lq, lk, lv = Rope(sem, "lq"), Split(sem, "lk"), Split(sem, "lv")
        me_gate, me_sig, me_term, me_sum = sem("me_gate"), sem("me_sig"), sem("me_term"), sem("me_sum")
        merged2 = Split(sem, "merged2")
        h_out = sem("h_out")
        p_turned, p_split = sem("p_turned"), Split(sem, "p_split")
        ml_x, ml_sq, ml_hid = sem("ml_x"), sem("ml_sq"), Split(sem, "ml_hid")
        ml_part, h_mlp = sem("ml_part"), sem("h_mlp")
        ple_kept, pg_x, pg_sig, pg_term, h_end = (sem(n) for n in ("ple_kept", "pg_x", "pg_sig", "pg_term", "h_end"))
        end_normed, end_turned, end_kept = sem("end_normed"), sem("end_turned"), sem("end_kept")

        block = ctx.enter_context(nc.Block())

        def landed(u):
            return 16 * (u // RING + 1 + sum(v <= u and v % RING == u % RING for v in TWO_PART))

        def done(u, i=None):
            return u + 2 if i is None else 4 * i + (u + 2)

        @block.sync
        def _(sp):
            def load(u, src, width, i=None, at_col=0):
                if i is not None:
                    sp.wait_ge(lo_ready, 4 * i + (u - RING + 1))
                elif u >= RING:
                    sp.wait_ge(lo_ready, u - RING + 1)
                dst = raw[:, u % RING, at_col:at_col + src.shape[1] * width].rearrange("p (k c) -> p k c", c=width)
                return sp.dma_start(dst, src)

            def rows(name, c0, width=P, k0=0, nk=KC):
                w = dram[name][0][k0 * P:(k0 + nk) * P]
                return w.rearrange("(k p) c -> p k c", p=P)[:, :, c0:c0 + width]

            def rows_at(name, c0, width=P, k0=0, nk=KC):
                w = dram[name][0][k0 * P:(k0 + nk) * P]
                return w.rearrange("(k p) c -> p k c", p=P)[:, :, bass.ds(c0, width)]

            def fetch(u, src, width):
                load(u, src, width).then_inc(raw_in[u % RING], 16)

            def loop(first, turns, source, peel=False):
                def turn(i, static):
                    for q in range(RING):
                        load(first + q, source(i, q), P, None if static else i).then_inc(raw_in[(first + q) % RING], 16)
                if peel:
                    turn(0, True)
                with sp.Fori(1 if peel else 0, turns) as i:
                    turn(i, False)

            def feed_forward(name):
                w1, w3, w2 = name + "_w1", name + "_w3", name + "_w2"

                def up(j0):
                    return lambda i, q: rows_at((w1, w3)[q % 2], i * (2 * P) + (j0 + q // 2) * P)
                loop(FIRST[name + "_up_a"], FF_A // 2, up(0), peel=FIRST[name + "_up_a"] == 0)
                loop(FIRST[name + "_down_a"], KC // 2, lambda i, q: rows_at(w2, i * (2 * P) + q // 2 * P, k0=q % 2 * KC))
                loop(FIRST[name + "_up_b"], FF_B // 2, up(FF_A))
                loop(FIRST[name + "_down_b"], KC // RING, lambda i, q: rows_at(w2, i * (4 * P) + q * P, k0=FF_A, nk=FF_B))

            feed_forward("ffn1")
            u = FIRST["conv"]
            for j in range(4):
                for q, c in enumerate((C_GB, C_GC, C_CI)):
                    fetch(u + 3 * j + q, rows("w_in", c + j * P), P)
            u = FIRST["merge_conv"]
            for p in range(4):
                fetch(u + 3 * p, rows("w_b_out", 2 * P * p, 2 * P, nk=4), 2 * P)
                for q in range(2):
                    fetch(u + 3 * p + 1 + q, rows("w_in", C_GBB + (2 * p + q) * P), P)

            def fetch_twin(u, name, c0):
                dst = raw[:, u % RING, :].rearrange("p (k c) -> p k c", c=P)
                sp.wait_ge(lo_ready, u - RING + 1)
                sp.dma_start(dst[:, :, 0:HD], rows(name, c0, HD)).then_inc(raw_in[u % RING], 16)
                sp.dma_start(dst[:, :, HD:P], rows(name, c0, HD)).then_inc(raw_in[u % RING], 16)

            u = FIRST["index"]
            for c in range(4):
                fetch(u + c, rows("w_in", C_QI + c * P), P)
            fetch_twin(u + 4, "w_in", C_KI)
            u = FIRST["values"]
            dst = raw[:, u % RING, :].rearrange("p (k c) -> p k c", c=P)
            sp.wait_ge(lo_ready, u - RING + 1)
            sp.dma_start(dst[:, :, 0:HD], rows("w_in", C_VA, HD)).then_inc(raw_in[u % RING], 16)
            sp.dma_start(dst[:, :, HD:HD + HEADS], rows("w_in", C_WI, HEADS)).then_inc(raw_in[u % RING], 16)
            u = FIRST["queries"]
            for c in range(4):
                fetch(u + c, rows("w_in", C_QA + c * P), P)
            fetch_twin(u + 4, "w_in", C_KA)
            for m in range(KC):
                fetch(FIRST["gate_a"] + m, rows("w_in", C_GA + m * P), P)
            for p in range(4):
                fetch(FIRST["attn_out"] + p, rows("w_a_out", 2 * P * p, 2 * P, nk=4), 2 * P)
            for m in range(KC):
                fetch(FIRST["mix_out"] + m, rows("w_out", m * P), P)
            for m in range(KC):
                fetch(FIRST["mem_k"] + m, rows("xattn_w_kv", m * P), P)
            for n in range(8):
                fetch(FIRST["mem_v"] + n, rows("xattn_w_kv", D + n // 4 * T, T, k0=2 * (n % 4), nk=2), T)
            for m in range(KC):
                fetch(FIRST["x_q"] + m, rows("xattn_w_q", m * P), P)
            for m in range(KC):
                fetch(FIRST["x_out"] + m, rows("xattn_w_o", m * P), P)
            feed_forward("ffn2")
            u = FIRST["grouped"]
            for c in range(4):
                fetch(u + c, rows("w_in_2", Z_QB + c * P), P)
            for kv in range(2):
                fetch_twin(u + 4 + kv, "w_in_2", Z_KB + kv * HD)
            fetch(u + 6, rows("w_in_2", Z_VB), P)
            u = FIRST["latent"]
            for c in range(2):
                fetch(u + c, rows("w_in_2", Z_QL + c * P), P)
            fetch(u + 2, rows("w_in_2", Z_KVL), P)
            fetch(u + 3, rows("w_in_2", Z_KPE - NOPE), P)
            for c in range(4):
                u = FIRST["latent_heads"] + c
                load(u, rows("w_qb_2", 2 * c * QW, 2 * QW, nk=2), 2 * QW).then_inc(raw_in[u % RING], 16)
                sp.dma_start(raw[:, u % RING, 4 * QW:4 * QW + 2 * P],
                             dram["w_kvb_2"][0][:, 2 * c * P:2 * (c + 1) * P]).then_inc(raw_in[u % RING], 16)
            for p in range(4):
                u = FIRST["merge"] + 6 * p
                fetch(u, rows("w_oa_2", 2 * P * p, 2 * P, nk=4), 2 * P)
                fetch(u + 1, rows("w_ob_2", 2 * P * p, 2 * P, nk=4), 2 * P)
                for q in range(2):
                    fetch(u + 2 + 2 * q, rows("w_in_2", Z_GA + (2 * p + q) * P), P)
                    fetch(u + 3 + 2 * q, rows("w_in_2", Z_GB + (2 * p + q) * P), P)
            for m in range(KC):
                fetch(FIRST["out"] + m, rows("w_o_2", m * P), P)
            for half in "ab":
                j0 = FF2_HALF * "ab".index(half)
                loop(FIRST["mlp_up_" + half], FF2_HALF // RING,
                     lambda i, q: rows_at("w_up_2", i * (4 * P) + (j0 + q) * P))
                loop(FIRST["mlp_down_" + half], KC // 2,
                     lambda i, q: rows_at("w_down_2", i * (2 * P) + q // 2 * P, k0=j0 + q % 2 * KC))
            for n in range(2):
                fetch(FIRST["ple"] + n, rows("w_ple_2", n * T, T, nk=2), T)
            for m in range(KC):
                fetch(FIRST["ple_gate"] + m, rows("w_ple_gate_2", m * P), P)
            sp.wait_ge(end_kept, KC)
            for b in range(TB):
                sp.dma_start(out[0, b * P:(b + 1) * P, :], out_rows[:, b, :]).then_inc(out_sent, 16)
            sp.wait_ge(out_sent, 16 * TB)

        @block.gpsimd
        def _(pool):
            with pool.Fori(0, UNITS // RING) as i:
                for s in range(RING):
                    pool.wait_ge(hi_ready, 4 * i + (s + 1))
                    pool.tensor_tensor(wl[:, s, :], raw[:, s, :], wh[:, s, :].bitcast(F32),
                                       ALU.subtract).then_inc(lo_ready, 1)

        @block.tensor
        def _(pe):
            def three(to, a_hi, a_lo, b_hi, b_lo, start, stop):
                pe.matmul(to, a_hi, b_hi, start=start, stop=False, skip_group_check=True)
                pe.matmul(to, a_hi, b_lo, start=False, stop=False, skip_group_check=True)
                return pe.matmul(to, a_lo, b_hi, start=False, stop=stop, skip_group_check=True)

            def unit(u, i=None):
                pe.wait_ge(lo_ready, u + 1 if i is None else 4 * i + (u + 1))
                return wh[:, u % RING, :], wl[:, u % RING, :]

            def columns(u, to, hi, lo, ks, i=None, start=True, stop=True, width=P, at_col=0, use=True, before=None):
                w_h, w_l = unit(u, i)
                for n, k in enumerate(ks):
                    if before is not None:
                        before(k)
                    c = n * width + at_col
                    last = three(to, w_h[:, c:c + P], w_l[:, c:c + P], hi[:, k, :], lo[:, k, :],
                                 start and n == 0, stop and n == len(ks) - 1)
                if use:
                    last.then_inc(unit_used, 1)

            def sum_squares(N, k, i=None):
                r = N.chunk0 + k
                pe.wait_ge(norm.squares, r + 1 if i is None else 2 * i + (r + 1))
                for b in range(TB):
                    last = pe.matmul(bank[SUMS][:, b:b + 1], squares[:, r % 2, b * P:(b + 1) * P], ones[:, 0:1],
                                     start=(i is None and k == 0 and b == 0), stop=False, skip_group_check=True)
                last.then_inc(norm.summed, 1)

            def spread(N, to=SPREAD, n=0):
                pe.wait_ge(norm.expand, N.expand0 + n + 1)
                for b in range(TB):
                    last = pe.matmul(bank[to][:, b * P:(b + 1) * P], expand[:, b, :], ident, start=True, stop=True)
                last.then_inc(norm.spread, 1)

            def entering(X, N):
                def before(k):
                    pe.wait_ge(X.lo, X.first + k + 1)
                    if N is not None:
                        sum_squares(N, k)
                return before

            def rotate(R, n, x, m, to, rows=slice(0, P)):
                pe.wait_ge(R.x, n + 1)
                pe.matmul(bank[to][rows, :], m[rows, rows], x, start=True, stop=True).then_inc(R.rot, 1)

            def feed_forward(name, S, X, N, NP):
                u = FIRST[name + "_up_a"]

                def up(u, j, i, first=False):
                    for q in range(RING):
                        if not first:
                            pe.wait_ge((ffn.gate, ffn.up)[q % 2], 2 * i + (S.hid0 + j + q // 2 - 1))
                        columns(u + q, bank[q][:], xh, xl, range(KC), i,
                                before=entering(X, N) if first and q == 0 else None)
                        if first and q == 1:
                            spread(N)

                up(u, 0, None, first=True)
                with pe.Fori(1, FF_A // 2) as i:
                    up(u, 0, i)
                u = FIRST[name + "_down_a"]

                def down(i, first=False):
                    for q in range(RING):
                        if q % 2 == 0 and not first:
                            pe.wait_ge(ffn.part, 2 * i + (S.out0 + q // 2 - 1))
                        columns(u + q, bank[4 + q // 2][:], hid_h, hid_l, range(q % 2 * KC, q % 2 * KC + KC), i,
                                start=q % 2 == 0, stop=q % 2 == 1,
                                before=(lambda k: pe.wait_ge(ffn.hid.lo, S.hid0 + k + 1)) if first and q < 2 else None)
                down(None, first=True)
                with pe.Fori(1, KC // 2) as i:
                    down(i)
                with pe.Fori(0, FF_B // 2) as i:
                    up(FIRST[name + "_up_b"], FF_A, i)
                u = FIRST[name + "_down_b"]
                for m in range(KC):
                    if m == 0:
                        pe.wait_ge(ffn.part, S.out0 + KC)
                    elif m >= 2:
                        pe.wait_ge(ffn.full, S.out0 + m - 1)
                    columns(u + m, bank[4 + m % 2][:], hid_h, hid_l, range(FF_B),
                            before=(lambda k: pe.wait_ge(ffn.hid.lo, S.hid0 + FF_A + k + 1)) if m == 0 else None)
                    if m >= 1:
                        sum_squares(NP, m - 1)
                sum_squares(NP, KC - 1)
                spread(NP)

            def attention(A, blocks, logits, blocks_of_keys, values, exp_reads_psum=True, lead=None):
                lo, hi = blocks
                for n in range(lo, hi + 5):
                    r = A.block0 + n
                    if n < hi:
                        if n >= lo + 3:
                            pe.wait_ge(att.exp if exp_reads_psum else att.top, r - 2)
                        if lead is not None:
                            lead(n)
                        logits(n, bank[n % 3]).then_inc(att.logits, 1)
                    m, r = n - 2, A.block0 + n - 2
                    if lo <= m < hi:
                        pe.wait_ge(att.probs, r + 1)
                        if m >= lo + 2:
                            pe.wait_ge(att.pt.lo, r - 1)
                        for s in range(blocks_of_keys(m)):
                            last = pe.transpose(bank[3 + m % 2][:, s * P:(s + 1) * P],
                                                probs[:, r % 3, s * P:(s + 1) * P], ident)
                        last.then_inc(att.turned, 1)
                    if (n - 5) % 2 == 0 and lo <= n - 5 < hi:
                        g = (n - 5) // 2
                        pe.wait_ge(att.pt.lo, A.block0 + 2 * g + 2)
                        values(g).then_inc(att.pv, 1)

            def paired_values(A, g, key_blocks, v_of, p_h, p_l, first_pair=0):
                head, half = g // 2, g % 2
                par, pair = head % 2, head // 2
                if par == 0 and pair > first_pair:
                    pe.wait_ge(att.out.lo, A.piece0 + 2 * (pair - 1) + half + 1)
                slot = (A.half0 + g) % 2
                n_s = key_blocks(2 * g + 1)
                for s in range(n_s):
                    c = max(0, (s - 2 * half) * P) if n_s != TB or key_blocks(2 * g) != TB else 0
                    v_h, v_l = v_of(head, s)
                    last = three(bank[5 + half][:, c:256], v_h[:, par * HD:par * HD + P], v_l[:, par * HD:par * HD + P],
                                 p_h[:, slot, s, c:256], p_l[:, slot, s, c:256],
                                 par == 0 and s == 0, par == 1 and s == n_s - 1)
                return last

            pe.wait_ge(const_in, 16 * CONST_DMAS)
            pe.transpose(bank[0][:, 0:GAIN_ROWS], gain_rows[0:GAIN_ROWS, :], ident[0:GAIN_ROWS, 0:GAIN_ROWS]
                         ).then_inc(gains_turned, 1)
            pe.wait_ge(gains_kept, 1)
            pe.wait_ge(x_in, 16 * TB)
            for k in range(KC):
                for b in range(TB):
                    last = pe.transpose(bank[k][:, b * P:(b + 1) * P], x_rows[:, b, k * P:(k + 1) * P], ident)
                last.then_inc(x_turned, 1)
            pe.wait_ge(x_kept, KC)
            pe.transpose(bank[7][:, 0:P], ident, ident).then_inc(unit_used, 1)

            feed_forward("ffn1", ffn1, x_ffn1, n_ffn1, n_ffn1p)

            u = FIRST["conv"]
            for j in range(4):
                for q in range(3):
                    if j >= 2 and q == 0:
                        pe.wait_ge(conv_step, 7 * (j - 2) + 3)
                    columns(u + 3 * j + q, bank[3 * (j % 2) + q][:], xh, xl, range(KC),
                            before=entering(x_mix, n_mix) if j == q == 0 else None)
                    if j == 0 and q == 1:
                        spread(n_mix)
            u = FIRST["merge_conv"]
            for p in range(4):
                b0 = 4 * (p % 2)
                if p == 0:
                    pe.wait_ge(conv_step, 7 * 3 + 3)
                    pe.wait_ge(conv_out.lo, 4)
                elif p == 1:
                    pe.wait_ge(norm.scale, n_mix.scale0 + 1)
                else:
                    pe.wait_ge(mc_sum, 2 * p - 2)
                for q in range(2):
                    columns(u + 3 * p, bank[b0 + q][:], cz_h, cz_l, range(4), width=2 * P, at_col=q * P, use=q == 1)
                for q in range(2):
                    columns(u + 3 * p + 1 + q, bank[b0 + 2 + q][:], xh, xl, range(KC))

            def roped(r):
                if r >= 4:
                    pe.wait_ge(rope.x, r - 3)
                u = FIRST["index"] + r if r < 5 else FIRST["queries"] + r - 5
                columns(u, bank[r % 4][:], xh, xl, range(KC))

            def turn(r):
                if r >= 2:
                    pe.wait_ge(rope.sin, r - 1)
                rotate(rope, r, wa[:, r % 2, :], rot32, 4 + r % 2)

            pe.wait_ge(mc_sum, KC)
            for r in range(5):
                roped(r)
                if r >= 1:
                    turn(r - 1)
            w_h, w_l = unit(FIRST["values"])
            width = HD + HEADS
            for b in range(TB):
                for k in range(KC):
                    last = three(bank[6][:, b * width:(b + 1) * width], xh[:, k, b * P:(b + 1) * P],
                                 xl[:, k, b * P:(b + 1) * P], w_h[:, k * P:k * P + width], w_l[:, k * P:k * P + width],
                                 k == 0, k == KC - 1)
            last.then_inc(unit_used, 1)
            turn(4)
            roped(5)
            turn(5)
            idx_bank = (0, 2, 3, 7)
            pe.wait_ge(rope.out.lo, 5)
            for n in range(3 * HEADS):
                b, head = n // HEADS + 1, n % HEADS
                if n >= 4:
                    pe.wait_ge(idx_relu, n - 3)
                half = slice(head % 2 * HD, head % 2 * HD + HD)
                q = slice(b * P, (b + 1) * P)
                three(bank[idx_bank[n % 4]][:, 0:(b + 1) * P], qi_h[half, head // 2, q], qi_l[half, head // 2, q],
                      ki_h[half, 0:(b + 1) * P], ki_l[half, 0:(b + 1) * P], True, True).then_inc(idx_raw, 1)
            pe.wait_ge(idx_relu, 3 * HEADS)
            for r in range(6, 10):
                roped(r)
                if r >= 7:
                    turn(r - 1)
            turn(9)
            for m in range(KC):
                if m == 0:
                    pe.wait_ge(rope.x, 10)
                elif m >= 4:
                    pe.wait_ge(ga_scaled, m - 3)
                columns(FIRST["gate_a"] + m, bank[m % 4][:], xh, xl, range(KC))

            def main_logits(n, to):
                head, b = n // TB, n % TB
                half = slice(head % 2 * HD, head % 2 * HD + HD)
                q = slice(b * P, (b + 1) * P)
                return three(to[:, 0:(b + 1) * P], qa_h[half, head // 2, q], qa_l[half, head // 2, q],
                             ka_h[half, 0:(b + 1) * P], ka_l[half, 0:(b + 1) * P], True, True)

            pe.wait_ge(ga_scaled, KC)
            pe.wait_ge(rope.out.lo, 10)
            pe.wait_ge(v_split.lo, 2)
            attention(a_main, (0, HB), main_logits, lambda n: n % TB + 1,
                      lambda g: paired_values(a_main, g, lambda n: n % TB + 1,
                                              lambda head, s: (va_h[:, s, :], va_l[:, s, :]), a_pt_h, a_pt_l),
                      exp_reads_psum=False)
            pe.wait_ge(att.out.lo, a_main.piece0 + HEADS)
            for p in range(4):
                for q in range(2):
                    if p >= 2 and q == 0:
                        pe.wait_ge(ma_term, 2 * (p - 1))
                    columns(FIRST["attn_out"] + p, bank[(2 * p + q) % 4][:], xh, xl, range(4), width=2 * P, at_col=q * P,
                            use=q == 1)

            pe.wait_ge(mem_normed, MB)
            pe.wait_ge(ma_term, KC)
            for c in range(4):
                for k in (2 * c, 2 * c + 1):
                    for b in range(MB):
                        last = pe.transpose(bank[c][:, (k % 2) * N_MEM + b * P:(k % 2) * N_MEM + (b + 1) * P],
                                            mem_rows[:, b, k * P:(k + 1) * P], ident)
                last.then_inc(mem_turned, 1)

            def out_projection(u, full, NP, hi, lo, ready):
                for m in range(KC):
                    if m >= 2:
                        pe.wait_ge(full, m - 1)
                    columns(u + m, bank[4 + m % 2][:], hi, lo, range(KC), before=ready if m == 0 else None)
                    if m >= 1:
                        sum_squares(NP, m - 1)

            out_projection(FIRST["mix_out"], mo_full, n_mixp, mg_h, mg_l, lambda k: pe.wait_ge(merged.lo, k + 1))

            pe.wait_ge(memt.lo, KC)
            for m in range(KC):
                if m >= 4:
                    pe.wait_ge(mk.lo, m - 3)
                columns(FIRST["mem_k"] + m, bank[m % 4][:, 0:N_MEM], memt_h, memt_l, range(KC))
                if m == 0:
                    sum_squares(n_mixp, KC - 1)
                if m == 2:
                    spread(n_mixp)
            for n in range(8):
                c, q = n // 4, n % 4
                if q == 0:
                    if c == 0:
                        pe.wait_ge(mo_full, KC)
                    else:
                        pe.wait_ge(mk.lo, KC)
                w_h, w_l = unit(FIRST["mem_v"] + n)
                for kk in range(2):
                    k = 2 * q + kk
                    for b in range(MB):
                        last = three(bank[(4, 0)[c] + b][:], memt_h[:, k, b * P:(b + 1) * P], memt_l[:, k, b * P:(b + 1) * P],
                                     w_h[:, kk * T:(kk + 1) * T], w_l[:, kk * T:(kk + 1) * T], k == 0, k == KC - 1)
                last.then_inc(unit_used, 1)
                if n >= 1:
                    sum_squares(n_xq, n - 1)
            for m in range(KC):
                if m == 0:
                    pe.wait_ge(mk.lo, KC)
                elif m == 2:
                    pe.wait_ge(mv.lo, 4)
                elif m >= 4:
                    pe.wait_ge(xq_scaled, m - 3)
                columns(FIRST["x_q"] + m, bank[(2 + m) % 4][:], xh, xl, range(KC),
                        before=entering(x_x, None) if m == 0 else None)
                if m == 0:
                    sum_squares(n_xq, KC - 1)
                if m == 1:
                    spread(n_xq)

            def mem_logits(n, to):
                head, b = n // TB, n % TB
                q = slice(b * P, (b + 1) * P)
                for k in (2 * head, 2 * head + 1):
                    last = three(to[:, 0:N_MEM], xq_h[:, k, q], xq_l[:, k, q], mk_h[:, k, :], mk_l[:, k, :],
                                 k % 2 == 0, k % 2 == 1)
                return last

            def mem_values(g):
                head, slot = g // 2, (a_mem.half0 + g) % 2
                if g >= 1:
                    pe.wait_ge(att.out.lo, a_mem.piece0 + 2 * g)
                for c in range(2):
                    f0 = head * XD + c * P
                    for s in range(MB):
                        last = three(bank[5 + c][:, 0:256], mv_h[:, s, f0:f0 + P], mv_l[:, s, f0:f0 + P],
                                     x_pt_h[:, slot, s, :], x_pt_l[:, slot, s, :], s == 0, s == MB - 1)
                return last

            pe.wait_ge(xq.lo, KC)
            attention(a_mem, (0, XH * TB), mem_logits, lambda n: MB, mem_values)
            pe.wait_ge(att.out.lo, a_mem.piece0 + 4 * XH)
            out_projection(FIRST["x_out"], xo_full, n_xp, xh, xl, None)
            sum_squares(n_xp, KC - 1)
            spread(n_xp)

            feed_forward("ffn2", ffn2, x_ffn2, n_ffn2, n_ffn2p)

            def turn_grouped(n):
                if n >= 2:
                    pe.wait_ge(gx.sin, n - 1)
                pe.wait_ge(gx_normed, n + 1)
                pe.matmul(bank[n % 2][:], rot16, g_x[:, GROUPED_ORDER[n], :], start=True, stop=True).then_inc(gx.rot, 1)

            def head_squares(r):
                c = n_heads.chunk0 + r
                pe.wait_ge(norm.squares, c + 1)
                for b in range(TB):
                    to = bank[SUMS][:, 12 * b + 2 * r:12 * b + 2 * r + 2]
                    last = pe.matmul(to, squares[:, c % 2, b * P:(b + 1) * P], head_sel[:, 0:2],
                                     start=r == 0 and b == 0, stop=False, skip_group_check=True)
                last.then_inc(norm.summed, 1)

            for r in range(6):
                if r >= 4:
                    pe.wait_ge(gx.x, r - 3)
                columns(FIRST["grouped"] + r, bank[r % 4][:], xh, xl, range(KC),
                        before=entering(x_mix2, n_mix2) if r == 0 else None)
                if r == 1:
                    spread(n_mix2)
                if r >= 2:
                    head_squares(r - 2)
            w_h, w_l = unit(FIRST["grouped"] + 6)
            pe.wait_ge(norm.scale, n_mix2.scale0 + 1)
            for b in range(TB):
                for k in range(KC):
                    last = three(bank[6][:, b * P:(b + 1) * P], xh[:, k, b * P:(b + 1) * P], xl[:, k, b * P:(b + 1) * P],
                                 w_h[:, k * P:(k + 1) * P], w_l[:, k * P:(k + 1) * P], k == 0, k == KC - 1)
            last.then_inc(unit_used, 1)
            head_squares(4)
            head_squares(5)
            for n in range(6):
                if n >= 2:
                    pe.wait_ge(gx_normed, n - 1)
                spread(n_heads, 4 + n % 2, n)
                if n >= 1:
                    turn_grouped(n - 1)
            turn_grouped(5)

            def grp_logits(n, to):
                head, b = n // TB, n % TB
                half = slice(head % 2 * HD, head % 2 * HD + HD)
                q, kv = slice(b * P, (b + 1) * P), head // 4
                return three(to[:], gq_h[half, head // 2, q], gq_l[half, head // 2, q],
                             gk_h[half, kv, :], gk_l[half, kv, :], True, True)

            pe.wait_ge(gx.out.lo, 6)
            pe.wait_ge(gv.lo, 4)
            attention(a_grp, (0, HB), grp_logits, lambda n: TB,
                      lambda g: paired_values(a_grp, g, lambda n: TB,
                                              lambda head, s: (gv_h[:, head // 4, s, :], gv_l[:, head // 4, s, :]),
                                              g_pt_h, g_pt_l))

            u = FIRST["latent"]
            pe.wait_ge(att.out.lo, a_grp.piece0 + HEADS)
            for r in range(4):
                columns(u + r, bank[r][:], xh, xl, range(KC))
                if r == 2:
                    sum_squares(n_cq, 0)
                if r == 3:
                    sum_squares(n_cq, 1)
                    spread(n_cq)
            c = n_ckv.chunk0
            pe.wait_ge(norm.squares, c + 1)
            for b in range(TB):
                last = pe.matmul(bank[SUMS][:, 8 + b:9 + b], squares[:, c % 2, b * P:(b + 1) * P], ones[:, 0:1],
                                 start=b == 0, stop=False, skip_group_check=True)
            last.then_inc(norm.summed, 1)
            rotate(kpe, 0, l_x[:, 3, :], rot16, 4)
            spread(n_ckv, 5)

            def lat_heads(c):
                w_h, w_l = unit(FIRST["latent_heads"] + c)
                if c >= 1:
                    pe.wait_ge(att.out.lo, a_lat.piece0 + 2 * c)
                for q in range(2):
                    for k in range(2):
                        w = slice(k * 2 * QW + q * QW, k * 2 * QW + (q + 1) * QW)
                        three(bank[q][0:QW, :], w_h[:, w], w_l[:, w], cq_h[:, k, :], cq_l[:, k, :], k == 0, k == 1)
                kv0 = 4 * QW
                for q in range(2):
                    w = slice(kv0 + q * P, kv0 + (q + 1) * P)
                    three(bank[2 + q][:], w_h[:, w], w_l[:, w], ck_h[:], ck_l[:], True, True)
                v_h, v_l = (w[:, kv0:kv0 + 2 * P].rearrange("p (h c) -> p h c", c=P)[:, :, NOPE:P] for w in (w_h, w_l))
                for b in range(TB):
                    last = three(bank[7][:, b * P:(b + 1) * P].rearrange("p (h c) -> p h c", c=HD),
                                 ck_h[:, b * P:(b + 1) * P], ck_l[:, b * P:(b + 1) * P], v_h, v_l, True, True)
                last.then_inc(unit_used, 1)
                if c == 0:
                    pe.wait_ge(kpe.sin, 1)
                for q in range(2):
                    rotate(lq, 2 * c + q, l_q[0:QW, q, :], rot16, 4 + q, slice(0, QW))

            def lat_logits(n, to):
                head, b = n // TB, n % TB
                q = slice(b * P, (b + 1) * P)
                return three(to[:], lq_h[0:QW, head % 2, q], lq_l[0:QW, head % 2, q],
                             lk_h[0:QW, head % 2, :], lk_l[0:QW, head % 2, :], True, True)

            pe.wait_ge(l_lat.lo, 3)
            for c in range(4):
                lat_heads(c)
                pe.wait_ge(lq.out.lo, 2 * c + 2)
                pe.wait_ge(lk.lo, 2 * c + 2)
                if c == 0:
                    pe.wait_ge(kpe.out.lo, 2)
                pe.wait_ge(lv.lo, 2 * c + 2)
                attention(a_lat, (2 * TB * c, 2 * TB * (c + 1)), lat_logits, lambda n: TB,
                          lambda g: paired_values(a_lat, g, lambda n: TB,
                                                  lambda head, s: (lv_h[:, s, :], lv_l[:, s, :]), l_pt_h, l_pt_l,
                                                  first_pair=c))

            pe.wait_ge(att.out.lo, a_lat.piece0 + HEADS)
            for p in range(4):
                u = FIRST["merge"] + 6 * p
                if p >= 1:
                    pe.wait_ge(me_sum, 2 * p)
                for branch, (o_h, o_l) in enumerate(((lo_h, lo_l), (go_h, go_l))):
                    for q in range(2):
                        columns(u + branch, bank[2 * branch + q][:], o_h, o_l, range(4), width=2 * P, at_col=q * P,
                                use=q == 1)
                for n in range(4):
                    columns(u + 2 + n, bank[4 + n][:], xh, xl, range(KC))
            u = FIRST["out"]
            for m in range(KC):
                if m >= 3:
                    pe.wait_ge(h_out, m - 2)
                elif m == 0:
                    pe.wait_ge(me_gate, 2 * KC)
                columns(u + m, bank[4 + m % 3][:], mg_h, mg_l, range(KC),
                        before=(lambda k: pe.wait_ge(merged2.lo, k + 1)) if m == 0 else None)
                if m >= 2:
                    sum_squares(n_mlp, m - 2)

            pe.wait_ge(p_in, 16)
            pe.wait_ge(me_sum, KC)
            for k in range(2):
                for b in range(TB):
                    last = pe.transpose(bank[2 + k][:, b * P:(b + 1) * P], p_rows[:, b, k * P:(k + 1) * P], ident)
                last.then_inc(p_turned, 1)
            sum_squares(n_mlp, KC - 2)

            def mlp_up(first, j0, i, opening=False):
                for q in range(RING):
                    if not opening:
                        pe.wait_ge(ml_x, 4 * i + (j0 + q - 3))
                    elif q == 2:
                        pe.wait_ge(p_split.lo, 2)
                    columns(first + q, bank[q][:], xh, xl, range(KC), i,
                            before=entering(x_mlp, None) if opening and q == 0 else None)
                    if opening and q == 0:
                        sum_squares(n_mlp, KC - 1)
                    if opening and q == 1:
                        spread(n_mlp)

            def mlp_down(first, kept, k0, i, opening=False, N=None):
                for q in range(RING):
                    m = q // 2
                    if q % 2 == 0 and not opening:
                        pe.wait_ge(kept, 2 * i + (m - 1))
                    columns(first + q, bank[4 + m][:], hid_h, hid_l, range(q % 2 * KC, q % 2 * KC + KC), i,
                            start=q % 2 == 0, stop=q % 2 == 1,
                            before=(lambda k: pe.wait_ge(ml_hid.lo, k0 + k + 1)) if opening and m == 0 else None)
                    if N is not None and q % 2 == 1:
                        if m == 1:
                            sum_squares(N, 0, i)
                        elif not opening:
                            sum_squares(N, -1, i)

            mlp_up(FIRST["mlp_up_a"], 0, None, opening=True)
            with pe.Fori(1, FF2_HALF // RING) as i:
                mlp_up(FIRST["mlp_up_a"], 0, i)
            mlp_down(FIRST["mlp_down_a"], ml_part, 0, None, opening=True)
            with pe.Fori(1, KC // 2) as i:
                mlp_down(FIRST["mlp_down_a"], ml_part, 0, i)
            with pe.Fori(0, FF2_HALF // RING) as i:
                mlp_up(FIRST["mlp_up_b"], FF2_HALF, i)
            pe.wait_ge(ml_part, KC)
            mlp_down(FIRST["mlp_down_b"], h_mlp, FF2_HALF, None, opening=True, N=n_ple)
            with pe.Fori(1, KC // 2) as i:
                mlp_down(FIRST["mlp_down_b"], h_mlp, FF2_HALF, i, N=n_ple)

            for n in range(2):
                w_h, w_l = unit(FIRST["ple"] + n)
                for m in range(4):
                    if n == 1 and m == 0:
                        pe.wait_ge(h_mlp, KC)
                    if n == 1 and m == 2:
                        pe.wait_ge(ple_kept, 2)
                    if n == 0 and m == 0:
                        pe.wait_ge(ml_x, FF2)
                    to = bank[m if n == 0 else (4, 5, 0, 1)[m]]
                    for k in range(2):
                        w = slice(k * T + m * P, k * T + (m + 1) * P)
                        last = three(to[:], w_h[:, w], w_l[:, w], pt_h[:, k, :], pt_l[:, k, :], k == 0, k == 1)
                last.then_inc(unit_used, 1)
                if n == 0:
                    sum_squares(n_ple, KC - 1)
                else:
                    spread(n_ple)
            for m in range(KC):
                if m == 0:
                    pe.wait_ge(ple_kept, 4)
                elif m >= 2:
                    pe.wait_ge(pg_x, m - 1)
                columns(FIRST["ple_gate"] + m, bank[2 + m % 2][:], xh, xl, range(KC),
                        before=entering(x_ple, None) if m == 0 else None)
                if m >= 2:
                    sum_squares(n_end, m - 2)
            sum_squares(n_end, KC - 2)
            sum_squares(n_end, KC - 1)
            spread(n_end)

            end_bank = (0, 1, 4, 5)
            pe.wait_ge(ple_kept, KC)
            for k in range(KC):
                pe.wait_ge(end_normed, k + 1)
                if k >= 4:
                    pe.wait_ge(end_kept, k - 3)
                for b in range(TB):
                    last = pe.transpose(bank[end_bank[k % 4]][:, b * P:(b + 1) * P], normed[:, k, b * P:(b + 1) * P], ident)
                last.then_inc(end_turned, 1)

        @block.scalar
        def _(act):
            def hi(u, i=None):
                if u >= UNITS:
                    return
                s = u % RING
                act.wait_ge(raw_in[s], landed(u) if i is None else 16 * i + landed(u))
                if i is not None:
                    act.wait_ge(unit_used, 4 * i + done(u - RING))
                elif u >= RING:
                    act.wait_ge(unit_used, done(u - RING))
                act.activation(wh[:, s, :], raw[:, s, :], ACT.Copy).then_inc(hi_ready, 1)

            def ahead(u, i=None):
                hi(u + LOOKAHEAD, i)

            def square(N, k, src, i=None):
                r = N.chunk0 + k
                if i is not None:
                    act.wait_ge(gains_kept, 1)
                    act.wait_ge(norm.summed, 2 * i + (r - 1))
                elif r >= 2:
                    act.wait_ge(norm.summed, r - 1)
                act.activation(squares[:, r % 2, :], src, ACT.Square).then_inc(norm.squares, 1)

            def scaled(X, name, k):
                act.activation(xh[:, k, :], h[:, k, :], ACT.Copy, scale=gain(name, k)).then_inc(X.hi, 1)

            def keep_scale(N):
                act.wait_ge(norm.spread, N.expand0 + 1)
                act.activation(scale[:], bank[SPREAD][:], ACT.Copy).then_inc(norm.scale, 1)

            def enter(X, N, name, updated, first):
                for k in range(KC):
                    act.wait_ge(updated, first + k + 1)
                    scaled(X, name, k)
                    square(N, k, h[:, k, :])

            def feed_forward(name, S, X, N, NP, updated, first):
                u = FIRST[name + "_up_a"]

                def pair(u, j, i, n, opening=False):
                    c = n % 2
                    ahead(u, i)
                    if opening:
                        enter(X, N, name + "_pre_g", updated, first)
                    ahead(u + 1, i)
                    if opening:
                        keep_scale(N)
                    act.wait_ge(ffn.gate, S.hid0 + j + 1 if i is None else 2 * i + (S.hid0 + j + 1))
                    act.activation(wa[:, c, :], wa[:, c, :], ACT.Silu).then_inc(ffn.silu, 1)
                    act.wait_ge(ffn.prod, S.hid0 + j + 1 if i is None else 2 * i + (S.hid0 + j + 1))
                    dst = hid_h[:, n, :] if i is None else hid_h[:, 2 * i + n, :]
                    act.activation(dst, wb[:, c, :], ACT.Copy).then_inc(ffn.hid.hi, 1)

                pair(u, 0, None, 0, opening=True)
                pair(u + 2, 1, None, 1)
                with act.Fori(1, FF_A // 2) as i:
                    for c in range(2):
                        pair(u + 2 * c, c, i, c)
                u = FIRST[name + "_down_a"]
                with act.Fori(0, KC // 2) as i:
                    for q in range(RING):
                        ahead(u + q, i)
                u = FIRST[name + "_up_b"]
                with act.Fori(0, FF_B // 2) as i:
                    for c in range(2):
                        pair(u + 2 * c, FF_A + c, i, c)
                u = FIRST[name + "_down_b"]
                for m in range(KC):
                    ahead(u + m)
                    act.wait_ge(ffn.full, S.out0 + m + 1)
                    square(NP, m, f[:, m, :])

            def attention(A, blocks, source, exp_scale, blocks_of_keys, p_h, outputs):
                lo, hi_ = blocks
                for n in range(lo, hi_ + 5):
                    r = A.block0 + n
                    if n < hi_:
                        act.wait_ge(att.top, r + 1)
                        if r >= 3:
                            act.wait_ge(att.turned, r - 2)
                        src = source(n)
                        act.activation(probs[:, r % 3, 0:src.shape[1]], src, ACT.Exp, bias=top[:, r % 4:r % 4 + 1],
                                       scale=exp_scale, accum_out=sums[:, r % 4:r % 4 + 1]).then_inc(att.exp, 1)
                    m, r = n - 2, A.block0 + n - 2
                    if lo <= m < hi_:
                        g = A.half0 + m // 2
                        act.wait_ge(att.turned, r + 1)
                        if g >= 2:
                            act.wait_ge(att.pv, g - 1)
                        w = blocks_of_keys(m)
                        act.activation(p_h[:, g % 2, 0:w, m % 2 * P:(m % 2 + 1) * P],
                                       bank[3 + m % 2][:, 0:w * P].rearrange("p (s q) -> p s q", q=P),
                                       ACT.Copy).then_inc(att.pt.hi, 1)
                    if (n - 6) % 2 == 0 and lo <= n - 6 < hi_:
                        output(A, (n - 6) // 2, outputs)

            def output(A, g, outputs):
                for dst, src in outputs(g):
                    act.wait_ge(att.pv, A.half0 + g + 1)
                    act.activation(dst, src, ACT.Copy).then_inc(att.out.hi, 1)

            def paired(o_h):
                def outputs(g):
                    head, half = g // 2, g % 2
                    if head % 2 == 0:
                        return []
                    return [(o_h[:, head // 2, half * 256:(half + 1) * 256], bank[5 + half][:, 0:256])]
                return outputs

            act.dma_start(mats[:], dram["shape_mats"].rearrange("p (n c) -> p n c", c=P)).then_inc(const_in, 16)
            for n, name in enumerate(GAINS):
                g = dram[name] if name != "g_final_2" else dram[name].unsqueeze(0)
                act.dma_start(gain_rows[n * KC:(n + 1) * KC, :], g.rearrange("o (k p) -> (o k) p", p=P)).then_inc(const_in, 16)
            act.dma_start(gain_rows[G_QA_ROW:G_KVA_ROW, :], dram["g_qa_2"].rearrange("o (k p) -> (o k) p", p=P)).then_inc(const_in, 16)
            act.dma_start(gain_rows[G_KVA_ROW:G_KVA_ROW + 1, :], dram["g_kva_2"]).then_inc(const_in, 16)
            act.dma_start(gain_rows[CONV_ROW:G_QN_ROW, :],
                          dram["conv_w"][0].rearrange("t (k p) -> (t k) p", p=P)).then_inc(const_in, 16)
            for row, name in ((G_QN_ROW, "g_qn_2"), (G_KN_ROW, "g_kn_2")):
                for half in range(2):
                    act.dma_start(gain_rows[row:row + 1, half * HD:(half + 1) * HD], dram[name]).then_inc(const_in, 16)
            for b in range(TB):
                act.dma_start(x_rows[:, b, :], dram["x"][0, b * P:(b + 1) * P, :]).then_inc(x_in, 16)
            tabs = dram["shape_tabs"].rearrange("p (n c t) -> p n c t", n=3, c=2)
            act.dma_start(tab[:], tabs[:, 0]).then_inc(tab_in, 16)
            for u in range(LOOKAHEAD):
                hi(u)
            act.wait_ge(gains_turned, 1)
            act.activation(gains[:, 0:GAIN_ROWS], bank[0][:, 0:GAIN_ROWS], ACT.Copy).then_inc(gains_kept, 1)
            for k in range(KC):
                act.wait_ge(x_turned, k + 1)
                act.activation(h[:, k, :], bank[k][:], ACT.Copy).then_inc(x_kept, 1)
            act.wait_ge(gains_kept, 1)
            feed_forward("ffn1", ffn1, x_ffn1, n_ffn1, n_ffn1p, x_kept, 0)

            u = FIRST["conv"]
            for j in range(4):
                c = j % 2
                for q in range(3):
                    ahead(u + 3 * j + q)
                    if j == 0 and q == 0:
                        enter(x_mix, n_mix, "mix_pre_g", r_ffn1.h, r_ffn1.first)
                    if j == 0 and q == 1:
                        keep_scale(n_mix)
                act.wait_ge(conv_step, 7 * j + 4)
                act.activation(c_z[:, c, :], c_y[:, c, 2:2 + T], ACT.Copy,
                               scale=gain_row(CONV_ROW + 8 + j)).then_inc(conv_tap, 1)
                act.wait_ge(conv_step, 7 * j + 7)
                act.activation(cz_h[:, j, :], c_z[:, c, :], ACT.Copy).then_inc(conv_out.hi, 1)
            u = FIRST["merge_conv"]
            for p in range(4):
                for q in range(3):
                    ahead(u + 3 * p + q)
                    if q >= 1:
                        m = 2 * p + q - 1
                        act.wait_ge(mc_gate, m + 1)
                        act.activation(wa[:, m % 2, :], wa[:, m % 2, :], ACT.Sigmoid).then_inc(mc_sig, 1)

            def rope_hi(r):
                dst = (qi_h[:, r, :] if r < 4 else ki_h[:] if r == 4 else qa_h[:, r - 5, :] if r < 9 else ka_h[:])
                act.wait_ge(rope.sum, r + 1)
                act.activation(dst, wb[:, r % 2, :], ACT.Copy, scale=HD ** -0.5 if 5 <= r < 9 else 1.0).then_inc(rope.out.hi, 1)

            for r in range(5):
                ahead(FIRST["index"] + r)
                if r >= 1:
                    rope_hi(r - 1)
            ahead(FIRST["values"])
            act.wait_ge(v_scaled, 2 * TB)
            for par in range(2):
                act.activation(va_h[:, :, par * P:par * P + HD], v_rows[:], ACT.Copy).then_inc(v_split.hi, 1)
            rope_hi(4)
            ahead(FIRST["queries"])
            act.wait_ge(v_split.lo, 2)
            for n in range(3 * HEADS):
                w = (n // HEADS + 2) * P
                act.wait_ge(idx_raw, n + 1)
                if n >= 3:
                    act.wait_ge(idx_sum, IDX_SUM[n - 3])
                act.activation(probs[:, n % 3, 0:w], bank[(0, 2, 3, 7)[n % 4]][:, 0:w], ACT.Relu).then_inc(idx_relu, 1)
            for r in range(6, 10):
                ahead(FIRST["queries"] + r - 5)
                rope_hi(r - 1)
            rope_hi(9)
            for m in range(KC):
                ahead(FIRST["gate_a"] + m)
                act.wait_ge(ga_scaled, m + 1)
                act.activation(gate_a[:, m, :], gate_a[:, m, :], ACT.Sigmoid).then_inc(ga_sig, 1)

            act.wait_ge(unit_used, done(FIRST["gate_a"] + KC - 1))
            act.dma_start(mem_rows[:], dram["mem"][0].rearrange("(b p) c -> p b c", p=P)).then_inc(mem_in, 16)
            act.wait_ge(rope.sin, 10)
            act.dma_start(tab[:], tabs[:, 2]).then_inc(tab_in, 16)
            attention(a_main, (0, HB), lambda n: wb[:, n % 2, 0:(n % TB + 1) * P], -1.0, lambda n: n % TB + 1, a_pt_h,
                      paired(xh))
            act.wait_ge(mem_in, 16)
            for b in range(MB):
                if b:
                    act.wait_ge(mem_sum, b)
                act.activation(mem_squares[:], mem_rows[:, b, :], ACT.Square,
                               accum_out=mem_sq[:, b:b + 1]).then_inc(mem_sum, 1)
            for p in range(4):
                ahead(FIRST["attn_out"] + p)
                for m in (2 * p, 2 * p + 1):
                    act.wait_ge(ma_sum, m + 1)
                    act.activation(mg_h[:, m, :], mixed[:, m, :], ACT.Copy).then_inc(merged.hi, 1)
            for k in range(KC):
                act.wait_ge(mem_turned, k // 2 + 1)
                act.activation(memt_h[:, k, :], bank[k // 2][:, k % 2 * N_MEM:(k % 2 + 1) * N_MEM], ACT.Copy,
                               scale=gain("mem_g", k)).then_inc(memt.hi, 1)
            for m in range(KC):
                ahead(FIRST["mix_out"] + m)
                act.wait_ge(mo_full, m + 1)
                square(n_mixp, m, f[:, m, :])

            def enter_mem(k):
                act.wait_ge(r_mix.h, r_mix.first + k + 1)
                scaled(x_x, "xattn_pre_g", k)

            for m in range(KC):
                ahead(FIRST["mem_k"] + m)
                act.wait_ge(unit_used, done(FIRST["mem_k"] + m))
                act.activation(mk_h[:, m, :], bank[m % 4][:, 0:N_MEM], ACT.Copy).then_inc(mk.hi, 1)
                if m >= 3:
                    enter_mem(m - 3)
            for n in range(8):
                ahead(FIRST["mem_v"] + n)
                if n < 3:
                    enter_mem(n + 5)
                if n % 4 == 3:
                    c = n // 4
                    act.wait_ge(unit_used, done(FIRST["mem_v"] + n))
                    for b in range(MB):
                        act.activation(mv_h[:, b, c * T:(c + 1) * T], bank[(4, 0)[c] + b][:], ACT.Copy).then_inc(mv.hi, 1)
                square(n_xq, n, h[:, n, :])
            for m in range(KC + 1):
                if m < KC:
                    ahead(FIRST["x_q"] + m)
                if m == 1:
                    keep_scale(n_xq)
                if m >= 1:
                    act.wait_ge(xq_scaled, m)
                    act.activation(xq_h[:, m - 1, :], wa[:, (m - 1) % 2, :], ACT.Copy).then_inc(xq.hi, 1)
            attention(a_mem, (0, XH * TB), lambda n: bank[n % 3][:, 0:N_MEM], 1.0, lambda n: MB, x_pt_h,
                      lambda g: [(xh[:, g // 2 * 2 + c, g % 2 * 256:(g % 2 + 1) * 256], bank[5 + c][:, 0:256]) for c in range(2)])
            for m in range(KC):
                ahead(FIRST["x_out"] + m)
                act.wait_ge(xo_full, m + 1)
                square(n_xp, m, f[:, m, :])

            feed_forward("ffn2", ffn2, x_ffn2, n_ffn2, n_ffn2p, r_x.h, r_x.first)

            for r in range(6):
                ahead(FIRST["grouped"] + r)
                if r == 0:
                    enter(x_mix2, n_mix2, "g_mix_2", r_ffn2.h, r_ffn2.first)
                elif r == 1:
                    keep_scale(n_mix2)
                else:
                    act.wait_ge(gx.x, r - 1)
                    square(n_heads, r - 2, g_x[:, r - 2, :])
            ahead(FIRST["grouped"] + 6)
            for r in (4, 5):
                act.wait_ge(gx.x, r + 1)
                square(n_heads, r, g_x[:, r, :])
            act.wait_ge(gv_scaled, TB)
            for kv in range(2):
                for par in range(2):
                    act.activation(gv_h[:, kv, :, par * P:par * P + HD], g_v[:, :, kv * HD:(kv + 1) * HD], ACT.Copy).then_inc(gv.hi, 1)
            for n, r in enumerate(GROUPED_ORDER):
                act.wait_ge(gx.sum, n + 1)
                act.activation(gq_h[:, r, :] if r < 4 else gk_h[:, r - 4, :], wb[:, n % 2, :], ACT.Copy,
                               scale=HD ** -0.5 if r < 4 else 1.0).then_inc(gx.out.hi, 1)
            act.wait_ge(gx.sin, 6)
            act.dma_start(tab[:], tabs[:, 1]).then_inc(tab_in, 16)
            act.wait_ge(gv.lo, 4)
            attention(a_grp, (0, HB), lambda n: bank[n % 3][:], 1.0, lambda n: TB, g_pt_h, paired(go_h))

            for r in range(4):
                ahead(FIRST["latent"] + r)
                if r >= 1:
                    act.wait_ge(lx, r)
                    N, k = ((n_cq, 0), (n_cq, 1), (n_ckv, 0))[r - 1]
                    square(N, k, l_x[:, r - 1, :])
            for k in range(3):
                act.wait_ge(l_normed, k + 1)
                act.activation((cq_h[:, 0, :], cq_h[:, 1, :], ck_h[:])[k], (wb[:, 0, :], wb[:, 1, :], wa[:, 0, :])[k],
                               ACT.Copy).then_inc(l_lat.hi, 1)
            act.wait_ge(kpe.sum, 1)
            for q in range(2):
                act.activation(lk_h[NOPE:QW, q, :], wa[NOPE:QW, 1, :], ACT.Copy).then_inc(kpe.out.hi, 1)
            act.wait_ge(kpe.out.lo, 2)
            for c in range(4):
                u = FIRST["latent_heads"] + c
                ahead(u)
                act.wait_ge(unit_used, done(u))
                for q in range(2):
                    act.activation(l_q[0:QW, q, :], bank[q][0:QW, :], ACT.Copy).then_inc(lq.x, 1)
                for q in range(2):
                    act.activation(lk_h[0:NOPE, q, :], bank[2 + q][0:NOPE, :], ACT.Copy).then_inc(lk.hi, 1)
                for q in range(2):
                    act.activation(lv_h[:, :, q * P:q * P + HD],
                                   bank[7][:].rearrange("p (s c) -> p s c", c=P)[:, :, q * HD:(q + 1) * HD],
                                   ACT.Copy).then_inc(lv.hi, 1)
                for q in range(2):
                    act.wait_ge(lq.sum, 2 * c + q + 1)
                    act.activation(lq_h[0:QW, q, :], wb[0:QW, q, :], ACT.Copy, scale=QW ** -0.5).then_inc(lq.out.hi, 1)
                attention(a_lat, (2 * TB * c, 2 * TB * (c + 1)), lambda n: bank[n % 3][:], 1.0, lambda n: TB, l_pt_h,
                          paired(lo_h))

            def merge_chunk(m):
                c = m % 2
                for n, t in enumerate((wa, wb)):
                    act.wait_ge(me_gate, 2 * m + n + 1)
                    act.activation(t[:, c, :], t[:, c, :], ACT.Sigmoid).then_inc(me_sig, 1)
                act.wait_ge(me_sum, m + 1)
                act.activation(mg_h[:, m, :], wa[:, c, :], ACT.Copy).then_inc(merged2.hi, 1)

            for p in range(4):
                u = FIRST["merge"] + 6 * p
                for n in range(6):
                    ahead(u + n)
                    if n >= 4:
                        merge_chunk(2 * p + n - 4)
            act.wait_ge(unit_used, done(FIRST["merge"] + 23))
            act.dma_start(p_rows[:], dram["p_2"][0, 0].rearrange("(b p) c -> p b c", p=P)).then_inc(p_in, 16)
            for m in range(KC):
                ahead(FIRST["out"] + m)
                act.wait_ge(h_out, m + 1)
                scaled(x_mlp, "g_mlp_2", m)
                square(n_mlp, m, h[:, m, :])
            for k in range(2):
                act.wait_ge(p_turned, k + 1)
                act.activation(pt_h[:, k, :], bank[2 + k][:], ACT.Copy).then_inc(p_split.hi, 1)

            def mlp_chunk(j, i, n):
                act.wait_ge(ml_sq, j + 1 if i is None else 4 * i + (j + 1))
                act.activation(hid_h[:, n, :] if i is None else hid_h[:, 4 * i + n, :], wb[:, n % 2, :],
                               ACT.Copy).then_inc(ml_hid.hi, 1)

            def mlp_up(u, j0, i):
                for q in range(RING):
                    ahead(u + q, i)
                    mlp_chunk(j0 + q, i, q)

            u = FIRST["mlp_up_a"]
            ahead(u)
            ahead(u + 1)
            keep_scale(n_mlp)
            mlp_chunk(0, None, 0)
            mlp_chunk(1, None, 1)
            for q in (2, 3):
                ahead(u + q)
                mlp_chunk(q, None, q)
            with act.Fori(1, FF2_HALF // RING) as i:
                mlp_up(u, 0, i)
            with act.Fori(0, KC // 2) as i:
                for q in range(RING):
                    ahead(FIRST["mlp_down_a"] + q, i)
            with act.Fori(0, FF2_HALF // RING) as i:
                mlp_up(FIRST["mlp_up_b"], FF2_HALF, i)

            def leave_mlp(i):
                for q in range(RING):
                    ahead(FIRST["mlp_down_b"] + q, i)
                    if q % 2 == 1:
                        m = q // 2
                        act.wait_ge(h_mlp, m + 1 if i is None else 2 * i + (m + 1))
                        row = GAINS.index("g_ple_2") * KC + m
                        if i is None:
                            g, x, to = gains[:, row:row + 1], h[:, m, :], xh[:, m, :]
                        else:
                            g, x, to = gains[:, bass.ds(2 * i + row, 1)], h[:, 2 * i + m, :], xh[:, 2 * i + m, :]
                        act.activation(to, x, ACT.Copy, scale=g).then_inc(x_ple.hi, 1)
                        square(n_ple, m, x, i)

            leave_mlp(None)
            with act.Fori(1, KC // 2) as i:
                leave_mlp(i)

            for n in range(2):
                ahead(FIRST["ple"] + n)
                if n == 1:
                    keep_scale(n_ple)
                act.wait_ge(unit_used, done(FIRST["ple"] + n))
                for m in range(4):
                    act.activation(ple[:, 4 * n + m, :], bank[m if n == 0 else (4, 5, 0, 1)[m]][:], ACT.Copy).then_inc(ple_kept, 1)
            for m in range(KC + 1):
                if m < KC:
                    ahead(FIRST["ple_gate"] + m)
                    act.wait_ge(pg_x, m + 1)
                    act.activation(wa[:, m % 2, :], wa[:, m % 2, :], ACT.Sigmoid).then_inc(pg_sig, 1)
                if m >= 1:
                    act.wait_ge(h_end, m)
                    square(n_end, m - 1, h[:, m - 1, :])
            for k in range(KC):
                act.wait_ge(end_turned, k + 1)
                act.activation(out_rows[:, :, k * P:(k + 1) * P],
                               bank[(0, 1, 4, 5)[k % 4]][:].rearrange("p (b c) -> p b c", c=P), ACT.Copy).then_inc(end_kept, 1)

        @block.vector
        def _(dve):
            def rsqrt(x, y, t, mean_sq, d, steps, before):
                dve.tensor_scalar(x, mean_sq, 1.0 / d, EPS, ALU.mult, ALU.add).then_inc(steps, 1)
                dve.wait_ge(steps, before + 1)
                dve.tensor_scalar(y.bitcast(I32), x.bitcast(I32), -0.5, RSQRT_SEED, ALU.mult, ALU.add).then_inc(steps, 1)
                for n in range(NEWTON_STEPS):
                    dve.wait_ge(steps, before + 3 * n + 2)
                    dve.scalar_tensor_tensor(t, x, -0.5, y, ALU.mult, ALU.mult).then_inc(steps, 1)
                    dve.wait_ge(steps, before + 3 * n + 3)
                    dve.tensor_tensor(t, t, y, ALU.mult).then_inc(steps, 1)
                    dve.wait_ge(steps, before + 3 * n + 4)
                    dve.scalar_tensor_tensor(y, t, 1.5, y, ALU.add, ALU.mult).then_inc(steps, 1)
                dve.wait_ge(steps, before + 2 + 3 * NEWTON_STEPS)

            def zero(middle):
                return dve.tensor_scalar(middle, ones[:, 0:HD].unsqueeze(1).to_broadcast([P, TB, HD]), 0.0, None, ALU.mult)

            def newton(N, d, columns=slice(0, TB)):
                n = columns.stop - columns.start
                dve.wait_ge(norm.summed, N.chunk0 + N.chunks)
                rsqrt(n_x[:, 0:n], n_y[:, 0:n], n_t[:, 0:n], bank[SUMS][:, columns], d, norm.newton, N.newton0)

            def lay_out(N):
                if N.expand0:
                    dve.wait_ge(norm.spread, N.expand0)
                dve.tensor_copy(expand[:], n_y[:, 0:TB].unsqueeze(2).to_broadcast([P, TB, P])).then_inc(norm.expand, 1)

            def remainder(X, k, name):
                dve.wait_ge(X.hi, X.first + k + 1)
                dve.scalar_tensor_tensor(xl[:, k, :], h[:, k, :], gain(name, k), xh[:, k, :].bitcast(F32),
                                         ALU.mult, ALU.subtract).then_inc(X.lo, 1)

            def enter(X, name):
                for k in range(KC):
                    remainder(X, k, name)

            def residual_chunk(R, NP, post, factor, k):
                if k == 0:
                    dve.wait_ge(norm.spread, NP.expand0 + 1)
                dve.scalar_tensor_tensor(wa[:, k % 2, :], f[:, k, :], gain(post, k), bank[SPREAD][:],
                                         ALU.mult, ALU.mult).then_inc(R.term, 1)
                dve.wait_ge(R.term, R.first + k + 1)
                dve.scalar_tensor_tensor(h[:, k, :], wa[:, k % 2, :], factor, h[:, k, :], ALU.mult, ALU.add).then_inc(R.h, 1)

            def residual(R, NP, post, factor, X, pre):
                newton(NP, D)
                lay_out(NP)
                for k in range(KC):
                    residual_chunk(R, NP, post, factor, k)
                    if k >= 1:
                        remainder(X, k - 1, pre)
                remainder(X, KC - 1, pre)

            def feed_forward(name, S, N):
                newton(N, D)
                lay_out(N)
                dve.wait_ge(norm.scale, N.scale0 + 1)
                u = FIRST[name + "_up_a"]

                def pair(u, j, i, n):
                    c = n % 2

                    def at(v):
                        return 2 * i + (S.hid0 + v)
                    dve.wait_ge(unit_used, done(u, i))
                    dve.tensor_tensor(wa[:, c, :], bank[2 * c][:], scale[:], ALU.mult).then_inc(ffn.gate, 1)
                    dve.wait_ge(unit_used, done(u + 1, i))
                    dve.tensor_tensor(wb[:, c, :], bank[2 * c + 1][:], scale[:], ALU.mult).then_inc(ffn.up, 1)
                    dve.wait_ge(ffn.silu, at(j + 1))
                    dve.wait_ge(ffn.up, at(j + 1))
                    dve.tensor_tensor(wb[:, c, :], wb[:, c, :], wa[:, c, :], ALU.mult).then_inc(ffn.prod, 1)
                    dve.wait_ge(ffn.hid.hi, at(j + 1))
                    h_, l_ = (hid_h[:, n, :], hid_l[:, n, :]) if i is None else (hid_h[:, 2 * i + n, :], hid_l[:, 2 * i + n, :])
                    dve.tensor_tensor(l_, wb[:, c, :], h_.bitcast(F32), ALU.subtract).then_inc(ffn.hid.lo, 1)

                with dve.Fori(0, FF_A // 2) as i:
                    for c in range(2):
                        pair(u + 2 * c, c, i, c)
                u = FIRST[name + "_down_a"]
                with dve.Fori(0, KC // 2) as i:
                    for m in range(2):
                        dve.wait_ge(unit_used, done(u + 2 * m + 1, i))
                        dve.tensor_copy(f[:, 2 * i + m, :], bank[4 + m][:]).then_inc(ffn.part, 1)
                u = FIRST[name + "_up_b"]
                with dve.Fori(0, FF_B // 2) as i:
                    for c in range(2):
                        pair(u + 2 * c, FF_A + c, i, c)
                u = FIRST[name + "_down_b"]
                dve.wait_ge(ffn.part, S.out0 + KC)
                for m in range(KC):
                    dve.wait_ge(unit_used, done(u + m))
                    dve.tensor_tensor(f[:, m, :], bank[4 + m % 2][:], f[:, m, :], ALU.add).then_inc(ffn.full, 1)

            def attention(A, blocks, find_top, blocks_of_keys, p_h, p_l, outputs):
                lo, hi_ = blocks
                for n in range(lo, hi_ + 5):
                    if n < hi_:
                        r = A.block0 + n
                        dve.wait_ge(att.logits, r + 1)
                        find_top(n, r).then_inc(att.top, 1)
                    m, r = n - 1, A.block0 + n - 1
                    if lo <= m < hi_:
                        c = slice(r % 4, r % 4 + 1)
                        dve.wait_ge(att.exp, r + 1)
                        dve.reciprocal(invs[:, c], sums[:, c]).then_inc(att.inv, 1)
                        dve.wait_ge(att.inv, r + 1)
                        p = probs[:, r % 3, 0:blocks_of_keys(m) * P]
                        dve.tensor_scalar(p, p, invs[:, c], None, ALU.mult).then_inc(att.probs, 1)
                    m, r = n - 3, A.block0 + n - 3
                    if lo <= m < hi_:
                        w, g = blocks_of_keys(m), A.half0 + m // 2
                        part = (slice(None), g % 2, slice(0, w), slice(m % 2 * P, (m % 2 + 1) * P))
                        dve.wait_ge(att.pt.hi, r + 1)
                        dve.tensor_tensor(p_l[part], bank[3 + m % 2][:, 0:w * P].rearrange("p (s q) -> p s q", q=P),
                                          p_h[part].bitcast(F32), ALU.subtract).then_inc(att.pt.lo, 1)
                    if (n - 6) % 2 == 0 and lo <= n - 6 < hi_:
                        for piece, to, src, top_ in outputs((n - 6) // 2):
                            dve.wait_ge(att.out.hi, A.piece0 + piece + 1)
                            dve.tensor_tensor(to, src, top_.bitcast(F32), ALU.subtract).then_inc(att.out.lo, 1)

            def plain_top(width):
                return lambda n, r: dve.tensor_reduce(top[:, r % 4:r % 4 + 1], bank[n % 3][:, 0:width], AX.X, ALU.max, negate=True)

            def paired(o_h, o_l):
                def outputs(g):
                    head, half = g // 2, g % 2
                    if head % 2 == 0:
                        return []
                    part = (slice(None), head // 2, slice(half * 256, (half + 1) * 256))
                    return [(head // 2 * 2 + half, o_l[part], bank[5 + half][:, 0:256], o_h[part])]
                return outputs

            enter(x_ffn1, "ffn1_pre_g")
            feed_forward("ffn1", ffn1, n_ffn1)
            residual(r_ffn1, n_ffn1p, "ffn1_post_g", 0.5, x_mix, "mix_pre_g")

            dve.memset(c_y[:, :, 0:2], 0.0).then_inc(v_zero, 1)
            newton(n_mix, D)
            lay_out(n_mix)
            dve.wait_ge(norm.scale, n_mix.scale0 + 1)
            dve.wait_ge(v_zero, 1)
            u = FIRST["conv"]
            for j in range(4):
                c, b0, s0 = j % 2, 3 * (j % 2), 7 * j
                y, z = c_y[:, c, :], c_z[:, c, :]
                dve.wait_ge(unit_used, done(u + 3 * j))
                dve.tensor_tensor(c_gb[:, c, :], bank[b0][:], scale[:], ALU.mult).then_inc(conv_step, 1)
                dve.wait_ge(unit_used, done(u + 3 * j + 1))
                dve.tensor_tensor(c_gc[:, c, :], bank[b0 + 1][:], scale[:], ALU.mult).then_inc(conv_step, 1)
                dve.wait_ge(unit_used, done(u + 3 * j + 2))
                dve.tensor_tensor(y[:, 2:2 + T], bank[b0 + 2][:], scale[:], ALU.mult).then_inc(conv_step, 1)
                dve.wait_ge(conv_step, s0 + 3)
                dve.tensor_tensor(y[:, 2:2 + T], y[:, 2:2 + T], c_gc[:, c, :], ALU.mult).then_inc(conv_step, 1)
                dve.wait_ge(conv_step, s0 + 4)
                dve.wait_ge(conv_tap, j + 1)
                for n, tap in enumerate((1, 0)):
                    dve.scalar_tensor_tensor(z, y[:, tap:tap + T], gain_row(CONV_ROW + 4 * tap + j), z,
                                             ALU.mult, ALU.add).then_inc(conv_step, 1)
                    dve.wait_ge(conv_step, s0 + 5 + n)
                dve.tensor_tensor(z, z, c_gb[:, c, :], ALU.mult).then_inc(conv_step, 1)
                dve.wait_ge(conv_out.hi, j + 1)
                dve.tensor_tensor(cz_l[:, j, :], z, cz_h[:, j, :].bitcast(F32), ALU.subtract).then_inc(conv_out.lo, 1)
            u = FIRST["merge_conv"]
            for m in range(KC):
                p, q, b0 = m // 2, m % 2, 4 * (m // 2 % 2)
                dve.wait_ge(unit_used, done(u + 3 * p + 1 + q))
                dve.tensor_tensor(wa[:, q, :], bank[b0 + 2 + q][:], scale[:], ALU.mult).then_inc(mc_gate, 1)
                dve.wait_ge(mc_sig, m + 1)
                dve.tensor_tensor(mixed[:, m, :], bank[b0 + q][:], wa[:, q, :], ALU.mult).then_inc(mc_sum, 1)

            def rope_x(r):
                if r >= 2:
                    dve.wait_ge(rope.rot, r - 1)
                u = FIRST["index"] + r if r < 5 else FIRST["queries"] + r - 5
                dve.wait_ge(unit_used, done(u))
                dve.tensor_tensor(wa[:, r % 2, :], bank[r % 4][:], scale[:], ALU.mult).then_inc(rope.x, 1)
                dve.wait_ge(rope.x, r + 1)
                dve.tensor_tensor(wb[:, r % 2, :], wa[:, r % 2, :], tab[:, 0, :], ALU.mult).then_inc(rope.cos, 1)

            def rope_sum(r):
                dve.wait_ge(rope.rot, r + 1)
                dve.tensor_tensor(wa[:, r % 2, :], bank[4 + r % 2][:], tab[:, 1, :], ALU.mult).then_inc(rope.sin, 1)
                dve.wait_ge(rope.sin, r + 1)
                dve.tensor_tensor(wb[:, r % 2, :], wb[:, r % 2, :], wa[:, r % 2, :], ALU.add).then_inc(rope.sum, 1)

            def rope_lo(r):
                if r < 4:
                    a, b, s = qi_l[:, r, :], qi_h[:, r, :], 1.0
                elif r == 4:
                    a, b, s = ki_l[:], ki_h[:], 1.0
                elif r < 9:
                    a, b, s = qa_l[:, r - 5, :], qa_h[:, r - 5, :], HD ** -0.5
                else:
                    a, b, s = ka_l[:], ka_h[:], 1.0
                dve.wait_ge(rope.out.hi, r + 1)
                dve.scalar_tensor_tensor(a, wb[:, r % 2, :], s, b.bitcast(F32), ALU.mult, ALU.subtract).then_inc(rope.out.lo, 1)

            dve.wait_ge(tab_in, 16)
            for r in range(5):
                if r >= 2:
                    rope_lo(r - 2)
                rope_x(r)
                if r >= 1:
                    rope_sum(r - 1)
            zero(va_h[:, :, HD:P])
            zero(va_l[:, :, HD:P]).then_inc(v_zero, 1)
            dve.wait_ge(unit_used, done(FIRST["values"]))
            width = HD + HEADS
            for b in range(TB):
                dve.tensor_scalar(v_rows[:, b, :], bank[6][:, b * width:b * width + HD], n_y[:, b:b + 1], None,
                                  ALU.mult).then_inc(v_scaled, 1)
            for b in range(TB):
                dve.tensor_scalar(w_idx[:, b, :], bank[6][:, b * width + HD:(b + 1) * width], n_y[:, b:b + 1],
                                  HEADS ** -0.5 * HD ** -0.5, ALU.mult, ALU.mult).then_inc(v_scaled, 1)
            for par in range(2):
                part = (slice(None), slice(None), slice(par * P, par * P + HD))
                dve.wait_ge(v_split.hi, par + 1)
                dve.tensor_tensor(va_l[part], v_rows[:], va_h[part].bitcast(F32), ALU.subtract).then_inc(v_split.lo, 1)
            rope_lo(3)
            rope_sum(4)
            rope_x(5)
            rope_lo(4)

            dve.wait_ge(v_scaled, 2 * TB)
            for n in range(3 * HEADS):
                b, head = n // HEADS + 1, n % HEADS
                score, relu, w = mask_of(b), probs[:, n % 3, 0:(b + 1) * P], w_idx[:, b, head:head + 1]
                dve.wait_ge(idx_relu, n + 1)
                if head == 0:
                    dve.tensor_scalar(score, relu, w, None, ALU.mult).then_inc(idx_sum, 1)
                else:
                    dve.wait_ge(idx_sum, IDX_SUM[n] - 1)
                    dve.scalar_tensor_tensor(score, relu, w, score, ALU.mult, ALU.add).then_inc(idx_sum, 1)
                if head == HEADS - 1:
                    dve.wait_ge(idx_sum, IDX_SUM[n])
                    own = score[:, b * P:(b + 1) * P]
                    dve.scalar_tensor_tensor(own, after_query, NOT_CAUSAL, own, ALU.mult, ALU.add).then_inc(idx_sum, 1)
            dve.tensor_scalar(mask_of(0), after_query, MASKED, None, ALU.mult).then_inc(masked, 1)

            def take_top(b, between=None):
                score, rounds = mask_of(b), TOP_K // 8
                before = (b - 1) * 2 * rounds
                dve.wait_ge(idx_sum, b * (HEADS + 1))
                for n in range(rounds):
                    if n:
                        dve.wait_ge(taken, before + 2 * n)
                    dve.max(best8[:], score).then_inc(taken, 1)
                    dve.wait_ge(taken, before + 2 * n + 1)
                    dve.match_replace(score, best8[:], score, REPLACED).then_inc(taken, 1)
                    if between is not None:
                        between(n)
                dve.wait_ge(taken, before + 2 * rounds)
                dve.tensor_scalar(score, score, REPLACED, MASKED, ALU.not_equal, ALU.mult).then_inc(masked, 1)

            def gate_chunk(n):
                if n % 2 == 0:
                    m = n // 2
                    dve.wait_ge(unit_used, done(FIRST["gate_a"] + m))
                    dve.tensor_tensor(gate_a[:, m, :], bank[m % 4][:], scale[:], ALU.mult).then_inc(ga_scaled, 1)

            take_top(1)
            for r in range(6, 10):
                if r >= 7:
                    rope_lo(r - 2)
                if r == 6:
                    rope_sum(r - 1)
                rope_x(r)
                if r >= 7:
                    rope_sum(r - 1)
                if r == 7:
                    take_top(2)
            rope_lo(8)
            rope_sum(9)
            rope_lo(9)
            take_top(3, gate_chunk)

            def masked_top(n, r):
                b = n % TB
                if n >= 2:
                    dve.wait_ge(att.exp, r - 1)
                w = (b + 1) * P
                return dve.tensor_tensor_reduce(wb[:, n % 2, 0:w], bank[n % 3][:, 0:w], mask_of(b), -1.0, 3.0e38,
                                                ALU.add, ALU.min, top[:, r % 4:r % 4 + 1])

            dve.wait_ge(masked, TB)
            attention(a_main, (0, HB), masked_top, lambda n: n % TB + 1, a_pt_h, a_pt_l, paired(xh, xl))

            dve.wait_ge(mem_sum, MB)
            rsqrt(n_x[:, 0:MB], n_y[:, 0:MB], n_t[:, 0:MB], mem_sq[:], D, n_mem, 0)
            for b in range(MB):
                dve.tensor_scalar(mem_rows[:, b, :], mem_rows[:, b, :], n_y[:, b:b + 1], None, ALU.mult).then_inc(mem_normed, 1)
            for m in range(KC):
                c = m % 2
                dve.wait_ge(unit_used, done(FIRST["attn_out"] + m // 2))
                dve.wait_ge(ga_sig, m + 1)
                dve.tensor_tensor(wa[:, c, :], bank[m % 4][:], gate_a[:, m, :], ALU.mult).then_inc(ma_term, 1)
                dve.wait_ge(ma_term, m + 1)
                dve.tensor_tensor(mixed[:, m, :], mixed[:, m, :], wa[:, c, :], ALU.add).then_inc(ma_sum, 1)
                dve.wait_ge(merged.hi, m + 1)
                dve.tensor_tensor(mg_l[:, m, :], mixed[:, m, :], mg_h[:, m, :].bitcast(F32), ALU.subtract).then_inc(merged.lo, 1)
            for k in range(KC):
                dve.wait_ge(memt.hi, k // 2 * 2 + 2)
                dve.scalar_tensor_tensor(memt_l[:, k, :], bank[k // 2][:, k % 2 * N_MEM:(k % 2 + 1) * N_MEM], gain("mem_g", k),
                                         memt_h[:, k, :].bitcast(F32), ALU.mult, ALU.subtract).then_inc(memt.lo, 1)

            def out_chunks(u, full):
                for m in range(KC):
                    dve.wait_ge(unit_used, done(u + m))
                    dve.tensor_copy(f[:, m, :], bank[4 + m % 2][:]).then_inc(full, 1)

            out_chunks(FIRST["mix_out"], mo_full)

            def mem_key(m):
                dve.wait_ge(mk.hi, m + 1)
                dve.tensor_tensor(mk_l[:, m, :], bank[m % 4][:, 0:N_MEM], mk_h[:, m, :].bitcast(F32), ALU.subtract).then_inc(mk.lo, 1)

            newton(n_mixp, D)
            lay_out(n_mixp)
            for m in range(3):
                mem_key(m)
            for k in range(KC):
                residual_chunk(r_mix, n_mixp, "mix_post_g", 1.0, k)
                if k + 3 < KC:
                    mem_key(k + 3)
                if k >= 1:
                    remainder(x_x, k - 1, "xattn_pre_g")
            remainder(x_x, KC - 1, "xattn_pre_g")
            for c in range(2):
                for b in range(MB):
                    part = (slice(None), b, slice(c * T, (c + 1) * T))
                    dve.wait_ge(mv.hi, 2 * c + b + 1)
                    dve.tensor_tensor(mv_l[part], bank[(4, 0)[c] + b][:], mv_h[part].bitcast(F32), ALU.subtract).then_inc(mv.lo, 1)
            newton(n_xq, D)
            lay_out(n_xq)
            dve.wait_ge(norm.scale, n_xq.scale0 + 1)
            for m in range(KC + 1):
                if m < KC:
                    dve.wait_ge(unit_used, done(FIRST["x_q"] + m))
                    if m >= 2:
                        dve.wait_ge(xq.lo, m - 1)
                    dve.scalar_tensor_tensor(wa[:, m % 2, :], bank[(2 + m) % 4][:], XD ** -0.5, scale[:],
                                             ALU.mult, ALU.mult).then_inc(xq_scaled, 1)
                if m >= 1:
                    dve.wait_ge(xq.hi, m)
                    dve.tensor_tensor(xq_l[:, m - 1, :], wa[:, (m - 1) % 2, :], xq_h[:, m - 1, :].bitcast(F32),
                                      ALU.subtract).then_inc(xq.lo, 1)

            def mem_pieces(g):
                out = []
                for c in range(2):
                    part = (slice(None), g // 2 * 2 + c, slice(g % 2 * 256, (g % 2 + 1) * 256))
                    out.append((2 * g + c, xl[part], bank[5 + c][:, 0:256], xh[part]))
                return out

            attention(a_mem, (0, XH * TB), plain_top(N_MEM), lambda n: MB, x_pt_h, x_pt_l, mem_pieces)
            out_chunks(FIRST["x_out"], xo_full)
            residual(r_x, n_xp, "xattn_post_g", 1.0, x_ffn2, "ffn2_pre_g")

            feed_forward("ffn2", ffn2, n_ffn2)
            residual(r_ffn2, n_ffn2p, "ffn2_post_g", 0.5, x_mix2, "g_mix_2")

            newton(n_mix2, D)
            lay_out(n_mix2)
            dve.wait_ge(norm.scale, n_mix2.scale0 + 1)
            for r in range(6):
                dve.wait_ge(unit_used, done(FIRST["grouped"] + r))
                dve.tensor_tensor(g_x[:, r, :], bank[r % 4][:], scale[:], ALU.mult).then_inc(gx.x, 1)
            for kv in range(2):
                zero(gv_h[:, kv, :, HD:P])
                zero(gv_l[:, kv, :, HD:P]).then_inc(v_zero, 1)
            dve.wait_ge(unit_used, done(FIRST["grouped"] + 6))
            for b in range(TB):
                dve.tensor_scalar(g_v[:, b, :], bank[6][:, b * P:(b + 1) * P], n_y[:, b:b + 1], None, ALU.mult).then_inc(gv_scaled, 1)
            for n in range(4):
                kv, par = n // 2, n % 2
                part = (slice(None), kv, slice(None), slice(par * P, par * P + HD))
                dve.wait_ge(gv.hi, n + 1)
                dve.tensor_tensor(gv_l[part], g_v[:, :, kv * HD:(kv + 1) * HD], gv_h[part].bitcast(F32), ALU.subtract).then_inc(gv.lo, 1)
            newton(n_heads, HD, slice(0, 12 * TB))
            dve.wait_ge(tab_in, 32)

            def grouped_sum(n):
                r = GROUPED_ORDER[n]
                dve.wait_ge(gx.rot, n + 1)
                dve.tensor_tensor(g_x[:, r, :], bank[n % 2][:], tab[:, 1, :], ALU.mult).then_inc(gx.sin, 1)
                dve.wait_ge(gx.sin, n + 1)
                dve.tensor_tensor(wb[:, n % 2, :], wb[:, n % 2, :], g_x[:, r, :], ALU.add).then_inc(gx.sum, 1)

            def grouped_lo(n):
                r = GROUPED_ORDER[n]
                a, b, s = (gq_l[:, r, :], gq_h[:, r, :], HD ** -0.5) if r < 4 else (gk_l[:, r - 4, :], gk_h[:, r - 4, :], 1.0)
                dve.wait_ge(gx.out.hi, n + 1)
                dve.scalar_tensor_tensor(a, wb[:, n % 2, :], s, b.bitcast(F32), ALU.mult, ALU.subtract).then_inc(gx.out.lo, 1)

            by_head = n_y[:, 0:12 * TB].rearrange("p (b c) -> p b c", c=12)
            for n, r in enumerate(GROUPED_ORDER):
                dve.wait_ge(norm.spread, n_heads.expand0 + n)
                dve.tensor_copy(expand[:].rearrange("p b (h c) -> p b h c", c=HD),
                                by_head[:, :, 2 * r:2 * r + 2].unsqueeze(3).to_broadcast([P, TB, 2, HD])).then_inc(norm.expand, 1)
                if n >= 2:
                    grouped_lo(n - 2)
                dve.wait_ge(norm.spread, n_heads.expand0 + n + 1)
                dve.scalar_tensor_tensor(g_x[:, r, :], g_x[:, r, :], gain_row(G_QN_ROW if r < 4 else G_KN_ROW),
                                         bank[4 + n % 2][:], ALU.mult, ALU.mult).then_inc(gx_normed, 1)
                dve.wait_ge(gx_normed, n + 1)
                dve.tensor_tensor(wb[:, n % 2, :], g_x[:, r, :], tab[:, 0, :], ALU.mult).then_inc(gx.cos, 1)
                if n >= 1:
                    grouped_sum(n - 1)
            grouped_lo(4)
            grouped_sum(5)
            grouped_lo(5)
            attention(a_grp, (0, HB), plain_top(T), lambda n: TB, g_pt_h, g_pt_l, paired(go_h, go_l))

            u = FIRST["latent"]
            for r in range(3):
                dve.wait_ge(unit_used, done(u + r))
                dve.tensor_tensor(l_x[:, r, :], bank[r][:], scale[:], ALU.mult).then_inc(lx, 1)
            dve.wait_ge(unit_used, done(u + 3))
            dve.tensor_tensor(l_x[:, 3, :], bank[3][:], scale[:], ALU.mult).then_inc(kpe.x, 1)
            newton(n_cq, LAT_Q)
            lay_out(n_cq)
            dve.wait_ge(lx, 3)
            dve.wait_ge(norm.spread, n_cq.expand0 + 1)
            for k in range(2):
                dve.scalar_tensor_tensor(wb[:, k, :], l_x[:, k, :], gain_row(G_QA_ROW + k), bank[SPREAD][:],
                                         ALU.mult, ALU.mult).then_inc(l_normed, 1)
            newton(n_ckv, LAT_KV, slice(8, 8 + TB))
            lay_out(n_ckv)
            dve.wait_ge(norm.spread, n_ckv.expand0 + 1)
            dve.scalar_tensor_tensor(wa[:, 0, :], l_x[:, 2, :], gain_row(G_KVA_ROW), bank[5][:],
                                     ALU.mult, ALU.mult).then_inc(l_normed, 1)
            dve.wait_ge(tab_in, 48)
            dve.wait_ge(kpe.x, 1)
            dve.tensor_tensor(wa[:, 1, :], l_x[:, 3, :], tab[:, 0, :], ALU.mult).then_inc(kpe.cos, 1)
            dve.wait_ge(kpe.rot, 1)
            dve.wait_ge(kpe.cos, 1)
            dve.tensor_tensor(l_x[:, 3, :], bank[4][:], tab[:, 1, :], ALU.mult).then_inc(kpe.sin, 1)
            dve.wait_ge(kpe.sin, 1)
            dve.tensor_tensor(wa[:, 1, :], wa[:, 1, :], l_x[:, 3, :], ALU.add).then_inc(kpe.sum, 1)
            for k in range(3):
                a, b, s = ((cq_l[:, 0, :], cq_h[:, 0, :], wb[:, 0, :]), (cq_l[:, 1, :], cq_h[:, 1, :], wb[:, 1, :]),
                           (ck_l[:], ck_h[:], wa[:, 0, :]))[k]
                dve.wait_ge(l_lat.hi, k + 1)
                dve.tensor_tensor(a, s, b.bitcast(F32), ALU.subtract).then_inc(l_lat.lo, 1)
            for q in range(2):
                dve.wait_ge(kpe.out.hi, q + 1)
                dve.tensor_tensor(lk_l[NOPE:QW, q, :], wa[NOPE:QW, 1, :], lk_h[NOPE:QW, q, :].bitcast(F32),
                                  ALU.subtract).then_inc(kpe.out.lo, 1)
            zero(lv_h[:, :, HD:P])
            zero(lv_l[:, :, HD:P]).then_inc(v_zero, 1)
            for c in range(4):
                for q in range(2):
                    dve.wait_ge(lq.x, 2 * c + q + 1)
                    dve.tensor_tensor(wb[0:QW, q, :], l_q[0:QW, q, :], tab[0:QW, 0, :], ALU.mult).then_inc(lq.cos, 1)
                for q in range(2):
                    dve.wait_ge(lk.hi, 2 * c + q + 1)
                    dve.tensor_tensor(lk_l[0:NOPE, q, :], bank[2 + q][0:NOPE, :], lk_h[0:NOPE, q, :].bitcast(F32),
                                      ALU.subtract).then_inc(lk.lo, 1)
                for q in range(2):
                    dve.wait_ge(lq.rot, 2 * c + q + 1)
                    dve.wait_ge(lq.cos, 2 * c + q + 1)
                    dve.tensor_tensor(l_q[0:QW, q, :], bank[4 + q][0:QW, :], tab[0:QW, 1, :], ALU.mult).then_inc(lq.sin, 1)
                    dve.wait_ge(lq.sin, 2 * c + q + 1)
                    dve.tensor_tensor(wb[0:QW, q, :], wb[0:QW, q, :], l_q[0:QW, q, :], ALU.add).then_inc(lq.sum, 1)
                for q in range(2):
                    part = (slice(None), slice(None), slice(q * P, q * P + HD))
                    dve.wait_ge(lv.hi, 2 * c + 2)
                    dve.tensor_tensor(lv_l[part], bank[7][:].rearrange("p (s c) -> p s c", c=P)[:, :, q * HD:(q + 1) * HD],
                                      lv_h[part].bitcast(F32), ALU.subtract).then_inc(lv.lo, 1)
                for q in range(2):
                    dve.wait_ge(lq.out.hi, 2 * c + q + 1)
                    dve.scalar_tensor_tensor(lq_l[0:QW, q, :], wb[0:QW, q, :], QW ** -0.5, lq_h[0:QW, q, :].bitcast(F32),
                                             ALU.mult, ALU.subtract).then_inc(lq.out.lo, 1)
                attention(a_lat, (2 * TB * c, 2 * TB * (c + 1)), plain_top(T), lambda n: TB, l_pt_h, l_pt_l, paired(lo_h, lo_l))

            for m in range(KC):
                p, c, u = m // 2, m % 2, FIRST["merge"] + 6 * (m // 2)
                for n, t in enumerate((wa, wb)):
                    dve.wait_ge(unit_used, done(u + 2 + 2 * c + n))
                    if n == 0 and m >= 2:
                        dve.wait_ge(merged2.hi, m - 1)
                    dve.tensor_tensor(t[:, c, :], bank[4 + 2 * c + n][:], scale[:], ALU.mult).then_inc(me_gate, 1)
                for n, t in enumerate((wa, wb)):
                    dve.wait_ge(me_sig, 2 * m + n + 1)
                    dve.tensor_tensor(t[:, c, :], bank[2 * n + c][:], t[:, c, :], ALU.mult).then_inc(me_term, 1)
                dve.wait_ge(me_term, 2 * m + 2)
                dve.tensor_tensor(wa[:, c, :], wa[:, c, :], wb[:, c, :], ALU.add).then_inc(me_sum, 1)
                dve.wait_ge(merged2.hi, m + 1)
                dve.tensor_tensor(mg_l[:, m, :], wa[:, c, :], mg_h[:, m, :].bitcast(F32), ALU.subtract).then_inc(merged2.lo, 1)
            for m in range(KC):
                dve.wait_ge(unit_used, done(FIRST["out"] + m))
                dve.tensor_tensor(h[:, m, :], bank[4 + m % 3][:], h[:, m, :], ALU.add).then_inc(h_out, 1)
                if m >= 1:
                    remainder(x_mlp, m - 1, "g_mlp_2")
            remainder(x_mlp, KC - 1, "g_mlp_2")
            for k in range(2):
                dve.wait_ge(p_split.hi, k + 1)
                dve.tensor_tensor(pt_l[:, k, :], bank[2 + k][:], pt_h[:, k, :].bitcast(F32), ALU.subtract).then_inc(p_split.lo, 1)
            newton(n_mlp, D)
            lay_out(n_mlp)
            dve.wait_ge(norm.scale, n_mlp.scale0 + 1)

            def mlp_up(first, j0, i):
                for q in range(RING):
                    c = q % 2
                    dve.wait_ge(unit_used, done(first + q, i))
                    dve.tensor_tensor(wa[:, c, :], bank[q][:], scale[:], ALU.mult).then_inc(ml_x, 1)
                    dve.wait_ge(ml_x, 4 * i + (j0 + q + 1))
                    dve.scalar_tensor_tensor(wb[:, c, :], wa[:, c, :], 0.0, wa[:, c, :], ALU.max, ALU.mult).then_inc(ml_sq, 1)
                    dve.wait_ge(ml_hid.hi, 4 * i + (j0 + q + 1))
                    dve.tensor_tensor(hid_l[:, 4 * i + q, :], wb[:, c, :], hid_h[:, 4 * i + q, :].bitcast(F32),
                                      ALU.subtract).then_inc(ml_hid.lo, 1)

            def mlp_down(first, kept, i, split):
                for m in range(2):
                    dve.wait_ge(unit_used, done(first + 2 * m + 1, i))
                    x = h[:, 2 * i + m, :]
                    dve.tensor_tensor(x, bank[4 + m][:], x, ALU.add).then_inc(kept, 1)
                    if split:
                        row = GAINS.index("g_ple_2") * KC + m
                        dve.wait_ge(x_ple.hi, 2 * i + (x_ple.first + m + 1))
                        dve.scalar_tensor_tensor(xl[:, 2 * i + m, :], x, gains[:, bass.ds(2 * i + row, 1)],
                                                 xh[:, 2 * i + m, :].bitcast(F32), ALU.mult, ALU.subtract).then_inc(x_ple.lo, 1)

            with dve.Fori(0, FF2_HALF // RING) as i:
                mlp_up(FIRST["mlp_up_a"], 0, i)
            with dve.Fori(0, KC // 2) as i:
                mlp_down(FIRST["mlp_down_a"], ml_part, i, False)
            with dve.Fori(0, FF2_HALF // RING) as i:
                mlp_up(FIRST["mlp_up_b"], FF2_HALF, i)
            dve.wait_ge(ml_part, KC)
            with dve.Fori(0, KC // 2) as i:
                mlp_down(FIRST["mlp_down_b"], h_mlp, i, True)

            newton(n_ple, D)
            lay_out(n_ple)
            dve.wait_ge(norm.scale, n_ple.scale0 + 1)
            for m in range(KC):
                c = m % 2
                dve.wait_ge(unit_used, done(FIRST["ple_gate"] + m))
                dve.tensor_tensor(wa[:, c, :], bank[2 + c][:], scale[:], ALU.mult).then_inc(pg_x, 1)
                dve.wait_ge(pg_sig, m + 1)
                dve.wait_ge(ple_kept, m + 1)
                dve.tensor_tensor(wb[:, c, :], wa[:, c, :], ple[:, m, :], ALU.mult).then_inc(pg_term, 1)
                dve.wait_ge(pg_term, m + 1)
                dve.tensor_tensor(h[:, m, :], h[:, m, :], wb[:, c, :], ALU.add).then_inc(h_end, 1)
            newton(n_end, D)
            lay_out(n_end)
            dve.wait_ge(norm.spread, n_end.expand0 + 1)
            for k in range(KC):
                dve.scalar_tensor_tensor(normed[:, k, :], h[:, k, :], gain("g_final_2", k), bank[SPREAD][:],
                                         ALU.mult, ALU.mult).then_inc(end_normed, 1)


INPUTS = ["x", "mem", "ffn1_pre_g", "ffn1_post_g", "ffn1_w1", "ffn1_w3", "ffn1_w2", "mix_pre_g", "mix_post_g", "w_in",
          "conv_w", "w_a_out", "w_b_out", "w_out", "mem_g", "xattn_pre_g", "xattn_post_g", "xattn_w_q", "xattn_w_kv",
          "xattn_w_o", "ffn2_pre_g", "ffn2_post_g", "ffn2_w1", "ffn2_w3", "ffn2_w2", "p_2", "g_mix_2", "w_in_2", "g_qa_2",
          "w_qb_2", "g_kva_2", "w_kvb_2", "g_qn_2", "g_kn_2", "w_oa_2", "w_ob_2", "w_o_2", "g_mlp_2", "w_up_2", "w_down_2",
          "g_ple_2", "w_ple_gate_2", "w_ple_2", "g_final_2"]


def kernel(**inputs):
    import concourse.bacc as bacc
    from concourse.bass_utils import run_bass_kernel_spmd

    nc = bacc.Bacc("TRN2", target_bir_lowering=False, num_devices=1)
    arrays = {f"in_{name}": np.ascontiguousarray(inputs[name]) for name in INPUTS}
    mats, tabs = shape_constants()
    arrays["in_shape_mats"] = np.ascontiguousarray(mats.reshape(P, -1))
    arrays["in_shape_tabs"] = np.ascontiguousarray(tabs.reshape(P, -1))
    dram = {name[3:]: nc.dram_tensor(name, a.shape, mybir.dt.from_np(a.dtype), kind="ExternalInput").ap()
            for name, a in arrays.items()}
    out = nc.dram_tensor("out_0", (1, T, D), F32, kind="ExternalOutput").ap()
    build(nc, dram, out)
    result = run_bass_kernel_spmd(nc, [arrays], core_ids=[0])
    return result.results[0]["out_0"]
```

```python
from contextlib import ExitStack

import numpy as np

import concourse.bass as bass
from concourse import mybir

F32 = mybir.dt.float32
F32R = mybir.dt.float32r
I32 = mybir.dt.int32
ALU = mybir.AluOpType
ACT = mybir.ActivationFunctionType
AX = mybir.AxisListType

P = 128
T = 512
TB = T // P
D = 1024
KC = D // P
N_MEM = 256
MB = N_MEM // P
FF = 2816 // P
FF_A, FF_B = 16, 6
FF2 = 4096 // P
FF2_HALF = FF2 // 2
HEADS = 8
HD = 64
TOP_K = 128
LAT_Q, LAT_KV, ROPE_D, NOPE = 256, 128, 32, 64
QW = NOPE + ROPE_D
XH, XD = 4, 256
PLE = 256
EPS = 1e-6
RSQRT_SEED = float(0x5F3759DF)
NEWTON_STEPS = 3
RING = 4
LOOKAHEAD = 3
UNIT = 1024
REPLACED = -(2.0 ** 127)
NOT_CAUSAL = -(2.0 ** 126)
MASKED = -(2.0 ** 100)

C_QA, C_KA, C_VA, C_QI, C_KI, C_WI = 0, 512, 576, 640, 1152, 1216
C_GB, C_GC, C_CI, C_GA, C_GBB = 1224, 1736, 2248, 2760, 3784
Z_QL, Z_KVL, Z_KPE, Z_QB, Z_KB, Z_VB, Z_GA, Z_GB = 0, 256, 384, 416, 928, 1056, 1184, 2208

GAINS = ["ffn1_pre_g", "ffn1_post_g", "mix_pre_g", "mix_post_g", "mem_g", "xattn_pre_g", "xattn_post_g",
         "ffn2_pre_g", "ffn2_post_g", "g_mix_2", "g_mlp_2", "g_ple_2", "g_final_2"]
G_QA_ROW = len(GAINS) * KC
G_KVA_ROW = G_QA_ROW + LAT_Q // P
CONV_ROW = G_KVA_ROW + 1
G_QN_ROW = CONV_ROW + 3 * 4
G_KN_ROW = G_QN_ROW + 1
GAIN_ROWS = G_KN_ROW + 1

STEPS = [("ffn1_up_a", 2 * FF_A), ("ffn1_down_a", 2 * KC), ("ffn1_up_b", 2 * FF_B), ("ffn1_down_b", KC),
         ("index", 5), ("values", 1), ("queries", 5), ("conv", 12), ("merge_conv", 12), ("gate_a", 8),
         ("attn_out", 4), ("mix_out", 8),
         ("mem_k", 8), ("mem_v", 8), ("x_q", 8), ("x_out", 8),
         ("ffn2_up_a", 2 * FF_A), ("ffn2_down_a", 2 * KC), ("ffn2_up_b", 2 * FF_B), ("ffn2_down_b", KC),
         ("grouped", 7), ("gates", 8), ("latent", 4), ("latent_gates", 2), ("latent_heads", 10),
         ("merge", 8), ("out", 8),
         ("mlp_up_a", FF2_HALF), ("mlp_down_a", FF2_HALF), ("mlp_up_b", FF2_HALF), ("mlp_down_b", FF2_HALF),
         ("ple", 2), ("ple_gate", 8)]
FIRST = {}
UNITS = 0
for _name, _n in STEPS:
    FIRST[_name] = UNITS
    UNITS += _n
assert UNITS % RING == 0
GROUPED_GATES = {3: 6, 18: 7}
HEAD_UNITS = (0, 3, 6, 8)
PAIR_GATE = (10, 12, 14, 15)
PAIR_GATE_2 = {0: 11, 1: 13}
TWO_PART = [FIRST["index"] + 4, FIRST["values"], FIRST["queries"] + 4, FIRST["grouped"] + 4, FIRST["grouped"] + 5,
            *[FIRST["latent_heads"] + n for n in HEAD_UNITS]]


def gate_unit(g):
    if g < 8:
        return FIRST["gates"] + g
    if g < 10:
        return FIRST["latent_gates"] + g - 8
    return FIRST["latent_heads"] + (1, 2, 4, 5, 7, 9)[g - 10]


def shape_constants():
    i = np.arange(P)
    ident = np.eye(P, dtype=np.float32)

    def rotation(half):
        m = np.zeros((P, P), np.float32)
        first = (i % (2 * half)) < half
        m[i[first] + half, i[first]] = -1.0
        m[i[~first] - half, i[~first]] = 1.0
        return m

    causal = np.where(i[None, :] <= i[:, None], 0.0, 1.0).astype(np.float32)
    heads = np.zeros((P, P), np.float32)
    heads[:HD, 0] = 1.0
    heads[HD:, 1] = 1.0
    mats = np.concatenate([ident, np.ones((P, P), np.float32), rotation(32), rotation(16), causal, heads], 1)

    def angles(pos, dim):
        inv = (10000.0 ** (-(np.arange(0, dim, 2, dtype=np.float32) / np.float32(dim)).astype(np.float64)))
        return pos.astype(np.float32)[:, None] * inv.astype(np.float32)[None, :]

    def tables(ang_rows):
        ang = np.stack(ang_rows).astype(np.float64)
        return np.cos(ang).astype(np.float32), np.sin(ang).astype(np.float32)

    t = np.arange(T)
    a64 = angles(t, 64)
    main = tables([a64[:, p % 32] for p in range(P)])
    a32 = angles(t, ROPE_D)
    lat = tables([a32[:, p % 16] if NOPE <= p < QW else np.zeros(T) for p in range(P)])
    row, col = angles(t // 64, 32), angles(t % 64, 32)
    grid = tables([(row if p % 64 < 32 else col)[:, p % 16] for p in range(P)])
    return mats, np.concatenate([np.stack(x, 1) for x in (main, lat, grid)], 1).reshape(P, 3, 2, T)


CONV_BANKS = ((1, 4, 5), (0, 2, 3))
ROUNDS = 3 * TOP_K // 8
GROUPED_ORDER = (4, 5, 0, 1, 2, 3)
IDX_SUM = [n // HEADS * (HEADS + 1) + n % HEADS + 1 for n in range(3 * HEADS)]


class NormSems:

    def __init__(self, sem):
        self.squares = sem("norm_squares")
        self.added = sem("norm_added")
        self.summed = sem("norm_summed")
        self.newton = sem("norm_newton")
        self.expand = sem("norm_expand")
        self.spread = sem("norm_spread")
        self.scale = sem("norm_scale")


class Norm:

    def __init__(self, before, chunks, copies, expands=1, heads=False):
        self.before, self.chunks, self.copies, self.expands, self.heads = before, chunks, copies, expands, heads
        self.adds, self.sums = (0, chunks) if heads else (chunks, 1)
        self.add0 = before.add0 + before.adds if before else 0
        self.sum0 = before.sum0 + before.sums if before else 0
        self.chunk0 = before.chunk0 + before.chunks if before else 0
        self.expand0 = before.expand0 + before.expands if before else 0
        self.scale0 = before.scale0 + before.copies if before else 0
        self.newton0 = before.newton0 + 2 + 3 * NEWTON_STEPS if before else 0

    def slot_user(self, k):
        norm, n = self, k - 2
        while n < 0:
            if norm.before is None:
                return None
            norm = norm.before
            n += norm.chunks
        return ("summed", norm.sum0 + n + 1) if norm.heads else ("added", norm.add0 + n + 1)


class Split:

    def __init__(self, sem, name):
        self.hi = sem(name + "_hi")
        self.lo = sem(name + "_lo")


class Entry:

    def __init__(self, split, n):
        self.hi, self.lo, self.first = split.hi, split.lo, n * KC


class FfnSems:

    def __init__(self, sem):
        self.gate = sem("ffn_gate")
        self.silu = sem("ffn_silu")
        self.up = sem("ffn_up")
        self.prod = sem("ffn_prod")
        self.hid = Split(sem, "ffn_hid")
        self.part = sem("ffn_part")
        self.full = sem("ffn_full")


class Ffn:

    def __init__(self, n):
        self.hid0, self.out0 = n * FF, n * KC


class Residual:

    def __init__(self, term, h, n):
        self.term = term
        self.h = h
        self.first = n * KC


class Rope:
    def __init__(self, sem, name):
        self.x = sem(name + "_x")
        self.cos = sem(name + "_cos")
        self.rot = sem(name + "_rot")
        self.sin = sem(name + "_sin")
        self.sum = sem(name + "_sum")
        self.out = Split(sem, name + "_out")


class AttentionSems:

    def __init__(self, sem):
        self.logits = sem("att_logits")
        self.top = sem("att_top")
        self.exp = sem("att_exp")
        self.inv = sem("att_inv")
        self.probs = sem("att_probs")
        self.turned = sem("att_turned")
        self.pt = Split(sem, "att_pt")
        self.pv = sem("att_pv")
        self.out = Split(sem, "att_out")


class Attention:

    def __init__(self, block0, piece0):
        self.block0, self.half0, self.piece0 = block0, block0 // 2, piece0


def build(nc, dram, out):
    base = -(-nc.sbuf_base // 32) * 32
    place = [base]

    def fixed(name, shape, dt):
        words = int(np.prod(shape[1:]))
        t = nc.alloc_sbuf_tensor_at(name, shape, dt, offset=place[0])
        place[0] += -(-words * 4 // 32) * 32
        return t

    mats = fixed("mats", [P, 6, P], F32)
    ident, ones, rot32, rot16, after_query, head_sel = (mats[:, n, :] for n in range(6))
    gains = fixed("gains", [P, GAIN_ROWS], F32)
    tab = fixed("rope_tab", [P, 2, T], F32)
    scale = fixed("scale", [P, T], F32)
    n_x = fixed("newton_x", [P, 48], F32)
    n_y = fixed("newton_y", [P, 48], F32)
    n_t = fixed("newton_t", [P, 48], F32)
    top = fixed("top", [P, 4], F32)
    sums = fixed("sums", [P, 4], F32)
    invs = fixed("invs", [P, 4], F32)
    w_idx = fixed("w_idx", [P, TB, HEADS], F32)
    best8 = fixed("best8", [P, 8], F32)
    mem_sq = fixed("mem_sq", [P, MB], F32)
    h = fixed("h", [P, KC, T], F32)
    mem_rows = nc.alloc_sbuf_tensor_at("mem_rows", [P, MB, D], F32, offset=place[0] + 4 * T * 4)
    xh = fixed("xh", [P, KC, T], F32R)
    mem_squares = nc.alloc_sbuf_tensor_at("mem_squares", [P, D], F32, offset=place[0] + 4 * T * 4)
    xl = fixed("xl", [P, KC, T], F32R)
    raw = fixed("ring_raw", [P, RING, UNIT], F32)
    wh = fixed("ring_hi", [P, RING, UNIT], F32R)
    wl = fixed("ring_lo", [P, RING, UNIT], F32R)
    arena = place[0]
    K = 1024

    def at(name, kib, shape, dt):
        offset = arena + int(kib * K)
        assert offset + int(np.prod(shape[1:])) * 4 <= nc.sbuf_usable_end, name
        return nc.alloc_sbuf_tensor_at(name, shape, dt, offset=offset)

    f = at("f", 0, [P, KC, T], F32)
    squares = at("squares", 80, [P, 2, T], F32)
    wa = at("work_a", 84, [P, 2, T], F32)
    wb = at("work_b", 88, [P, 2, T], F32)
    expand = at("expand", 92, [P, TB, P], F32)
    square_sum = expand[:].rearrange("p b c -> p (b c)")
    probs = at("probs", 94, [P, 3, T], F32)
    x_rows = at("x_rows", 16, [P, TB, D], F32)
    hid_h = at("hid_h", 16, [P, FF2_HALF, T], F32R)
    hid_l = at("hid_l", 48, [P, FF2_HALF, T], F32R)
    cz_h = at("cz_h", 67, [P, 4, T], F32R)
    cz_l = at("cz_l", 75, [P, 4, T], F32R)
    c_gb = at("c_gb", 32, [P, 2, T], F32)
    c_gc = at("c_gc", 36, [P, 2, T], F32)
    c_y = at("c_y", 40, [P, 2, T + 8], F32)
    c_z = at("c_z", 52, [P, 2, T], F32)
    mixed = at("mixed", 0, [P, KC, T], F32)
    qa_h = at("qa_h", 16, [P, 4, T], F32R)
    qa_l = at("qa_l", 24, [P, 4, T], F32R)
    qi_h = at("qi_h", 32, [P, 4, T], F32R)
    qi_l = at("qi_l", 40, [P, 4, T], F32R)
    a_pt_h = at("a_pt_h", 32, [P, 2, 4, 256], F32R)
    a_pt_l = at("a_pt_l", 40, [P, 2, 4, 256], F32R)
    ka_h = at("ka_h", 48, [P, T], F32R)
    ka_l = at("ka_l", 50, [P, T], F32R)
    ki_h = at("ki_h", 52, [P, T], F32R)
    ki_l = at("ki_l", 54, [P, T], F32R)
    va_h = at("va_h", 56, [P, TB, 192], F32R)
    va_l = at("va_l", 59, [P, TB, 192], F32R)
    v_cols = at("v_cols", 94, [P, T], F32)
    mask = at("mask", 62, [P, TB * (TB + 1) // 2 * P], F32)
    gate_a = at("gate_a", 67, [P, KC, T], F32)
    mm_h = at("mm_h", 32, [P, KC, T], F32R)
    mm_l = at("mm_l", 48, [P, KC, T], F32R)
    mg_h = at("mg_h", 16, [P, KC, T], F32R)
    mg_l = at("mg_l", 32, [P, KC, T], F32R)
    memt_h = at("memt_h", 16, [P, KC, N_MEM], F32R)
    memt_l = at("memt_l", 24, [P, KC, N_MEM], F32R)
    mk_h = at("mk_h", 32, [P, KC, N_MEM], F32R)
    mk_l = at("mk_l", 40, [P, KC, N_MEM], F32R)
    mv_h = at("mv_h", 48, [P, MB, D], F32R)
    mv_l = at("mv_l", 56, [P, MB, D], F32R)
    xq_h = at("xq_h", 0, [P, KC, T], F32R)
    xq_l = at("xq_l", 16, [P, KC, T], F32R)
    x_pt_h = at("x_pt_h", 64, [P, 2, MB, 256], F32R)
    x_pt_l = at("x_pt_l", 68, [P, 2, MB, 256], F32R)
    go_h = at("go_h", 0, [P, 4, T], F32R)
    go_l = at("go_l", 8, [P, 4, T], F32R)
    gq_h = at("gq_h", 16, [P, 4, T], F32R)
    gq_l = at("gq_l", 24, [P, 4, T], F32R)
    gk_h = at("gk_h", 32, [P, 2, T], F32R)
    gk_l = at("gk_l", 36, [P, 2, T], F32R)
    gv_h = at("gv_h", 40, [P, 2, TB, 192], F32R)
    gv_l = at("gv_l", 46, [P, 2, TB, 192], F32R)
    g_pt_h = at("g_pt_h", 52, [P, 2, 4, 256], F32R)
    g_pt_l = at("g_pt_l", 60, [P, 2, 4, 256], F32R)
    g_x = at("g_x", 68, [P, 6, T], F32)
    g_v = at("g_v", 94, [P, T], F32)
    cq_h = at("cq_h", 16, [P, 2, T], F32R)
    cq_l = at("cq_l", 20, [P, 2, T], F32R)
    ck_h = at("ck_h", 24, [P, T], F32R)
    ck_l = at("ck_l", 26, [P, T], F32R)
    lq_h = at("lq_h", 28, [P, 2, T], F32R)
    lq_l = at("lq_l", 32, [P, 2, T], F32R)
    lk_h = at("lk_h", 36, [P, 2, T], F32R)
    lk_l = at("lk_l", 40, [P, 2, T], F32R)
    lv_h = at("lv_h", 44, [P, TB, 192], F32R)
    lv_l = at("lv_l", 47, [P, TB, 192], F32R)
    l_pt_h = at("l_pt_h", 50, [P, 2, 4, 256], F32R)
    l_pt_l = at("l_pt_l", 58, [P, 2, 4, 256], F32R)
    l_x = at("l_x", 66, [P, 4, T], F32)
    l_q = at("l_q", 84, [P, 2, T], F32)
    lo_h = at("lo_h", 66, [P, 4, T], F32R)
    lo_l = at("lo_l", 74, [P, 4, T], F32R)
    gate_stage = at("gate_stage", 82, [P, T], F32)
    gates_back = at("gates_back", 48, [P, 4, 2, T], F32)
    gate_store = nc.dram_tensor("gate_store", (2 * KC, P, T), F32, kind="Internal").ap()
    p_rows = at("p_rows", 0, [P, TB, PLE], F32)
    pt_h = at("pt_h", 4, [P, 2, T], F32R)
    pt_l = at("pt_l", 8, [P, 2, T], F32R)
    ple = at("ple", 16, [P, KC, T], F32)
    normed = at("normed", 0, [P, KC, T], F32)
    out_rows = at("out_rows", 32, [P, TB, D], F32)

    def mask_of(b):
        lo = b * (b + 1) // 2 * P
        return mask[:, lo:lo + (b + 1) * P]

    def gain(name, k):
        row = GAINS.index(name) * KC + k
        return gains[:, row:row + 1]

    def gain_row(row):
        return gains[:, row:row + 1]

    with ExitStack() as ctx:
        def sem(name):
            return ctx.enter_context(nc.semaphore(name))

        bank = [ctx.enter_context(nc.psum_tensor(f"bank{n}", [P, T], F32)) for n in range(8)]
        SPREAD, SUMS = 6, 7

        raw_in = [sem(f"raw_in{s}") for s in range(RING)]
        hi_ready = sem("hi_ready")
        lo_ready = sem("lo_ready")
        unit_used = sem("unit_used")
        const_in = sem("const_in")
        x_in = [sem(f"x_in{n}") for n in range(2)]
        mem_in = sem("mem_in")
        p_in = sem("p_in")
        tab_in = sem("tab_in")
        out_sent = sem("out_sent")
        gains_in = sem("gains_in")
        x_turned = sem("x_turned")
        x_kept = sem("x_kept")
        norm = NormSems(sem)
        n_ffn1 = Norm(None, KC, 1)
        n_ffn1p = Norm(n_ffn1, KC, 0)
        n_mix = Norm(n_ffn1p, KC, 1)
        n_mixp = Norm(n_mix, KC, 0)
        n_xq = Norm(n_mixp, KC, 1)
        n_xp = Norm(n_xq, KC, 0)
        n_ffn2 = Norm(n_xp, KC, 1)
        n_ffn2p = Norm(n_ffn2, KC, 0)
        n_mix2 = Norm(n_ffn2p, KC, 1)
        n_heads = Norm(n_mix2, 6, 0, expands=6, heads=True)
        n_cq = Norm(n_heads, LAT_Q // P, 0)
        n_ckv = Norm(n_cq, 1, 0)
        n_mlp = Norm(n_ckv, KC, 1)
        n_ple = Norm(n_mlp, KC, 1)
        n_end = Norm(n_ple, KC, 0)
        n_mem = sem("n_mem")
        entry = Split(sem, "entry")
        x_ffn1, x_mix, x_x, x_ffn2, x_mix2, x_mlp, x_ple = (Entry(entry, n) for n in range(7))
        ffn = FfnSems(sem)
        ffn1, ffn2 = Ffn(0), Ffn(1)
        normed_term, h_added = sem("normed_term"), sem("h_added")
        r_ffn1, r_mix, r_x, r_ffn2 = (Residual(normed_term, h_added, n) for n in range(4))
        conv_step = sem("conv_step")
        conv_tap = sem("conv_tap")
        conv_out = Split(sem, "conv_out")
        mc_gate, mc_sig, mc_sum = sem("mc_gate"), sem("mc_sig"), sem("mc_sum")
        rope = Rope(sem, "rope")
        v_scaled, v_turned, v_split = sem("v_scaled"), sem("v_turned"), Split(sem, "v_split")
        v_zero = sem("v_zero")
        idx_raw, idx_relu, idx_sum = sem("idx_raw"), sem("idx_relu"), sem("idx_sum")
        taken = sem("taken")
        masked = sem("masked")
        ga_scaled, ga_sig = sem("ga_scaled"), sem("ga_sig")
        att = AttentionSems(sem)
        HB = HEADS * TB
        a_main, a_mem = Attention(0, 0), Attention(HB, HEADS)
        a_grp = Attention(HB + XH * TB, HEADS + 4 * XH)
        a_lat = Attention(2 * HB + XH * TB, 2 * HEADS + 4 * XH)
        ma_term, ma_sum, merged = sem("ma_term"), sem("ma_sum"), Split(sem, "merged")
        mo_full = sem("mo_full")
        mem_sum, mem_normed, mem_turned = sem("mem_sum"), sem("mem_normed"), sem("mem_turned")
        memt, mk, mv = Split(sem, "memt"), Split(sem, "mk"), Split(sem, "mv")
        xq_scaled, xq = sem("xq_scaled"), Split(sem, "xq")
        xo_full = sem("xo_full")
        gx, gx_normed = Rope(sem, "gx"), sem("gx_normed")
        gv_scaled, gv_turned, gv = sem("gv_scaled"), sem("gv_turned"), Split(sem, "gv")
        lx, l_normed, l_lat = sem("lx"), sem("l_normed"), Split(sem, "l_lat")
        kpe = Rope(sem, "kpe")
        lq, lk, lv = Rope(sem, "lq"), Split(sem, "lk"), Split(sem, "lv")
        gate_scaled, gate_sig = sem("gate_scaled"), sem("gate_sig")
        gate_out = sem("gate_out")
        gate_in = [sem(f"gate_in{n}") for n in range(4)]
        me_term, me_sum = sem("me_term"), sem("me_sum")
        merged2 = Split(sem, "merged2")
        h_out = sem("h_out")
        p_turned, p_split = sem("p_turned"), Split(sem, "p_split")
        ml_x, ml_sq, ml_hid = sem("ml_x"), sem("ml_sq"), Split(sem, "ml_hid")
        ml_part, h_mlp = sem("ml_part"), sem("h_mlp")
        ple_kept, pg_x, pg_sig, pg_term, h_end = (sem(n) for n in ("ple_kept", "pg_x", "pg_sig", "pg_term", "h_end"))
        end_normed, end_turned, end_kept = sem("end_normed"), sem("end_turned"), sem("end_kept")

        block = ctx.enter_context(nc.Block())

        def landed(u):
            return 16 * (u // RING + 1 + sum(v <= u and v % RING == u % RING for v in TWO_PART))

        def done(u, i=None):
            return u + 2 if i is None else 4 * i + (u + 2)

        @block.sync
        def _(sp):
            def load(u, src, width, i=None, at_col=0):
                if i is not None:
                    sp.wait_ge(lo_ready, 4 * i + (u - RING + 1))
                elif u >= RING:
                    sp.wait_ge(lo_ready, u - RING + 1)
                dst = raw[:, u % RING, at_col:at_col + src.shape[1] * width].rearrange("p (k c) -> p k c", c=width)
                return sp.dma_start(dst, src)

            def rows(name, c0, width=P, k0=0, nk=KC):
                w = dram[name][0][k0 * P:(k0 + nk) * P]
                return w.rearrange("(k p) c -> p k c", p=P)[:, :, c0:c0 + width]

            def rows_at(name, c0, width=P, k0=0, nk=KC):
                w = dram[name][0][k0 * P:(k0 + nk) * P]
                return w.rearrange("(k p) c -> p k c", p=P)[:, :, bass.ds(c0, width)]

            def fetch(u, src, width):
                load(u, src, width).then_inc(raw_in[u % RING], 16)

            def loop(first, turns, source, peel=False):
                def turn(i, static):
                    for q in range(RING):
                        load(first + q, source(i, q), P, None if static else i).then_inc(raw_in[(first + q) % RING], 16)
                if peel:
                    turn(0, True)
                with sp.Fori(1 if peel else 0, turns) as i:
                    turn(i, False)

            def feed_forward(name):
                w1, w3, w2 = name + "_w1", name + "_w3", name + "_w2"

                def up(j0):
                    return lambda i, q: rows_at((w1, w3)[q % 2], i * (2 * P) + (j0 + q // 2) * P)
                loop(FIRST[name + "_up_a"], FF_A // 2, up(0), peel=FIRST[name + "_up_a"] == 0)
                loop(FIRST[name + "_down_a"], KC // 2, lambda i, q: rows_at(w2, i * (2 * P) + q // 2 * P, k0=q % 2 * KC))
                loop(FIRST[name + "_up_b"], FF_B // 2, up(FF_A))
                loop(FIRST[name + "_down_b"], KC // RING, lambda i, q: rows_at(w2, i * (4 * P) + q * P, k0=FF_A, nk=FF_B))

            for b in range(TB // 2, TB):
                sp.dma_start(x_rows[:, b, :], dram["x"][0, b * P:(b + 1) * P, :]).then_inc(x_in[1], 16)
            feed_forward("ffn1")
            def fetch_twin(u, name, c0):
                dst = raw[:, u % RING, :].rearrange("p (k c) -> p k c", c=P)
                sp.wait_ge(lo_ready, u - RING + 1)
                sp.dma_start(dst[:, :, 0:HD], rows(name, c0, HD)).then_inc(raw_in[u % RING], 16)
                sp.dma_start(dst[:, :, HD:P], rows(name, c0, HD)).then_inc(raw_in[u % RING], 16)

            u = FIRST["index"]
            for c in range(4):
                fetch(u + c, rows("w_in", C_QI + c * P), P)
            fetch_twin(u + 4, "w_in", C_KI)
            u = FIRST["values"]
            dst = raw[:, u % RING, :].rearrange("p (k c) -> p k c", c=P)
            sp.wait_ge(lo_ready, u - RING + 1)
            sp.dma_start(dst[:, :, 0:HD], rows("w_in", C_VA, HD)).then_inc(raw_in[u % RING], 16)
            sp.dma_start(dst[:, :, HD:HD + HEADS], rows("w_in", C_WI, HEADS)).then_inc(raw_in[u % RING], 16)
            u = FIRST["queries"]
            for c in range(4):
                fetch(u + c, rows("w_in", C_QA + c * P), P)
            fetch_twin(u + 4, "w_in", C_KA)
            u = FIRST["conv"]
            for j in range(4):
                for q, c in enumerate((C_GB, C_GC, C_CI)):
                    fetch(u + 3 * j + q, rows("w_in", c + j * P), P)
            u = FIRST["merge_conv"]
            for p in range(4):
                for q in range(2):
                    fetch(u + 3 * p + q, rows("w_in", C_GBB + (2 * p + q) * P), P)
                fetch(u + 3 * p + 2, rows("w_b_out", 2 * P * p, 2 * P, nk=4), 2 * P)
            for m in range(KC):
                fetch(FIRST["gate_a"] + m, rows("w_in", C_GA + m * P), P)
            for p in range(4):
                fetch(FIRST["attn_out"] + p, rows("w_a_out", 2 * P * p, 2 * P, nk=4), 2 * P)
            for m in range(KC):
                fetch(FIRST["mix_out"] + m, rows("w_out", m * P), P)
            for m in range(KC):
                fetch(FIRST["mem_k"] + m, rows("xattn_w_kv", m * P), P)
            for n in range(8):
                fetch(FIRST["mem_v"] + n, rows("xattn_w_kv", D + n // 4 * T, T, k0=2 * (n % 4), nk=2), T)
            for m in range(KC):
                fetch(FIRST["x_q"] + m, rows("xattn_w_q", m * P), P)
            for m in range(KC):
                fetch(FIRST["x_out"] + m, rows("xattn_w_o", m * P), P)
            feed_forward("ffn2")
            u = FIRST["grouped"]
            for c in range(4):
                fetch(u + c, rows("w_in_2", Z_QB + c * P), P)
            for kv in range(2):
                fetch_twin(u + 4 + kv, "w_in_2", Z_KB + kv * HD)
            fetch(u + 6, rows("w_in_2", Z_VB), P)
            def fetch_gate(g):
                fetch(gate_unit(g), rows("w_in_2", (Z_GA, Z_GB)[g % 2] + g // 2 * P), P)

            for g in range(8):
                fetch_gate(g)
            u = FIRST["latent"]
            for c in range(2):
                fetch(u + c, rows("w_in_2", Z_QL + c * P), P)
            fetch(u + 2, rows("w_in_2", Z_KVL), P)
            fetch(u + 3, rows("w_in_2", Z_KPE - NOPE), P)
            for g in (8, 9):
                fetch_gate(g)
            for c in range(4):
                u = FIRST["latent_heads"] + HEAD_UNITS[c]
                load(u, rows("w_qb_2", 2 * c * QW, 2 * QW, nk=2), 2 * QW).then_inc(raw_in[u % RING], 16)
                sp.dma_start(raw[:, u % RING, 4 * QW:4 * QW + 2 * P],
                             dram["w_kvb_2"][0][:, 2 * c * P:2 * (c + 1) * P]).then_inc(raw_in[u % RING], 16)
                fetch_gate(PAIR_GATE[c])
                if c in PAIR_GATE_2:
                    fetch_gate(PAIR_GATE_2[c])
            for p in range(4):
                u = FIRST["merge"] + 2 * p
                fetch(u, rows("w_oa_2", 2 * P * p, 2 * P, nk=4), 2 * P)
                fetch(u + 1, rows("w_ob_2", 2 * P * p, 2 * P, nk=4), 2 * P)
            for m in range(KC):
                fetch(FIRST["out"] + m, rows("w_o_2", m * P), P)
            for half in "ab":
                j0 = FF2_HALF * "ab".index(half)
                loop(FIRST["mlp_up_" + half], FF2_HALF // RING,
                     lambda i, q: rows_at("w_up_2", i * (4 * P) + (j0 + q) * P))
                loop(FIRST["mlp_down_" + half], KC // 2,
                     lambda i, q: rows_at("w_down_2", i * (2 * P) + q // 2 * P, k0=j0 + q % 2 * KC))
            for n in range(2):
                fetch(FIRST["ple"] + n, rows("w_ple_2", n * T, T, nk=2), T)
            for m in range(KC):
                fetch(FIRST["ple_gate"] + m, rows("w_ple_gate_2", m * P), P)
            sp.wait_ge(end_kept, KC)
            for b in range(TB):
                sp.dma_start(out[0, b * P:(b + 1) * P, :], out_rows[:, b, :]).then_inc(out_sent, 16)
            sp.wait_ge(out_sent, 16 * TB)

        @block.gpsimd
        def _(pool):
            with pool.Fori(0, UNITS // RING) as i:
                for s in range(RING):
                    pool.wait_ge(hi_ready, 4 * i + (s + 1))
                    pool.tensor_tensor(wl[:, s, :], raw[:, s, :], wh[:, s, :].bitcast(F32),
                                       ALU.subtract).then_inc(lo_ready, 1)

        @block.tensor
        def _(pe):
            def three(to, a_hi, a_lo, b_hi, b_lo, start, stop):
                pe.matmul(to, a_hi, b_hi, start=start, stop=False, skip_group_check=True)
                pe.matmul(to, a_hi, b_lo, start=False, stop=False, skip_group_check=True)
                return pe.matmul(to, a_lo, b_hi, start=False, stop=stop, skip_group_check=True)

            def unit(u, i=None):
                pe.wait_ge(lo_ready, u + 1 if i is None else 4 * i + (u + 1))
                return wh[:, u % RING, :], wl[:, u % RING, :]

            def columns(u, to, hi, lo, ks, i=None, start=True, stop=True, width=P, at_col=0, use=True, before=None):
                w_h, w_l = unit(u, i)
                for n, k in enumerate(ks):
                    if before is not None:
                        before(k)
                    c = n * width + at_col
                    last = three(to, w_h[:, c:c + P], w_l[:, c:c + P], hi[:, k, :], lo[:, k, :],
                                 start and n == 0, stop and n == len(ks) - 1)
                if use:
                    last.then_inc(unit_used, 1)

            def sum_squares(N, column=0):
                pe.wait_ge(norm.added, N.add0 + N.chunks)
                for b in range(TB):
                    last = pe.matmul(bank[SUMS][:, column + b:column + b + 1], square_sum[:, b * P:(b + 1) * P], ones[:, 0:1],
                                     start=b == 0, stop=False, skip_group_check=True)
                last.then_inc(norm.summed, 1)

            def spread(N, to=SPREAD):
                pe.wait_ge(norm.expand, N.expand0 + 1)
                pe.matmul(bank[to][:], ones, expand[:].rearrange("p b c -> p (b c)"), start=True, stop=True
                          ).then_inc(norm.spread, 1)

            def entering(X):
                return lambda k: pe.wait_ge(X.lo, X.first + k + 1)

            def entry(X, N, u):
                weights = [unit(u + q) for q in range(RING)]

                def product(q, k):
                    c = slice(k * P, (k + 1) * P)
                    return three(bank[q][:], weights[q][0][:, c], weights[q][1][:, c], xh[:, k, :], xl[:, k, :],
                                 k == 0, k == KC - 1)
                for k in range(KC - 2):
                    pe.wait_ge(X.lo, X.first + k + 1)
                    for q in range(RING):
                        product(q, k)
                for q in range(RING):
                    for k in range(KC - 2, KC):
                        if q == 0:
                            pe.wait_ge(X.lo, X.first + k + 1)
                        last = product(q, k)
                    last.then_inc(unit_used, 1)
                    if q == 1:
                        sum_squares(N)
                spread(N)

            def rotate(R, n, x, m, to, rows=slice(0, P)):
                pe.wait_ge(R.x, n + 1)
                pe.matmul(bank[to][rows, :], m[rows, rows], x, start=True, stop=True).then_inc(R.rot, 1)

            def feed_forward(name, S, X, N, NP):
                u = FIRST[name + "_up_a"]

                def up(u, j, i):
                    for q in range(RING):
                        pe.wait_ge((ffn.gate, ffn.up)[q % 2], 2 * i + (S.hid0 + j + q // 2 - 1))
                        columns(u + q, bank[q][:], xh, xl, range(KC), i)

                entry(X, N, u)
                with pe.Fori(1, FF_A // 2) as i:
                    up(u, 0, i)
                u = FIRST[name + "_down_a"]

                def down(i, first=False):
                    for q in range(RING):
                        if q % 2 == 0 and not first:
                            pe.wait_ge(ffn.part, 2 * i + (S.out0 + q // 2 - 1))
                        columns(u + q, bank[4 + q // 2][:], hid_h, hid_l, range(q % 2 * KC, q % 2 * KC + KC), i,
                                start=q % 2 == 0, stop=q % 2 == 1,
                                before=(lambda k: pe.wait_ge(ffn.hid.lo, S.hid0 + k + 1)) if first and q < 2 else None)
                down(None, first=True)
                with pe.Fori(1, KC // 2) as i:
                    down(i)
                with pe.Fori(0, FF_B // 2) as i:
                    up(FIRST[name + "_up_b"], FF_A, i)
                u = FIRST[name + "_down_b"]
                for m in range(KC):
                    if m == 0:
                        pe.wait_ge(ffn.part, S.out0 + KC)
                    elif m >= 2:
                        pe.wait_ge(ffn.full, S.out0 + m - 1)
                    columns(u + m, bank[4 + m % 2][:], hid_h, hid_l, range(FF_B),
                            before=(lambda k: pe.wait_ge(ffn.hid.lo, S.hid0 + FF_A + k + 1)) if m == 0 else None)
                sum_squares(NP)
                spread(NP)

            def attention(A, blocks, logits, blocks_of_keys, values, exp_reads_psum=True, lead=None):
                lo, hi = blocks
                for n in range(lo, hi + 6):
                    r = A.block0 + n
                    if n < hi:
                        if n >= lo + 3:
                            pe.wait_ge(att.exp if exp_reads_psum else att.top, r - 2)
                        if lead is not None:
                            lead(n)
                        logits(n, bank[n % 3]).then_inc(att.logits, 1)
                    m, r = n - 3, A.block0 + n - 3
                    if lo <= m < hi:
                        pe.wait_ge(att.probs, r + 1)
                        if m >= lo + 2:
                            pe.wait_ge(att.pt.lo, r - 1)
                        for s in range(blocks_of_keys(m)):
                            last = pe.transpose(bank[3 + m % 2][:, s * P:(s + 1) * P],
                                                probs[:, r % 3, s * P:(s + 1) * P], ident)
                        last.then_inc(att.turned, 1)
                    if (n - 6) % 2 == 0 and lo <= n - 6 < hi:
                        g = (n - 6) // 2
                        pe.wait_ge(att.pt.lo, A.block0 + 2 * g + 2)
                        values(g).then_inc(att.pv, 1)

            def paired_values(A, g, key_blocks, v_of, p_h, p_l, first_pair=0):
                head, half = g // 2, g % 2
                par, pair = head % 2, head // 2
                if par == 0 and pair > first_pair:
                    pe.wait_ge(att.out.lo, A.piece0 + 2 * (pair - 1) + half + 1)
                slot = (A.half0 + g) % 2
                n_s = key_blocks(2 * g + 1)
                for s in range(n_s):
                    c = max(0, (s - 2 * half) * P) if n_s != TB or key_blocks(2 * g) != TB else 0
                    v_h, v_l = v_of(head, s)
                    last = three(bank[5 + half][:, c:256], v_h[:, par * HD:par * HD + P], v_l[:, par * HD:par * HD + P],
                                 p_h[:, slot, s, c:256], p_l[:, slot, s, c:256],
                                 par == 0 and s == 0, par == 1 and s == n_s - 1)
                return last

            pe.wait_ge(const_in, 16)
            for x_part in x_in:
                pe.wait_ge(x_part, 16 * TB // 2)
            for k in range(KC):
                for b in range(TB):
                    last = pe.transpose(bank[k][:, b * P:(b + 1) * P], x_rows[:, b, k * P:(k + 1) * P], ident)
                last.then_inc(x_turned, 1)
            pe.wait_ge(x_kept, KC)
            pe.transpose(bank[7][:, 0:P], ident, ident).then_inc(unit_used, 1)

            feed_forward("ffn1", ffn1, x_ffn1, n_ffn1, n_ffn1p)

            def roped(r):
                if r > 4:
                    pe.wait_ge(rope.x, r - 3)
                u = FIRST["index"] + r if r < 5 else FIRST["queries"] + r - 5
                columns(u, bank[7 if r == 4 else r % 4][:], xh, xl, range(KC))

            def turn(r):
                if r >= 2:
                    pe.wait_ge(rope.sin, r - 1)
                rotate(rope, r, wa[:, r % 2, :], rot32, 4 + r % 2)

            def conv(n):
                j, q = n // 3, n % 3
                if q == 0 and j == 0:
                    pe.wait_ge(rope.x, 10)
                elif q > 0 and j == 0:
                    pe.wait_ge(rope.sin, 8 + q)
                elif q == 0 and j >= 2:
                    pe.wait_ge(conv_step, 7 * (j - 2) + 3)
                columns(FIRST["conv"] + n, bank[CONV_BANKS[j % 2][q]][:], xh, xl, range(KC))

            entry(x_mix, n_mix, FIRST["index"])
            roped(4)
            turn(0)
            turn(1)
            width = HD + HEADS
            w_h, w_l = unit(FIRST["values"])
            pe.wait_ge(norm.scale, n_mix.scale0 + 1)
            for k in range(KC):
                w = slice(k * P, k * P + width)
                last = three(bank[6][0:width, :], w_h[:, w], w_l[:, w], xh[:, k, :], xl[:, k, :], k == 0, k == KC - 1)
            last.then_inc(unit_used, 1)
            turn(2)
            roped(5)
            pe.wait_ge(v_scaled, 1)
            for b in range(TB):
                last = pe.transpose(bank[6][:, b * width:(b + 1) * width], v_cols[0:width, b * P:(b + 1) * P],
                                    ident[0:width, 0:width])
            last.then_inc(v_turned, 1)
            for r in range(3, 8):
                turn(r)
                if r < 7:
                    roped(r + 3)
            conv(0)
            turn(8)
            turn(9)
            conv(1)
            conv(2)
            idx_bank = (0, 2, 3, 7)
            pe.wait_ge(rope.out.lo, 5)
            for n in range(3 * HEADS):
                b, head = n // HEADS + 1, n % HEADS
                if n >= 4:
                    pe.wait_ge(idx_relu, n - 3)
                half = slice(head % 2 * HD, head % 2 * HD + HD)
                q = slice(b * P, (b + 1) * P)
                three(bank[idx_bank[n % 4]][:, 0:(b + 1) * P], qi_h[half, head // 2, q], qi_l[half, head // 2, q],
                      ki_h[half, 0:(b + 1) * P], ki_l[half, 0:(b + 1) * P], True, True).then_inc(idx_raw, 1)

            pe.wait_ge(idx_relu, 3 * HEADS)
            for n in range(3, 12):
                conv(n)
            u = FIRST["merge_conv"]
            for p in range(4):
                b0 = 4 * ((p + 1) % 2)
                if p == 1:
                    pe.wait_ge(conv_step, 7 * 3 + 3)
                elif p >= 2:
                    pe.wait_ge(mc_sum, 2 * p - 2)
                for q in range(2):
                    columns(u + 3 * p + q, bank[b0 + 2 + q][:], xh, xl, range(KC))
                if p == 0:
                    pe.wait_ge(conv_out.lo, 4)
                for q in range(2):
                    columns(u + 3 * p + 2, bank[b0 + q][:], cz_h, cz_l, range(4), width=2 * P, at_col=q * P, use=q == 1)

            def main_logits(n, to):
                head, b = n // TB, n % TB
                half = slice(head % 2 * HD, head % 2 * HD + HD)
                q = slice(b * P, (b + 1) * P)
                return three(to[:, 0:(b + 1) * P], qa_h[half, head // 2, q], qa_l[half, head // 2, q],
                             ka_h[half, 0:(b + 1) * P], ka_l[half, 0:(b + 1) * P], True, True)

            def main_gate(n):
                if n % TB == TB - 1:
                    m = n // TB
                    if m:
                        pe.wait_ge(ga_scaled, m)
                    columns(FIRST["gate_a"] + m, bank[7][:], xh, xl, range(KC))

            pe.wait_ge(mc_sum, KC)
            pe.wait_ge(rope.out.lo, 10)
            pe.wait_ge(v_split.lo, 2)
            attention(a_main, (0, HB), main_logits, lambda n: n % TB + 1,
                      lambda g: paired_values(a_main, g, lambda n: n % TB + 1,
                                              lambda head, s: (va_h[:, s, :], va_l[:, s, :]), a_pt_h, a_pt_l),
                      exp_reads_psum=False, lead=main_gate)
            pe.wait_ge(att.out.lo, a_main.piece0 + HEADS)
            for p in range(4):
                for q in range(2):
                    if p >= 2 and q == 0:
                        pe.wait_ge(ma_term, 2 * (p - 1))
                    columns(FIRST["attn_out"] + p, bank[(2 * p + q) % 4][:], qa_h, qa_l, range(4), width=2 * P, at_col=q * P,
                            use=q == 1)

            pe.wait_ge(mem_normed, MB)
            pe.wait_ge(ga_scaled, KC)
            for c in range(4):
                for k in (2 * c, 2 * c + 1):
                    for b in range(MB):
                        last = pe.transpose(bank[4 + c][:, (k % 2) * N_MEM + b * P:(k % 2) * N_MEM + (b + 1) * P],
                                            mem_rows[:, b, k * P:(k + 1) * P], ident)
                last.then_inc(mem_turned, 1)

            def out_projection(u, full, hi, lo, ready, b0):
                for m in range(KC):
                    if m >= 2:
                        pe.wait_ge(full, m - 1)
                    columns(u + m, bank[b0 + m % 2][:], hi, lo, range(KC), before=ready if m == 0 else None)

            pe.wait_ge(ma_term, KC)
            out_projection(FIRST["mix_out"], mo_full, mm_h, mm_l, lambda k: pe.wait_ge(merged.lo, k + 1), 2)

            pe.wait_ge(memt.lo, KC)
            for m in range(KC):
                if m >= 4:
                    pe.wait_ge(mk.lo, m - 3)
                elif m == 2:
                    pe.wait_ge(mo_full, KC)
                columns(FIRST["mem_k"] + m, bank[m % 4][:, 0:N_MEM], memt_h, memt_l, range(KC))
                if m == 0:
                    sum_squares(n_mixp)
                if m == 2:
                    spread(n_mixp)
            for n in range(8):
                c, q = n // 4, n % 4
                if q == 0:
                    if c == 1:
                        pe.wait_ge(mk.lo, KC)
                w_h, w_l = unit(FIRST["mem_v"] + n)
                for kk in range(2):
                    k = 2 * q + kk
                    for b in range(MB):
                        last = three(bank[(4, 0)[c] + b][:], memt_h[:, k, b * P:(b + 1) * P], memt_l[:, k, b * P:(b + 1) * P],
                                     w_h[:, kk * T:(kk + 1) * T], w_l[:, kk * T:(kk + 1) * T], k == 0, k == KC - 1)
                last.then_inc(unit_used, 1)
            for m in range(KC):
                if m == 0:
                    pe.wait_ge(mk.lo, KC)
                elif m == 2:
                    pe.wait_ge(mv.lo, 4)
                elif m >= 4:
                    pe.wait_ge(xq_scaled, m - 3)
                columns(FIRST["x_q"] + m, bank[(2 + m) % 4][:], xh, xl, range(KC),
                        before=entering(x_x) if m == 0 else None)
                if m == 0:
                    sum_squares(n_xq)
                if m == 1:
                    spread(n_xq)

            def mem_logits(n, to):
                head, b = n // TB, n % TB
                q = slice(b * P, (b + 1) * P)
                for k in (2 * head, 2 * head + 1):
                    last = three(to[:, 0:N_MEM], xq_h[:, k, q], xq_l[:, k, q], mk_h[:, k, :], mk_l[:, k, :],
                                 k % 2 == 0, k % 2 == 1)
                return last

            def mem_values(g):
                head, slot = g // 2, (a_mem.half0 + g) % 2
                if g >= 1:
                    pe.wait_ge(att.out.lo, a_mem.piece0 + 2 * g)
                for c in range(2):
                    f0 = head * XD + c * P
                    for s in range(MB):
                        last = three(bank[5 + c][:, 0:256], mv_h[:, s, f0:f0 + P], mv_l[:, s, f0:f0 + P],
                                     x_pt_h[:, slot, s, :], x_pt_l[:, slot, s, :], s == 0, s == MB - 1)
                return last

            pe.wait_ge(xq.lo, KC)
            attention(a_mem, (0, XH * TB), mem_logits, lambda n: MB, mem_values)
            pe.wait_ge(att.out.lo, a_mem.piece0 + 4 * XH)
            out_projection(FIRST["x_out"], xo_full, xh, xl, None, 4)
            sum_squares(n_xp)
            spread(n_xp)

            feed_forward("ffn2", ffn2, x_ffn2, n_ffn2, n_ffn2p)

            def turn_grouped(n):
                if n >= 2:
                    pe.wait_ge(gx.sin, n - 1)
                pe.wait_ge(gx_normed, n + 1)
                pe.matmul(bank[n % 2][:], rot16, g_x[:, GROUPED_ORDER[n], :], start=True, stop=True).then_inc(gx.rot, 1)

            def gate(g, to, banks=1):
                if g >= banks:
                    pe.wait_ge(gate_scaled, g - banks + 1)
                columns(gate_unit(g), bank[to][:], xh, xl, range(KC))

            def head_squares(r):
                c = n_heads.chunk0 + r
                pe.wait_ge(norm.squares, c + 1)
                for b in range(TB):
                    to = bank[SUMS][:, 12 * b + 2 * r:12 * b + 2 * r + 2]
                    last = pe.matmul(to, squares[:, c % 2, b * P:(b + 1) * P], head_sel[:, 0:2],
                                     start=r == 0 and b == 0, stop=False, skip_group_check=True)
                last.then_inc(norm.summed, 1)

            entry(x_mix2, n_mix2, FIRST["grouped"])
            for r in (4, 5):
                pe.wait_ge(gx.x, r - 3)
                columns(FIRST["grouped"] + r, bank[r % 4][:], xh, xl, range(KC))
                head_squares(2 * r - 8)
                head_squares(2 * r - 7)
            pe.wait_ge(norm.scale, n_mix2.scale0 + 1)
            columns(FIRST["grouped"] + 6, bank[6][:], xh, xl, range(KC))
            head_squares(4)
            head_squares(5)
            pe.wait_ge(gv_scaled, 1)
            for b in range(TB):
                last = pe.transpose(bank[6][:, b * P:(b + 1) * P], g_v[:, b * P:(b + 1) * P], ident)
            last.then_inc(gv_turned, 1)
            for n in range(6):
                if n >= 2:
                    pe.wait_ge(gx_normed, n - 1)
                pe.wait_ge(norm.expand, n_heads.expand0 + n + 1)
                for b in range(TB):
                    last = pe.matmul(bank[4 + n % 2][:, b * P:(b + 1) * P], expand[:, b, :], ident, start=True, stop=True)
                last.then_inc(norm.spread, 1)
                if n == 0:
                    pe.wait_ge(gx.x, 4)
                gate(n, 2 + n % 2, 2)
                if n >= 1:
                    turn_grouped(n - 1)
            turn_grouped(5)
            pe.wait_ge(gate_scaled, 6)

            def grp_logits(n, to):
                head, b = n // TB, n % TB
                half = slice(head % 2 * HD, head % 2 * HD + HD)
                q, kv = slice(b * P, (b + 1) * P), head // 4
                return three(to[:], gq_h[half, head // 2, q], gq_l[half, head // 2, q],
                             gk_h[half, kv, :], gk_l[half, kv, :], True, True)

            pe.wait_ge(gx.out.lo, 6)
            pe.wait_ge(gv.lo, 4)
            attention(a_grp, (0, HB), grp_logits, lambda n: TB,
                      lambda g: paired_values(a_grp, g, lambda n: TB,
                                              lambda head, s: (gv_h[:, head // 4, s, :], gv_l[:, head // 4, s, :]),
                                              g_pt_h, g_pt_l),
                      lead=lambda n: gate(GROUPED_GATES[n], 7) if n in GROUPED_GATES else None)

            u = FIRST["latent"]
            pe.wait_ge(att.exp, a_grp.block0 + HB)
            for r in range(4):
                if r == 3:
                    pe.wait_ge(att.pt.lo, a_grp.block0 + HB)
                columns(u + r, bank[r][:], xh, xl, range(KC))
            pe.wait_ge(gate_scaled, 8)
            sum_squares(n_cq)
            pe.wait_ge(kpe.x, 1)
            gate(8, 2)
            spread(n_cq)
            sum_squares(n_ckv, 8)
            rotate(kpe, 0, l_x[:, 3, :], rot16, 4)
            pe.wait_ge(att.out.lo, a_grp.piece0 + HEADS)
            spread(n_ckv, 5)
            gate(9, 3, 2)

            def lat_heads(c):
                w_h, w_l = unit(FIRST["latent_heads"] + HEAD_UNITS[c])
                if c >= 1:
                    pe.wait_ge(att.exp, a_lat.block0 + 2 * TB * c)
                else:
                    pe.wait_ge(gate_scaled, 10)
                for q in range(2):
                    for k in range(2):
                        w = slice(k * 2 * QW + q * QW, k * 2 * QW + (q + 1) * QW)
                        three(bank[q][0:QW, :], w_h[:, w], w_l[:, w], cq_h[:, k, :], cq_l[:, k, :], k == 0, k == 1)
                kv0 = 4 * QW
                for q in range(2):
                    if c >= 1 and q == 1:
                        pe.wait_ge(att.pt.lo, a_lat.block0 + 2 * TB * c)
                    w = slice(kv0 + q * P, kv0 + (q + 1) * P)
                    three(bank[2 + q][:], w_h[:, w], w_l[:, w], ck_h[:], ck_l[:], True, True)
                if c >= 1:
                    pe.wait_ge(att.out.lo, a_lat.piece0 + 2 * c)
                v_h, v_l = (w[:, kv0:kv0 + 2 * P].rearrange("p (h c) -> p h c", c=P)[:, :, NOPE:P] for w in (w_h, w_l))
                for b in range(TB):
                    last = three(bank[6][:, b * P:(b + 1) * P].rearrange("p (h c) -> p h c", c=HD),
                                 ck_h[:, b * P:(b + 1) * P], ck_l[:, b * P:(b + 1) * P], v_h, v_l, True, True)
                last.then_inc(unit_used, 1)
                if c == 0:
                    pe.wait_ge(kpe.sin, 1)
                for q in range(2):
                    rotate(lq, 2 * c + q, l_q[0:QW, q, :], rot16, 4 + q, slice(0, QW))
                gate(PAIR_GATE[c], 7)

            def lat_logits(n, to):
                head, b = n // TB, n % TB
                q = slice(b * P, (b + 1) * P)
                return three(to[:], lq_h[0:QW, head % 2, q], lq_l[0:QW, head % 2, q],
                             lk_h[0:QW, head % 2, :], lk_l[0:QW, head % 2, :], True, True)

            pe.wait_ge(l_lat.lo, 3)
            for c in range(4):
                lat_heads(c)
                pe.wait_ge(lq.out.lo, 2 * c + 2)
                pe.wait_ge(lk.lo, 2 * c + 2)
                if c == 0:
                    pe.wait_ge(kpe.out.lo, 2)
                pe.wait_ge(lv.lo, 2 * c + 2)
                attention(a_lat, (2 * TB * c, 2 * TB * (c + 1)), lat_logits, lambda n: TB,
                          lambda g: paired_values(a_lat, g, lambda n: TB,
                                                  lambda head, s: (lv_h[:, s, :], lv_l[:, s, :]), l_pt_h, l_pt_l,
                                                  first_pair=c),
                          lead=lambda n: gate(PAIR_GATE_2[c], 7) if n == 2 * TB * c + 3 and c in PAIR_GATE_2 else None)

            pe.wait_ge(att.out.lo, a_lat.piece0 + HEADS)
            for p in range(4):
                u, b0 = FIRST["merge"] + 2 * p, 4 * (p % 2)
                if p >= 2:
                    pe.wait_ge(me_term, 4 * (p - 1))
                for branch, (o_h, o_l) in enumerate(((lo_h, lo_l), (go_h, go_l))):
                    for q in range(2):
                        columns(u + branch, bank[b0 + 2 * branch + q][:], o_h, o_l, range(4), width=2 * P, at_col=q * P,
                                use=q == 1)
            u = FIRST["out"]
            for m in range(KC):
                if m >= 3:
                    pe.wait_ge(h_out, m - 2)
                elif m == 0:
                    pe.wait_ge(me_term, 3 * KC // 2)
                columns(u + m, bank[1 + m % 3][:], mg_h, mg_l, range(KC),
                        before=(lambda k: pe.wait_ge(merged2.lo, k + 1)) if m == 0 else None)

            pe.wait_ge(p_in, 16)
            pe.wait_ge(me_sum, KC)
            for k in range(2):
                for b in range(TB):
                    last = pe.transpose(bank[4 + k][:, b * P:(b + 1) * P], p_rows[:, b, k * P:(k + 1) * P], ident)
                last.then_inc(p_turned, 1)

            def mlp_up(first, j0, i, opening=False):
                for q in range(RING):
                    if not opening:
                        pe.wait_ge(ml_x, 4 * i + (j0 + q - 3))
                    columns(first + q, bank[q][:], xh, xl, range(KC), i,
                            before=entering(x_mlp) if opening and q == 0 else None)
                    if opening and q == 0:
                        sum_squares(n_mlp)
                    if opening and q == 1:
                        spread(n_mlp)

            def mlp_down(first, kept, k0, i, opening=False):
                for q in range(RING):
                    m = q // 2
                    if q % 2 == 0 and not opening:
                        pe.wait_ge(kept, 2 * i + (m - 1))
                    columns(first + q, bank[4 + m][:], hid_h, hid_l, range(q % 2 * KC, q % 2 * KC + KC), i,
                            start=q % 2 == 0, stop=q % 2 == 1,
                            before=(lambda k: pe.wait_ge(ml_hid.lo, k0 + k + 1)) if opening and m == 0 else None)

            mlp_up(FIRST["mlp_up_a"], 0, None, opening=True)
            with pe.Fori(1, FF2_HALF // RING) as i:
                mlp_up(FIRST["mlp_up_a"], 0, i)
            pe.wait_ge(p_split.lo, 2)
            mlp_down(FIRST["mlp_down_a"], ml_part, 0, None, opening=True)
            with pe.Fori(1, KC // 2) as i:
                mlp_down(FIRST["mlp_down_a"], ml_part, 0, i)
            with pe.Fori(0, FF2_HALF // RING) as i:
                mlp_up(FIRST["mlp_up_b"], FF2_HALF, i)
            pe.wait_ge(ml_part, KC)
            mlp_down(FIRST["mlp_down_b"], h_mlp, FF2_HALF, None, opening=True)
            with pe.Fori(1, KC // 2) as i:
                mlp_down(FIRST["mlp_down_b"], h_mlp, FF2_HALF, i)

            for n in range(2):
                w_h, w_l = unit(FIRST["ple"] + n)
                for m in range(4):
                    if n == 1 and m == 0:
                        pe.wait_ge(h_mlp, KC)
                    if n == 1 and m == 2:
                        pe.wait_ge(ple_kept, 2)
                    if n == 0 and m == 0:
                        pe.wait_ge(ml_x, FF2)
                    to = bank[m if n == 0 else (4, 5, 0, 1)[m]]
                    for k in range(2):
                        w = slice(k * T + m * P, k * T + (m + 1) * P)
                        last = three(to[:], w_h[:, w], w_l[:, w], pt_h[:, k, :], pt_l[:, k, :], k == 0, k == 1)
                last.then_inc(unit_used, 1)
                if n == 0:
                    sum_squares(n_ple)
                else:
                    spread(n_ple)
            for m in range(KC):
                if m == 0:
                    pe.wait_ge(ple_kept, 4)
                elif m >= 2:
                    pe.wait_ge(pg_x, m - 1)
                columns(FIRST["ple_gate"] + m, bank[2 + m % 2][:], xh, xl, range(KC),
                        before=entering(x_ple) if m == 0 else None)
            sum_squares(n_end)
            spread(n_end)

            end_bank = (0, 1, 4, 5)
            pe.wait_ge(ple_kept, KC)
            for k in range(KC):
                pe.wait_ge(end_normed, k + 1)
                if k >= 4:
                    pe.wait_ge(end_kept, k - 3)
                for b in range(TB):
                    last = pe.transpose(bank[end_bank[k % 4]][:, b * P:(b + 1) * P], normed[:, k, b * P:(b + 1) * P], ident)
                last.then_inc(end_turned, 1)

        @block.scalar
        def _(act):
            def hi(u, i=None):
                if u >= UNITS:
                    return
                s = u % RING
                act.wait_ge(raw_in[s], landed(u) if i is None else 16 * i + landed(u))
                if i is not None:
                    act.wait_ge(unit_used, 4 * i + done(u - RING))
                elif u >= RING:
                    act.wait_ge(unit_used, done(u - RING))
                act.activation(wh[:, s, :], raw[:, s, :], ACT.Copy).then_inc(hi_ready, 1)

            def ahead(u, i=None):
                hi(u + LOOKAHEAD, i)

            def square(N, k, src, free=False):
                r, user = N.chunk0 + k, N.slot_user(k)
                if user is not None and not free:
                    act.wait_ge(norm.summed if user[0] == "summed" else norm.added, user[1])
                act.activation(squares[:, r % 2, :], src, ACT.Square).then_inc(norm.squares, 1)

            def scaled(X, name, k):
                act.activation(xh[:, k, :], h[:, k, :], ACT.Copy, scale=gain(name, k)).then_inc(X.hi, 1)

            def keep_scale(N):
                act.wait_ge(norm.spread, N.expand0 + 1)
                act.activation(scale[:], bank[SPREAD][:], ACT.Copy).then_inc(norm.scale, 1)

            def enter(X, N, name, updated, first):
                for k in range(KC):
                    act.wait_ge(updated, first + k + 1)
                    scaled(X, name, k)
                    square(N, k, h[:, k, :])

            def feed_forward(name, S, X, N, NP, updated, first):
                u = FIRST[name + "_up_a"]

                def pair(u, j, i, n, opening=False):
                    c = n % 2
                    ahead(u, i)
                    if opening:
                        enter(X, N, name + "_pre_g", updated, first)
                    ahead(u + 1, i)
                    if opening:
                        keep_scale(N)
                    act.wait_ge(ffn.gate, S.hid0 + j + 1 if i is None else 2 * i + (S.hid0 + j + 1))
                    act.activation(wa[:, c, :], wa[:, c, :], ACT.Silu).then_inc(ffn.silu, 1)
                    act.wait_ge(ffn.prod, S.hid0 + j + 1 if i is None else 2 * i + (S.hid0 + j + 1))
                    dst = hid_h[:, n, :] if i is None else hid_h[:, 2 * i + n, :]
                    act.activation(dst, wb[:, c, :], ACT.Copy).then_inc(ffn.hid.hi, 1)

                pair(u, 0, None, 0, opening=True)
                pair(u + 2, 1, None, 1)
                with act.Fori(1, FF_A // 2) as i:
                    for c in range(2):
                        pair(u + 2 * c, c, i, c)
                u = FIRST[name + "_down_a"]
                with act.Fori(0, KC // 2) as i:
                    for q in range(RING):
                        ahead(u + q, i)
                u = FIRST[name + "_up_b"]
                with act.Fori(0, FF_B // 2) as i:
                    for c in range(2):
                        pair(u + 2 * c, FF_A + c, i, c)
                u = FIRST[name + "_down_b"]
                for m in range(KC):
                    ahead(u + m)
                    act.wait_ge(ffn.full, S.out0 + m + 1)
                    square(NP, m, f[:, m, :])

            def attention(A, blocks, source, exp_scale, blocks_of_keys, p_h, outputs, lead=None):
                lo, hi_ = blocks
                for n in range(lo, hi_ + 6):
                    r = A.block0 + n
                    if lead is not None:
                        lead(n)
                    if n < hi_:
                        act.wait_ge(att.top, r + 1)
                        if r >= 3:
                            act.wait_ge(att.turned, r - 2)
                        src = source(n)
                        act.activation(probs[:, r % 3, 0:src.shape[1]], src, ACT.Exp, bias=top[:, r % 4:r % 4 + 1],
                                       scale=exp_scale, accum_out=sums[:, r % 4:r % 4 + 1]).then_inc(att.exp, 1)
                    m, r = n - 1, A.block0 + n - 1
                    if lo <= m < hi_:
                        act.wait_ge(att.inv, r + 1)
                        p = probs[:, r % 3, 0:blocks_of_keys(m) * P]
                        act.activation(p, p, ACT.Copy, scale=invs[:, r % 4:r % 4 + 1]).then_inc(att.probs, 1)
                    m, r = n - 3, A.block0 + n - 3
                    if lo <= m < hi_:
                        g = A.half0 + m // 2
                        act.wait_ge(att.turned, r + 1)
                        if g >= 2:
                            act.wait_ge(att.pv, g - 1)
                        w = blocks_of_keys(m)
                        act.activation(p_h[:, g % 2, 0:w, m % 2 * P:(m % 2 + 1) * P],
                                       bank[3 + m % 2][:, 0:w * P].rearrange("p (s q) -> p s q", q=P),
                                       ACT.Copy).then_inc(att.pt.hi, 1)
                    if (n - 7) % 2 == 0 and lo <= n - 7 < hi_:
                        output(A, (n - 7) // 2, outputs)

            def output(A, g, outputs):
                for dst, src in outputs(g):
                    act.wait_ge(att.pv, A.half0 + g + 1)
                    act.activation(dst, src, ACT.Copy).then_inc(att.out.hi, 1)

            def paired(o_h):
                def outputs(g):
                    head, half = g // 2, g % 2
                    if head % 2 == 0:
                        return []
                    return [(o_h[:, head // 2, half * 256:(half + 1) * 256], bank[5 + half][:, 0:256])]
                return outputs

            act.dma_start(mats[:], dram["shape_mats"].rearrange("p (n c) -> p n c", c=P)).then_inc(const_in, 16)
            for b in range(TB // 2):
                act.dma_start(x_rows[:, b, :], dram["x"][0, b * P:(b + 1) * P, :]).then_inc(x_in[0], 16)
            act.dma_start(gains[:], dram["gain_columns"]).then_inc(gains_in, 16)
            tabs = dram["shape_tabs"].rearrange("p (n c t) -> p n c t", n=3, c=2)
            act.dma_start(tab[:], tabs[:, 0]).then_inc(tab_in, 16)
            for u in range(LOOKAHEAD):
                hi(u)
            act.wait_ge(gains_in, 16)
            feed_forward("ffn1", ffn1, x_ffn1, n_ffn1, n_ffn1p, x_kept, 0)

            def rope_hi(r):
                dst = (qi_h[:, r, :] if r < 4 else ki_h[:] if r == 4 else qa_h[:, r - 5, :] if r < 9 else ka_h[:])
                act.wait_ge(rope.sum, r + 1)
                act.activation(dst, wb[:, r % 2, :], ACT.Copy, scale=HD ** -0.5 if 5 <= r < 9 else 1.0).then_inc(rope.out.hi, 1)

            u = FIRST["index"]
            ahead(u)
            enter(x_mix, n_mix, "mix_pre_g", r_ffn1.h, r_ffn1.first)
            ahead(u + 1)
            keep_scale(n_mix)
            for n in (2, 3, 4, 5):
                ahead(u + n)
            rope_hi(0)
            rope_hi(1)
            ahead(u + 6)
            rope_hi(2)
            ahead(u + 7)
            act.wait_ge(v_turned, 1)
            turned = bank[6][:, 0:TB * (HD + HEADS)].rearrange("p (b c) -> p b c", c=HD + HEADS)
            for par in range(2):
                act.activation(va_h[:, :, par * P:par * P + HD], turned[:, :, 0:HD], ACT.Copy).then_inc(v_split.hi, 1)
            for r in range(3, 10):
                rope_hi(r)
                ahead(u + r + 5)
            for n in range(3 * HEADS):
                w = (n // HEADS + 2) * P
                act.wait_ge(idx_raw, n + 1)
                if n >= 3:
                    act.wait_ge(idx_sum, IDX_SUM[n - 3])
                act.activation(probs[:, n % 3, 0:w], bank[(0, 2, 3, 7)[n % 4]][:, 0:w], ACT.Relu).then_inc(idx_relu, 1)

            u = FIRST["conv"]
            for j in range(4):
                c = j % 2
                if j >= 1:
                    ahead(u + 3 * j + 3)
                act.wait_ge(conv_step, 7 * j + 4)
                act.activation(c_z[:, c, :], c_y[:, c, 2:2 + T], ACT.Copy,
                               scale=gain_row(CONV_ROW + 8 + j)).then_inc(conv_tap, 1)
                act.wait_ge(conv_step, 7 * j + 7)
                act.activation(cz_h[:, j, :], c_z[:, c, :], ACT.Copy).then_inc(conv_out.hi, 1)
                if j < 3:
                    ahead(u + 3 * j + 4)
                    ahead(u + 3 * j + 5)
            u = FIRST["merge_conv"]
            for p in range(4):
                for q in range(3):
                    if p or q:
                        ahead(u + 3 * p + q)
                    if q >= 1:
                        m = 2 * p + q - 1
                        act.wait_ge(mc_gate, m + 1)
                        act.activation(wa[:, m % 2, :], wa[:, m % 2, :], ACT.Sigmoid).then_inc(mc_sig, 1)

            act.wait_ge(rope.sin, 10)
            act.dma_start(tab[:], tabs[:, 2]).then_inc(tab_in, 16)

            def main_gate(n):
                if n < HB and n % TB == TB - 1:
                    ahead(FIRST["gate_a"] + n // TB)
                if n == HB + 2:
                    act.wait_ge(unit_used, done(FIRST["gate_a"] + KC - 1))
                    act.dma_start(mem_rows[:], dram["mem"][0].rearrange("(b p) c -> p b c", p=P)).then_inc(mem_in, 16)

            attention(a_main, (0, HB), lambda n: wb[:, n % 2, 0:(n % TB + 1) * P], -1.0, lambda n: n % TB + 1, a_pt_h,
                      paired(qa_h), main_gate)
            for m in range(KC):
                act.wait_ge(ga_scaled, m + 1)
                act.activation(gate_a[:, m, :], gate_a[:, m, :], ACT.Sigmoid).then_inc(ga_sig, 1)
            act.wait_ge(mem_in, 16)
            for b in range(MB):
                if b:
                    act.wait_ge(mem_sum, b)
                act.activation(mem_squares[:], mem_rows[:, b, :], ACT.Square,
                               accum_out=mem_sq[:, b:b + 1]).then_inc(mem_sum, 1)
            for p in range(4):
                ahead(FIRST["attn_out"] + p)
                for m in (2 * p, 2 * p + 1):
                    act.wait_ge(ma_sum, m + 1)
                    act.activation(mm_h[:, m, :], mixed[:, m, :], ACT.Copy).then_inc(merged.hi, 1)
            for k in range(KC):
                act.wait_ge(mem_turned, k // 2 + 1)
                act.activation(memt_h[:, k, :], bank[4 + k // 2][:, k % 2 * N_MEM:(k % 2 + 1) * N_MEM], ACT.Copy,
                               scale=gain("mem_g", k)).then_inc(memt.hi, 1)
            for m in range(KC):
                ahead(FIRST["mix_out"] + m)
                act.wait_ge(mo_full, m + 1)
                square(n_mixp, m, f[:, m, :])

            def enter_mem(k):
                act.wait_ge(r_mix.h, r_mix.first + k + 1)
                scaled(x_x, "xattn_pre_g", k)

            for m in range(KC):
                ahead(FIRST["mem_k"] + m)
                act.wait_ge(unit_used, done(FIRST["mem_k"] + m))
                act.activation(mk_h[:, m, :], bank[m % 4][:, 0:N_MEM], ACT.Copy).then_inc(mk.hi, 1)
                if m >= 3:
                    enter_mem(m - 3)
            for n in range(8):
                ahead(FIRST["mem_v"] + n)
                if n < 3:
                    enter_mem(n + 5)
                if n % 4 == 3:
                    c = n // 4
                    act.wait_ge(unit_used, done(FIRST["mem_v"] + n))
                    for b in range(MB):
                        act.activation(mv_h[:, b, c * T:(c + 1) * T], bank[(4, 0)[c] + b][:], ACT.Copy).then_inc(mv.hi, 1)
                square(n_xq, n, h[:, n, :])
            for m in range(KC + 1):
                if m < KC:
                    ahead(FIRST["x_q"] + m)
                if m == 1:
                    keep_scale(n_xq)
                if m >= 1:
                    act.wait_ge(xq_scaled, m)
                    act.activation(xq_h[:, m - 1, :], wa[:, (m - 1) % 2, :], ACT.Copy).then_inc(xq.hi, 1)
            attention(a_mem, (0, XH * TB), lambda n: bank[n % 3][:, 0:N_MEM], 1.0, lambda n: MB, x_pt_h,
                      lambda g: [(xh[:, g // 2 * 2 + c, g % 2 * 256:(g % 2 + 1) * 256], bank[5 + c][:, 0:256]) for c in range(2)])
            for m in range(KC):
                ahead(FIRST["x_out"] + m)
                act.wait_ge(xo_full, m + 1)
                square(n_xp, m, f[:, m, :])

            feed_forward("ffn2", ffn2, x_ffn2, n_ffn2, n_ffn2p, r_x.h, r_x.first)

            for r in range(6):
                ahead(FIRST["grouped"] + r)
                if r == 0:
                    enter(x_mix2, n_mix2, "g_mix_2", r_ffn2.h, r_ffn2.first)
                elif r == 1:
                    keep_scale(n_mix2)
                else:
                    act.wait_ge(gx.x, r - 1)
                    square(n_heads, r - 2, g_x[:, r - 2, :])
            ahead(FIRST["grouped"] + 6)
            for r in (4, 5):
                act.wait_ge(gx.x, r + 1)
                square(n_heads, r, g_x[:, r, :])
            act.wait_ge(gv_turned, 1)
            turned_g = bank[6][:].rearrange("p (b c) -> p b c", c=P)
            for kv in range(2):
                for par in range(2):
                    act.activation(gv_h[:, kv, :, par * P:par * P + HD], turned_g[:, :, kv * HD:(kv + 1) * HD],
                                   ACT.Copy).then_inc(gv.hi, 1)
            def gate(g):
                act.wait_ge(gate_scaled, g + 1)
                act.dma_start(gate_store[g], gate_stage[:]).then_inc(gate_out, 16)

            for n, r in enumerate(GROUPED_ORDER):
                ahead(gate_unit(n))
                gate(n)
                act.wait_ge(gx.sum, n + 1)
                act.activation(gq_h[:, r, :] if r < 4 else gk_h[:, r - 4, :], wb[:, n % 2, :], ACT.Copy,
                               scale=HD ** -0.5 if r < 4 else 1.0).then_inc(gx.out.hi, 1)
            act.wait_ge(gx.sin, 6)
            act.dma_start(tab[:], tabs[:, 1]).then_inc(tab_in, 16)
            act.wait_ge(gv.lo, 4)

            def grouped_gates(n):
                if n in GROUPED_GATES:
                    ahead(gate_unit(GROUPED_GATES[n]))
                if n - 2 in GROUPED_GATES:
                    gate(GROUPED_GATES[n - 2])

            attention(a_grp, (0, HB), lambda n: bank[n % 3][:], 1.0, lambda n: TB, g_pt_h, paired(go_h), grouped_gates)

            act.wait_ge(gate_out, 16 * 8)
            for r in range(4):
                ahead(FIRST["latent"] + r)
                if r >= 1:
                    act.wait_ge(lx, r)
                    N, k = ((n_cq, 0), (n_cq, 1), (n_ckv, 0))[r - 1]
                    square(N, k, l_x[:, r - 1, :])
            for k in range(3):
                act.wait_ge(l_normed, k + 1)
                act.activation((cq_h[:, 0, :], cq_h[:, 1, :], ck_h[:])[k], (wb[:, 0, :], wb[:, 1, :], wa[:, 0, :])[k],
                               ACT.Copy).then_inc(l_lat.hi, 1)
            act.wait_ge(kpe.sum, 1)
            for q in range(2):
                act.activation(lk_h[NOPE:QW, q, :], wa[NOPE:QW, 1, :], ACT.Copy).then_inc(kpe.out.hi, 1)
            act.wait_ge(kpe.out.lo, 2)
            for g in (8, 9):
                ahead(gate_unit(g))
                gate(g)

            def pair_gates(c, n):
                if n == 2:
                    gate(PAIR_GATE[c])
                if c in PAIR_GATE_2 and n == 3:
                    ahead(gate_unit(PAIR_GATE_2[c]))
                if c in PAIR_GATE_2 and n == 6:
                    gate(PAIR_GATE_2[c])

            for c in range(4):
                u = FIRST["latent_heads"] + HEAD_UNITS[c]
                ahead(u)
                act.wait_ge(unit_used, done(u))
                for q in range(2):
                    act.activation(l_q[0:QW, q, :], bank[q][0:QW, :], ACT.Copy).then_inc(lq.x, 1)
                for q in range(2):
                    act.activation(lk_h[0:NOPE, q, :], bank[2 + q][0:NOPE, :], ACT.Copy).then_inc(lk.hi, 1)
                for q in range(2):
                    act.activation(lv_h[:, :, q * P:q * P + HD],
                                   bank[6][:].rearrange("p (s c) -> p s c", c=P)[:, :, q * HD:(q + 1) * HD],
                                   ACT.Copy).then_inc(lv.hi, 1)
                for q in range(2):
                    act.wait_ge(lq.sum, 2 * c + q + 1)
                    act.activation(lq_h[0:QW, q, :], wb[0:QW, q, :], ACT.Copy, scale=QW ** -0.5).then_inc(lq.out.hi, 1)
                ahead(u + 1)
                attention(a_lat, (2 * TB * c, 2 * TB * (c + 1)), lambda n: bank[n % 3][:], 1.0, lambda n: TB, l_pt_h,
                          paired(lo_h), lambda n: pair_gates(c, n - 2 * TB * c))

            def gates_from_dram(m):
                act.dma_start(gates_back[:, m % 4], gate_store[2 * m:2 * m + 2].rearrange("g p t -> p g t")
                              ).then_inc(gate_in[m % 4], 16)

            act.wait_ge(gate_out, 16 * 2 * KC)
            act.wait_ge(att.pv, a_lat.half0 + HB // 2)
            for m in range(4):
                gates_from_dram(m)
            for m in range(KC + 1):
                if m < KC:
                    ahead(FIRST["merge"] + m)
                    act.wait_ge(gate_in[m % 4], 16 * (m // 4 + 1))
                    act.activation(gates_back[:, m % 4], gates_back[:, m % 4], ACT.Sigmoid).then_inc(gate_sig, 1)
                if m >= 1:
                    act.wait_ge(me_sum, m)
                    act.activation(mg_h[:, m - 1, :], wa[:, (m - 1) % 2, :], ACT.Copy).then_inc(merged2.hi, 1)
                    if m <= 4:
                        gates_from_dram(m + 3)
            act.wait_ge(unit_used, done(FIRST["merge"] + 7))
            act.dma_start(p_rows[:], dram["p_2"][0, 0].rearrange("(b p) c -> p b c", p=P)).then_inc(p_in, 16)
            for m in range(KC):
                ahead(FIRST["out"] + m)
                act.wait_ge(h_out, m + 1)
                scaled(x_mlp, "g_mlp_2", m)
                square(n_mlp, m, h[:, m, :])
            for k in range(2):
                act.wait_ge(p_turned, k + 1)
                act.activation(pt_h[:, k, :], bank[4 + k][:], ACT.Copy).then_inc(p_split.hi, 1)

            def mlp_chunk(j, i, n):
                act.wait_ge(ml_sq, j + 1 if i is None else 4 * i + (j + 1))
                act.activation(hid_h[:, n, :] if i is None else hid_h[:, 4 * i + n, :], wb[:, n % 2, :],
                               ACT.Copy).then_inc(ml_hid.hi, 1)

            def mlp_up(u, j0, i):
                for q in range(RING):
                    ahead(u + q, i)
                    mlp_chunk(j0 + q, i, q)

            u = FIRST["mlp_up_a"]
            ahead(u)
            ahead(u + 1)
            keep_scale(n_mlp)
            mlp_chunk(0, None, 0)
            mlp_chunk(1, None, 1)
            for q in (2, 3):
                ahead(u + q)
                mlp_chunk(q, None, q)
            with act.Fori(1, FF2_HALF // RING) as i:
                mlp_up(u, 0, i)
            with act.Fori(0, KC // 2) as i:
                for q in range(RING):
                    ahead(FIRST["mlp_down_a"] + q, i)
            with act.Fori(0, FF2_HALF // RING) as i:
                mlp_up(FIRST["mlp_up_b"], FF2_HALF, i)

            def leave_mlp(i):
                for q in range(RING):
                    ahead(FIRST["mlp_down_b"] + q, i)
                    if q % 2 == 1:
                        m = q // 2
                        if i is not None:
                            act.wait_ge(norm.added, 2 * i + (n_ple.add0 + m - 1))
                        act.wait_ge(h_mlp, m + 1 if i is None else 2 * i + (m + 1))
                        row = GAINS.index("g_ple_2") * KC + m
                        if i is None:
                            g, x, to = gains[:, row:row + 1], h[:, m, :], xh[:, m, :]
                        else:
                            g, x, to = gains[:, bass.ds(2 * i + row, 1)], h[:, 2 * i + m, :], xh[:, 2 * i + m, :]
                        act.activation(to, x, ACT.Copy, scale=g).then_inc(x_ple.hi, 1)
                        square(n_ple, m, x, free=i is not None)

            leave_mlp(None)
            with act.Fori(1, KC // 2) as i:
                leave_mlp(i)

            for n in range(2):
                ahead(FIRST["ple"] + n)
                if n == 1:
                    keep_scale(n_ple)
                act.wait_ge(unit_used, done(FIRST["ple"] + n))
                for m in range(4):
                    act.activation(ple[:, 4 * n + m, :], bank[m if n == 0 else (4, 5, 0, 1)[m]][:], ACT.Copy).then_inc(ple_kept, 1)
            for m in range(KC + 1):
                if m < KC:
                    ahead(FIRST["ple_gate"] + m)
                    act.wait_ge(pg_x, m + 1)
                    act.activation(wa[:, m % 2, :], wa[:, m % 2, :], ACT.Sigmoid).then_inc(pg_sig, 1)
                if m >= 1:
                    act.wait_ge(h_end, m)
                    square(n_end, m - 1, h[:, m - 1, :])
            for k in range(KC):
                act.wait_ge(end_turned, k + 1)
                act.activation(out_rows[:, :, k * P:(k + 1) * P],
                               bank[(0, 1, 4, 5)[k % 4]][:].rearrange("p (b c) -> p b c", c=P), ACT.Copy).then_inc(end_kept, 1)

        @block.vector
        def _(dve):
            def rsqrt(x, y, t, mean_sq, d, steps, before):
                dve.tensor_scalar(x, mean_sq, 1.0 / d, EPS, ALU.mult, ALU.add).then_inc(steps, 1)
                dve.wait_ge(steps, before + 1)
                dve.tensor_scalar(y.bitcast(I32), x.bitcast(I32), -0.5, RSQRT_SEED, ALU.mult, ALU.add).then_inc(steps, 1)
                for n in range(NEWTON_STEPS):
                    dve.wait_ge(steps, before + 3 * n + 2)
                    dve.scalar_tensor_tensor(t, x, -0.5, y, ALU.mult, ALU.mult).then_inc(steps, 1)
                    dve.wait_ge(steps, before + 3 * n + 3)
                    dve.tensor_tensor(t, t, y, ALU.mult).then_inc(steps, 1)
                    dve.wait_ge(steps, before + 3 * n + 4)
                    dve.scalar_tensor_tensor(y, t, 1.5, y, ALU.add, ALU.mult).then_inc(steps, 1)
                dve.wait_ge(steps, before + 2 + 3 * NEWTON_STEPS)

            def zero(middle):
                return dve.tensor_scalar(middle, ones[:, 0:HD].unsqueeze(1).to_broadcast([P, TB, HD]), 0.0, None, ALU.mult)

            def newton(N, d, columns=slice(0, TB)):
                n = columns.stop - columns.start
                dve.wait_ge(norm.summed, N.sum0 + N.sums)
                rsqrt(n_x[:, 0:n], n_y[:, 0:n], n_t[:, 0:n], bank[SUMS][:, columns], d, norm.newton, N.newton0)

            def lay_out(N):
                dve.tensor_tensor(expand[:], ident.unsqueeze(1).to_broadcast([P, TB, P]),
                                  n_y[:, 0:TB].unsqueeze(2).to_broadcast([P, TB, P]), ALU.mult).then_inc(norm.expand, 1)

            def remainder(X, k, name):
                dve.wait_ge(X.hi, X.first + k + 1)
                dve.scalar_tensor_tensor(xl[:, k, :], h[:, k, :], gain(name, k), xh[:, k, :].bitcast(F32),
                                         ALU.mult, ALU.subtract).then_inc(X.lo, 1)

            def add_squares(N, k, i=None):
                r = N.chunk0 + k
                dve.wait_ge(norm.squares, r + 1 if i is None else 2 * i + (r + 1))
                if k == 0 and i is None:
                    if N.expand0:
                        dve.wait_ge(norm.spread, N.expand0)
                    dve.tensor_copy(square_sum, squares[:, r % 2, :]).then_inc(norm.added, 1)
                else:
                    dve.wait_ge(norm.added, N.add0 + k if i is None else 2 * i + (N.add0 + k))
                    dve.tensor_tensor(square_sum, square_sum, squares[:, r % 2, :], ALU.add).then_inc(norm.added, 1)

            def residual_chunk(R, NP, post, factor, k):
                if k == 0:
                    dve.wait_ge(norm.spread, NP.expand0 + 1)
                dve.scalar_tensor_tensor(wa[:, k % 2, :], f[:, k, :], gain(post, k), bank[SPREAD][:],
                                         ALU.mult, ALU.mult).then_inc(R.term, 1)
                dve.wait_ge(R.term, R.first + k + 1)
                dve.scalar_tensor_tensor(h[:, k, :], wa[:, k % 2, :], factor, h[:, k, :], ALU.mult, ALU.add).then_inc(R.h, 1)

            def residual(R, NP, post, factor, X, pre, N):
                newton(NP, D)
                lay_out(NP)
                for k in range(KC):
                    residual_chunk(R, NP, post, factor, k)
                    if k >= 1:
                        remainder(X, k - 1, pre)
                        add_squares(N, k - 1)
                remainder(X, KC - 1, pre)
                add_squares(N, KC - 1)

            def feed_forward(name, S, N, NP):
                newton(N, D)
                lay_out(N)
                dve.wait_ge(norm.scale, N.scale0 + 1)
                u = FIRST[name + "_up_a"]

                def pair(u, j, i, n):
                    c = n % 2

                    def at(v):
                        return 2 * i + (S.hid0 + v)
                    dve.wait_ge(unit_used, done(u, i))
                    dve.tensor_tensor(wa[:, c, :], bank[2 * c][:], scale[:], ALU.mult).then_inc(ffn.gate, 1)
                    dve.wait_ge(unit_used, done(u + 1, i))
                    dve.tensor_tensor(wb[:, c, :], bank[2 * c + 1][:], scale[:], ALU.mult).then_inc(ffn.up, 1)
                    dve.wait_ge(ffn.silu, at(j + 1))
                    dve.wait_ge(ffn.up, at(j + 1))
                    dve.tensor_tensor(wb[:, c, :], wb[:, c, :], wa[:, c, :], ALU.mult).then_inc(ffn.prod, 1)
                    dve.wait_ge(ffn.hid.hi, at(j + 1))
                    h_, l_ = (hid_h[:, n, :], hid_l[:, n, :]) if i is None else (hid_h[:, 2 * i + n, :], hid_l[:, 2 * i + n, :])
                    dve.tensor_tensor(l_, wb[:, c, :], h_.bitcast(F32), ALU.subtract).then_inc(ffn.hid.lo, 1)

                with dve.Fori(0, FF_A // 2) as i:
                    for c in range(2):
                        pair(u + 2 * c, c, i, c)
                u = FIRST[name + "_down_a"]
                with dve.Fori(0, KC // 2) as i:
                    for m in range(2):
                        dve.wait_ge(unit_used, done(u + 2 * m + 1, i))
                        dve.tensor_copy(f[:, 2 * i + m, :], bank[4 + m][:]).then_inc(ffn.part, 1)
                u = FIRST[name + "_up_b"]
                with dve.Fori(0, FF_B // 2) as i:
                    for c in range(2):
                        pair(u + 2 * c, FF_A + c, i, c)
                u = FIRST[name + "_down_b"]
                dve.wait_ge(ffn.part, S.out0 + KC)
                for m in range(KC):
                    dve.wait_ge(unit_used, done(u + m))
                    dve.tensor_tensor(f[:, m, :], bank[4 + m % 2][:], f[:, m, :], ALU.add).then_inc(ffn.full, 1)
                    if m >= 1:
                        add_squares(NP, m - 1)
                add_squares(NP, KC - 1)

            def attention(A, blocks, find_top, blocks_of_keys, p_h, p_l, outputs, lead=None):
                lo, hi_ = blocks
                for n in range(lo, hi_ + 6):
                    if lead is not None:
                        lead(n)
                    if n < hi_:
                        r = A.block0 + n
                        dve.wait_ge(att.logits, r + 1)
                        find_top(n, r).then_inc(att.top, 1)
                    m, r = n - 1, A.block0 + n - 1
                    if lo <= m < hi_:
                        c = slice(r % 4, r % 4 + 1)
                        dve.wait_ge(att.exp, r + 1)
                        dve.reciprocal(invs[:, c], sums[:, c]).then_inc(att.inv, 1)
                    m, r = n - 4, A.block0 + n - 4
                    if lo <= m < hi_:
                        w, g = blocks_of_keys(m), A.half0 + m // 2
                        part = (slice(None), g % 2, slice(0, w), slice(m % 2 * P, (m % 2 + 1) * P))
                        dve.wait_ge(att.pt.hi, r + 1)
                        dve.tensor_tensor(p_l[part], bank[3 + m % 2][:, 0:w * P].rearrange("p (s q) -> p s q", q=P),
                                          p_h[part].bitcast(F32), ALU.subtract).then_inc(att.pt.lo, 1)
                    if (n - 7) % 2 == 0 and lo <= n - 7 < hi_:
                        for piece, to, src, top_ in outputs((n - 7) // 2):
                            dve.wait_ge(att.out.hi, A.piece0 + piece + 1)
                            dve.tensor_tensor(to, src, top_.bitcast(F32), ALU.subtract).then_inc(att.out.lo, 1)

            def plain_top(width):
                return lambda n, r: dve.tensor_reduce(top[:, r % 4:r % 4 + 1], bank[n % 3][:, 0:width], AX.X, ALU.max, negate=True)

            def paired(o_h, o_l):
                def outputs(g):
                    head, half = g // 2, g % 2
                    if head % 2 == 0:
                        return []
                    part = (slice(None), head // 2, slice(half * 256, (half + 1) * 256))
                    return [(head // 2 * 2 + half, o_l[part], bank[5 + half][:, 0:256], o_h[part])]
                return outputs

            dve.wait_ge(gains_in, 16)
            for k in range(KC + 1):
                if k < KC:
                    dve.wait_ge(x_turned, k + 1)
                    dve.tensor_copy(h[:, k, :], bank[k][:]).then_inc(x_kept, 1)
                if k >= 1:
                    remainder(x_ffn1, k - 1, "ffn1_pre_g")
                    add_squares(n_ffn1, k - 1)
            feed_forward("ffn1", ffn1, n_ffn1, n_ffn1p)
            residual(r_ffn1, n_ffn1p, "ffn1_post_g", 0.5, x_mix, "mix_pre_g", n_mix)

            def rope_x(r):
                if r >= 2:
                    dve.wait_ge(rope.rot, r - 1)
                u = FIRST["index"] + r if r < 5 else FIRST["queries"] + r - 5
                dve.wait_ge(unit_used, done(u))
                dve.tensor_tensor(wa[:, r % 2, :], bank[7 if r == 4 else r % 4][:], scale[:], ALU.mult).then_inc(rope.x, 1)
                dve.wait_ge(rope.x, r + 1)
                dve.tensor_tensor(wb[:, r % 2, :], wa[:, r % 2, :], tab[:, 0, :], ALU.mult).then_inc(rope.cos, 1)

            def rope_sum(r):
                dve.wait_ge(rope.rot, r + 1)
                dve.wait_ge(rope.cos, r + 1)
                dve.tensor_tensor(wa[:, r % 2, :], bank[4 + r % 2][:], tab[:, 1, :], ALU.mult).then_inc(rope.sin, 1)
                dve.wait_ge(rope.sin, r + 1)
                dve.tensor_tensor(wb[:, r % 2, :], wb[:, r % 2, :], wa[:, r % 2, :], ALU.add).then_inc(rope.sum, 1)

            def rope_lo(r):
                if r < 4:
                    a, b, s = qi_l[:, r, :], qi_h[:, r, :], 1.0
                elif r == 4:
                    a, b, s = ki_l[:], ki_h[:], 1.0
                elif r < 9:
                    a, b, s = qa_l[:, r - 5, :], qa_h[:, r - 5, :], HD ** -0.5
                else:
                    a, b, s = ka_l[:], ka_h[:], 1.0
                dve.wait_ge(rope.out.hi, r + 1)
                dve.scalar_tensor_tensor(a, wb[:, r % 2, :], s, b.bitcast(F32), ALU.mult, ALU.subtract).then_inc(rope.out.lo, 1)

            newton(n_mix, D)
            lay_out(n_mix)
            dve.wait_ge(norm.scale, n_mix.scale0 + 1)
            dve.wait_ge(tab_in, 16)
            width = HD + HEADS
            turned = bank[6][:, 0:TB * width].rearrange("p (b c) -> p b c", c=width)
            for r in range(10):
                if r >= 2:
                    rope_lo(r - 2)
                rope_x(r)
                if r == 3:
                    dve.wait_ge(unit_used, done(FIRST["values"]))
                    dve.tensor_tensor(v_cols[0:width, :], bank[6][0:width, :], scale[0:width, :], ALU.mult).then_inc(v_scaled, 1)
                if r >= 1:
                    rope_sum(r - 1)
                if r == 4:
                    zero(va_h[:, :, HD:P])
                    zero(va_l[:, :, HD:P]).then_inc(v_zero, 1)
                    dve.wait_ge(v_split.hi, 2)
                    dve.tensor_scalar(w_idx[:], turned[:, :, HD:width], HEADS ** -0.5 * HD ** -0.5, None,
                                      ALU.mult).then_inc(v_scaled, 1)
                    for par in range(2):
                        part = (slice(None), slice(None), slice(par * P, par * P + HD))
                        dve.tensor_tensor(va_l[part], turned[:, :, 0:HD], va_h[part].bitcast(F32),
                                          ALU.subtract).then_inc(v_split.lo, 1)
            rope_lo(8)
            rope_sum(9)
            rope_lo(9)

            dve.wait_ge(v_scaled, 2)
            for n in range(3 * HEADS):
                b, head = n // HEADS + 1, n % HEADS
                score, relu, w = mask_of(b), probs[:, n % 3, 0:(b + 1) * P], w_idx[:, b, head:head + 1]
                dve.wait_ge(idx_relu, n + 1)
                if head == 0:
                    dve.tensor_scalar(score, relu, w, None, ALU.mult).then_inc(idx_sum, 1)
                else:
                    dve.wait_ge(idx_sum, IDX_SUM[n] - 1)
                    dve.scalar_tensor_tensor(score, relu, w, score, ALU.mult, ALU.add).then_inc(idx_sum, 1)
                if head == HEADS - 1:
                    dve.wait_ge(idx_sum, IDX_SUM[n])
                    own = score[:, b * P:(b + 1) * P]
                    dve.scalar_tensor_tensor(own, after_query, NOT_CAUSAL, own, ALU.mult, ALU.add).then_inc(idx_sum, 1)
            dve.tensor_scalar(mask_of(0), after_query, MASKED, None, ALU.mult).then_inc(masked, 1)

            def search(n):
                score = mask_of(n // (TOP_K // 8) + 1)
                if n:
                    dve.wait_ge(taken, 2 * n)
                else:
                    dve.wait_ge(idx_sum, 3 * (HEADS + 1))
                dve.max(best8[:], score).then_inc(taken, 1)
                dve.wait_ge(taken, 2 * n + 1)
                dve.match_replace(score, best8[:], score, REPLACED).then_inc(taken, 1)
                if (n + 1) % (TOP_K // 8) == 0:
                    dve.wait_ge(taken, 2 * n + 2)
                    dve.tensor_scalar(score, score, REPLACED, MASKED, ALU.not_equal, ALU.mult).then_inc(masked, 1)

            dve.memset(c_y[:, :, 0:2], 0.0).then_inc(v_zero, 1)
            dve.wait_ge(v_zero, 2)
            u = FIRST["conv"]
            for j in range(4):
                c, banks, s0 = j % 2, CONV_BANKS[j % 2], 7 * j
                y, z = c_y[:, c, :], c_z[:, c, :]
                for q, to in enumerate((c_gb[:, c, :], c_gc[:, c, :], y[:, 2:2 + T])):
                    dve.wait_ge(unit_used, done(u + 3 * j + q))
                    dve.tensor_tensor(to, bank[banks[q]][:], scale[:], ALU.mult).then_inc(conv_step, 1)
                dve.wait_ge(conv_step, s0 + 3)
                dve.tensor_tensor(y[:, 2:2 + T], y[:, 2:2 + T], c_gc[:, c, :], ALU.mult).then_inc(conv_step, 1)
                dve.wait_ge(conv_step, s0 + 4)
                dve.wait_ge(conv_tap, j + 1)
                for n, tap in enumerate((1, 0)):
                    dve.scalar_tensor_tensor(z, y[:, tap:tap + T], gain_row(CONV_ROW + 4 * tap + j), z,
                                             ALU.mult, ALU.add).then_inc(conv_step, 1)
                    dve.wait_ge(conv_step, s0 + 5 + n)
                dve.tensor_tensor(z, z, c_gb[:, c, :], ALU.mult).then_inc(conv_step, 1)
                dve.wait_ge(conv_out.hi, j + 1)
                dve.tensor_tensor(cz_l[:, j, :], z, cz_h[:, j, :].bitcast(F32), ALU.subtract).then_inc(conv_out.lo, 1)
                for n in range(j * ROUNDS // 4, (j + 1) * ROUNDS // 4):
                    search(n)
            u = FIRST["merge_conv"]
            for p in range(4):
                b0 = 4 * ((p + 1) % 2)
                for q in range(2):
                    dve.wait_ge(unit_used, done(u + 3 * p + q))
                    if p >= 1:
                        dve.wait_ge(mc_sum, 2 * p)
                    dve.tensor_tensor(wa[:, q, :], bank[b0 + 2 + q][:], scale[:], ALU.mult).then_inc(mc_gate, 1)
                dve.wait_ge(unit_used, done(u + 3 * p + 2))
                for q in range(2):
                    m = 2 * p + q
                    dve.wait_ge(mc_sig, m + 1)
                    dve.tensor_tensor(mixed[:, m, :], bank[b0 + q][:], wa[:, q, :], ALU.mult).then_inc(mc_sum, 1)

            def masked_top(n, r):
                b = n % TB
                if n >= 2:
                    dve.wait_ge(att.exp, r - 1)
                w = (b + 1) * P
                return dve.tensor_tensor_reduce(wb[:, n % 2, 0:w], bank[n % 3][:, 0:w], mask_of(b), -1.0, 3.0e38,
                                                ALU.add, ALU.min, top[:, r % 4:r % 4 + 1])

            dve.wait_ge(masked, TB)
            def main_gate(n):
                if n % TB == 0 and 0 < n <= HB:
                    m = n // TB - 1
                    dve.wait_ge(unit_used, done(FIRST["gate_a"] + m))
                    dve.tensor_tensor(gate_a[:, m, :], bank[7][:], scale[:], ALU.mult).then_inc(ga_scaled, 1)

            attention(a_main, (0, HB), masked_top, lambda n: n % TB + 1, a_pt_h, a_pt_l, paired(qa_h, qa_l), main_gate)

            dve.wait_ge(mem_sum, MB)
            rsqrt(n_x[:, 0:MB], n_y[:, 0:MB], n_t[:, 0:MB], mem_sq[:], D, n_mem, 0)
            for b in range(MB):
                dve.tensor_scalar(mem_rows[:, b, :], mem_rows[:, b, :], n_y[:, b:b + 1], None, ALU.mult).then_inc(mem_normed, 1)
            for m in range(KC):
                c = m % 2
                dve.wait_ge(unit_used, done(FIRST["attn_out"] + m // 2))
                dve.wait_ge(ga_sig, m + 1)
                dve.tensor_tensor(wa[:, c, :], bank[m % 4][:], gate_a[:, m, :], ALU.mult).then_inc(ma_term, 1)
                dve.wait_ge(ma_term, m + 1)
                dve.tensor_tensor(mixed[:, m, :], mixed[:, m, :], wa[:, c, :], ALU.add).then_inc(ma_sum, 1)
                dve.wait_ge(merged.hi, m + 1)
                dve.tensor_tensor(mm_l[:, m, :], mixed[:, m, :], mm_h[:, m, :].bitcast(F32), ALU.subtract).then_inc(merged.lo, 1)
            for k in range(KC):
                dve.wait_ge(memt.hi, k // 2 * 2 + 2)
                dve.scalar_tensor_tensor(memt_l[:, k, :], bank[4 + k // 2][:, k % 2 * N_MEM:(k % 2 + 1) * N_MEM], gain("mem_g", k),
                                         memt_h[:, k, :].bitcast(F32), ALU.mult, ALU.subtract).then_inc(memt.lo, 1)

            def out_chunks(u, full, NP, b0):
                for m in range(KC):
                    dve.wait_ge(unit_used, done(u + m))
                    dve.tensor_copy(f[:, m, :], bank[b0 + m % 2][:]).then_inc(full, 1)
                    if m >= 1:
                        add_squares(NP, m - 1)
                add_squares(NP, KC - 1)

            out_chunks(FIRST["mix_out"], mo_full, n_mixp, 2)

            def mem_key(m):
                dve.wait_ge(mk.hi, m + 1)
                dve.tensor_tensor(mk_l[:, m, :], bank[m % 4][:, 0:N_MEM], mk_h[:, m, :].bitcast(F32), ALU.subtract).then_inc(mk.lo, 1)

            newton(n_mixp, D)
            lay_out(n_mixp)
            for m in range(3):
                mem_key(m)
            for k in range(KC):
                residual_chunk(r_mix, n_mixp, "mix_post_g", 1.0, k)
                if k + 3 < KC:
                    mem_key(k + 3)
                if k >= 1:
                    remainder(x_x, k - 1, "xattn_pre_g")
            remainder(x_x, KC - 1, "xattn_pre_g")
            for c in range(2):
                for k in range(4 * c - c, 3 + 4 * c):
                    add_squares(n_xq, k)
                for b in range(MB):
                    part = (slice(None), b, slice(c * T, (c + 1) * T))
                    dve.wait_ge(mv.hi, 2 * c + b + 1)
                    dve.tensor_tensor(mv_l[part], bank[(4, 0)[c] + b][:], mv_h[part].bitcast(F32), ALU.subtract).then_inc(mv.lo, 1)
            add_squares(n_xq, KC - 1)
            newton(n_xq, D)
            lay_out(n_xq)
            dve.wait_ge(norm.scale, n_xq.scale0 + 1)
            for m in range(KC + 1):
                if m < KC:
                    dve.wait_ge(unit_used, done(FIRST["x_q"] + m))
                    if m >= 2:
                        dve.wait_ge(xq.lo, m - 1)
                    dve.scalar_tensor_tensor(wa[:, m % 2, :], bank[(2 + m) % 4][:], XD ** -0.5, scale[:],
                                             ALU.mult, ALU.mult).then_inc(xq_scaled, 1)
                if m >= 1:
                    dve.wait_ge(xq.hi, m)
                    dve.tensor_tensor(xq_l[:, m - 1, :], wa[:, (m - 1) % 2, :], xq_h[:, m - 1, :].bitcast(F32),
                                      ALU.subtract).then_inc(xq.lo, 1)

            def mem_pieces(g):
                out = []
                for c in range(2):
                    part = (slice(None), g // 2 * 2 + c, slice(g % 2 * 256, (g % 2 + 1) * 256))
                    out.append((2 * g + c, xl[part], bank[5 + c][:, 0:256], xh[part]))
                return out

            attention(a_mem, (0, XH * TB), plain_top(N_MEM), lambda n: MB, x_pt_h, x_pt_l, mem_pieces)
            out_chunks(FIRST["x_out"], xo_full, n_xp, 4)
            residual(r_x, n_xp, "xattn_post_g", 1.0, x_ffn2, "ffn2_pre_g", n_ffn2)

            feed_forward("ffn2", ffn2, n_ffn2, n_ffn2p)
            residual(r_ffn2, n_ffn2p, "ffn2_post_g", 0.5, x_mix2, "g_mix_2", n_mix2)

            newton(n_mix2, D)
            lay_out(n_mix2)
            dve.wait_ge(norm.scale, n_mix2.scale0 + 1)
            for r in range(6):
                dve.wait_ge(unit_used, done(FIRST["grouped"] + r))
                dve.tensor_tensor(g_x[:, r, :], bank[r % 4][:], scale[:], ALU.mult).then_inc(gx.x, 1)
            for kv in range(2):
                zero(gv_h[:, kv, :, HD:P])
                zero(gv_l[:, kv, :, HD:P]).then_inc(v_zero, 1)
            dve.wait_ge(unit_used, done(FIRST["grouped"] + 6))
            dve.tensor_tensor(g_v[:], bank[6][:], scale[:], ALU.mult).then_inc(gv_scaled, 1)
            turned_g = bank[6][:].rearrange("p (b c) -> p b c", c=P)
            for n in range(4):
                kv, par = n // 2, n % 2
                part = (slice(None), kv, slice(None), slice(par * P, par * P + HD))
                dve.wait_ge(gv.hi, 4)
                dve.tensor_tensor(gv_l[part], turned_g[:, :, kv * HD:(kv + 1) * HD], gv_h[part].bitcast(F32), ALU.subtract).then_inc(gv.lo, 1)
            newton(n_heads, HD, slice(0, 12 * TB))
            dve.wait_ge(tab_in, 32)

            def grouped_sum(n):
                r = GROUPED_ORDER[n]
                dve.wait_ge(gx.rot, n + 1)
                dve.tensor_tensor(g_x[:, r, :], bank[n % 2][:], tab[:, 1, :], ALU.mult).then_inc(gx.sin, 1)
                dve.wait_ge(gx.sin, n + 1)
                dve.tensor_tensor(wb[:, n % 2, :], wb[:, n % 2, :], g_x[:, r, :], ALU.add).then_inc(gx.sum, 1)

            def grouped_lo(n):
                r = GROUPED_ORDER[n]
                a, b, s = (gq_l[:, r, :], gq_h[:, r, :], HD ** -0.5) if r < 4 else (gk_l[:, r - 4, :], gk_h[:, r - 4, :], 1.0)
                dve.wait_ge(gx.out.hi, n + 1)
                dve.scalar_tensor_tensor(a, wb[:, n % 2, :], s, b.bitcast(F32), ALU.mult, ALU.subtract).then_inc(gx.out.lo, 1)

            def gate(g, source):
                dve.wait_ge(unit_used, done(gate_unit(g)))
                if g:
                    dve.wait_ge(gate_out, 16 * g)
                dve.tensor_tensor(gate_stage[:], bank[source][:], scale[:], ALU.mult).then_inc(gate_scaled, 1)

            by_head = n_y[:, 0:12 * TB].rearrange("p (b c) -> p b c", c=12)

            def lay_out_heads(n):
                r = GROUPED_ORDER[n]
                dve.tensor_copy(expand[:].rearrange("p b (h c) -> p b h c", c=HD),
                                by_head[:, :, 2 * r:2 * r + 2].unsqueeze(3).to_broadcast([P, TB, 2, HD])).then_inc(norm.expand, 1)

            for n, r in enumerate(GROUPED_ORDER):
                if n == 0:
                    dve.wait_ge(norm.spread, n_heads.expand0)
                    lay_out_heads(0)
                if n >= 2:
                    grouped_lo(n - 2)
                dve.wait_ge(norm.spread, n_heads.expand0 + n + 1)
                if n + 1 < 6:
                    lay_out_heads(n + 1)
                dve.scalar_tensor_tensor(g_x[:, r, :], g_x[:, r, :], gain_row(G_QN_ROW if r < 4 else G_KN_ROW),
                                         bank[4 + n % 2][:], ALU.mult, ALU.mult).then_inc(gx_normed, 1)
                dve.wait_ge(gx_normed, n + 1)
                dve.tensor_tensor(wb[:, n % 2, :], g_x[:, r, :], tab[:, 0, :], ALU.mult).then_inc(gx.cos, 1)
                if n >= 1:
                    gate(n - 1, 2 + (n - 1) % 2)
                    grouped_sum(n - 1)
            grouped_lo(4)
            gate(5, 3)
            grouped_sum(5)
            grouped_lo(5)
            attention(a_grp, (0, HB), plain_top(T), lambda n: TB, g_pt_h, g_pt_l, paired(go_h, go_l),
                      lambda n: gate(GROUPED_GATES[n - 1], 7) if n - 1 in GROUPED_GATES else None)

            u = FIRST["latent"]
            for r in range(3):
                dve.wait_ge(unit_used, done(u + r))
                dve.tensor_tensor(l_x[:, r, :], bank[r][:], scale[:], ALU.mult).then_inc(lx, 1)
            dve.wait_ge(unit_used, done(u + 3))
            dve.tensor_tensor(l_x[:, 3, :], bank[3][:], scale[:], ALU.mult).then_inc(kpe.x, 1)
            for k in range(2):
                add_squares(n_cq, k)
            newton(n_cq, LAT_Q)
            lay_out(n_cq)
            dve.wait_ge(lx, 3)
            dve.wait_ge(norm.spread, n_cq.expand0 + 1)
            for k in range(2):
                dve.scalar_tensor_tensor(wb[:, k, :], l_x[:, k, :], gain_row(G_QA_ROW + k), bank[SPREAD][:],
                                         ALU.mult, ALU.mult).then_inc(l_normed, 1)
            add_squares(n_ckv, 0)
            newton(n_ckv, LAT_KV, slice(8, 8 + TB))
            lay_out(n_ckv)
            dve.wait_ge(norm.spread, n_ckv.expand0 + 1)
            dve.scalar_tensor_tensor(wa[:, 0, :], l_x[:, 2, :], gain_row(G_KVA_ROW), bank[5][:],
                                     ALU.mult, ALU.mult).then_inc(l_normed, 1)
            dve.wait_ge(tab_in, 48)
            dve.wait_ge(kpe.x, 1)
            dve.tensor_tensor(wa[:, 1, :], l_x[:, 3, :], tab[:, 0, :], ALU.mult).then_inc(kpe.cos, 1)
            dve.wait_ge(kpe.rot, 1)
            dve.wait_ge(kpe.cos, 1)
            dve.tensor_tensor(l_x[:, 3, :], bank[4][:], tab[:, 1, :], ALU.mult).then_inc(kpe.sin, 1)
            dve.wait_ge(kpe.sin, 1)
            dve.tensor_tensor(wa[:, 1, :], wa[:, 1, :], l_x[:, 3, :], ALU.add).then_inc(kpe.sum, 1)
            gate(8, 2)
            for k in range(3):
                a, b, s = ((cq_l[:, 0, :], cq_h[:, 0, :], wb[:, 0, :]), (cq_l[:, 1, :], cq_h[:, 1, :], wb[:, 1, :]),
                           (ck_l[:], ck_h[:], wa[:, 0, :]))[k]
                dve.wait_ge(l_lat.hi, k + 1)
                dve.tensor_tensor(a, s, b.bitcast(F32), ALU.subtract).then_inc(l_lat.lo, 1)
            for q in range(2):
                dve.wait_ge(kpe.out.hi, q + 1)
                dve.tensor_tensor(lk_l[NOPE:QW, q, :], wa[NOPE:QW, 1, :], lk_h[NOPE:QW, q, :].bitcast(F32),
                                  ALU.subtract).then_inc(kpe.out.lo, 1)
            zero(lv_h[:, :, HD:P])
            zero(lv_l[:, :, HD:P]).then_inc(v_zero, 1)
            gate(9, 3)

            def pair_gates(c, n):
                if n == 1:
                    gate(PAIR_GATE[c], 7)
                if c in PAIR_GATE_2 and n == 4:
                    gate(PAIR_GATE_2[c], 7)

            for c in range(4):
                for q in range(2):
                    dve.wait_ge(lq.x, 2 * c + q + 1)
                    dve.tensor_tensor(wb[0:QW, q, :], l_q[0:QW, q, :], tab[0:QW, 0, :], ALU.mult).then_inc(lq.cos, 1)
                for q in range(2):
                    dve.wait_ge(lk.hi, 2 * c + q + 1)
                    dve.tensor_tensor(lk_l[0:NOPE, q, :], bank[2 + q][0:NOPE, :], lk_h[0:NOPE, q, :].bitcast(F32),
                                      ALU.subtract).then_inc(lk.lo, 1)
                for q in range(2):
                    dve.wait_ge(lq.rot, 2 * c + q + 1)
                    dve.wait_ge(lq.cos, 2 * c + q + 1)
                    dve.tensor_tensor(l_q[0:QW, q, :], bank[4 + q][0:QW, :], tab[0:QW, 1, :], ALU.mult).then_inc(lq.sin, 1)
                    dve.wait_ge(lq.sin, 2 * c + q + 1)
                    dve.tensor_tensor(wb[0:QW, q, :], wb[0:QW, q, :], l_q[0:QW, q, :], ALU.add).then_inc(lq.sum, 1)
                for q in range(2):
                    part = (slice(None), slice(None), slice(q * P, q * P + HD))
                    dve.wait_ge(lv.hi, 2 * c + 2)
                    dve.tensor_tensor(lv_l[part], bank[6][:].rearrange("p (s c) -> p s c", c=P)[:, :, q * HD:(q + 1) * HD],
                                      lv_h[part].bitcast(F32), ALU.subtract).then_inc(lv.lo, 1)
                for q in range(2):
                    dve.wait_ge(lq.out.hi, 2 * c + q + 1)
                    dve.scalar_tensor_tensor(lq_l[0:QW, q, :], wb[0:QW, q, :], QW ** -0.5, lq_h[0:QW, q, :].bitcast(F32),
                                             ALU.mult, ALU.subtract).then_inc(lq.out.lo, 1)
                attention(a_lat, (2 * TB * c, 2 * TB * (c + 1)), plain_top(T), lambda n: TB, l_pt_h, l_pt_l, paired(lo_h, lo_l),
                          lambda n: pair_gates(c, n - 2 * TB * c))

            def merged_lo(m):
                dve.wait_ge(merged2.hi, m + 1)
                dve.tensor_tensor(mg_l[:, m, :], wa[:, m % 2, :], mg_h[:, m, :].bitcast(F32), ALU.subtract).then_inc(merged2.lo, 1)

            for m in range(KC):
                c, b0 = m % 2, 4 * (m // 2 % 2)
                dve.wait_ge(unit_used, done(FIRST["merge"] + m // 2 * 2 + 1))
                dve.wait_ge(gate_sig, m + 1)
                if m >= 2:
                    dve.wait_ge(merged2.lo, m - 1)
                for n, t in enumerate((wa, wb)):
                    dve.tensor_tensor(t[:, c, :], bank[b0 + 2 * n + c][:], gates_back[:, m % 4, n, :], ALU.mult).then_inc(me_term, 1)
                dve.wait_ge(me_term, 2 * m + 2)
                dve.tensor_tensor(wa[:, c, :], wa[:, c, :], wb[:, c, :], ALU.add).then_inc(me_sum, 1)
                if m >= 1:
                    merged_lo(m - 1)
            merged_lo(KC - 1)
            for m in range(KC):
                dve.wait_ge(unit_used, done(FIRST["out"] + m))
                dve.tensor_tensor(h[:, m, :], bank[1 + m % 3][:], h[:, m, :], ALU.add).then_inc(h_out, 1)
                if m >= 1:
                    remainder(x_mlp, m - 1, "g_mlp_2")
                    add_squares(n_mlp, m - 1)
            remainder(x_mlp, KC - 1, "g_mlp_2")
            add_squares(n_mlp, KC - 1)
            for k in range(2):
                dve.wait_ge(p_split.hi, k + 1)
                dve.tensor_tensor(pt_l[:, k, :], bank[4 + k][:], pt_h[:, k, :].bitcast(F32), ALU.subtract).then_inc(p_split.lo, 1)
            newton(n_mlp, D)
            lay_out(n_mlp)
            dve.wait_ge(norm.scale, n_mlp.scale0 + 1)

            def mlp_up(first, j0, i):
                for q in range(RING):
                    c = q % 2
                    dve.wait_ge(unit_used, done(first + q, i))
                    dve.tensor_tensor(wa[:, c, :], bank[q][:], scale[:], ALU.mult).then_inc(ml_x, 1)
                    dve.wait_ge(ml_x, 4 * i + (j0 + q + 1))
                    dve.scalar_tensor_tensor(wb[:, c, :], wa[:, c, :], 0.0, wa[:, c, :], ALU.max, ALU.mult).then_inc(ml_sq, 1)
                    dve.wait_ge(ml_hid.hi, 4 * i + (j0 + q + 1))
                    dve.tensor_tensor(hid_l[:, 4 * i + q, :], wb[:, c, :], hid_h[:, 4 * i + q, :].bitcast(F32),
                                      ALU.subtract).then_inc(ml_hid.lo, 1)

            def mlp_down(first, kept, i, split, opening=False):
                for m in range(2):
                    dve.wait_ge(unit_used, done(first + 2 * m + 1, i))
                    x = h[:, 2 * i + m, :]
                    dve.tensor_tensor(x, bank[4 + m][:], x, ALU.add).then_inc(kept, 1)
                    if split:
                        row = GAINS.index("g_ple_2") * KC + m
                        dve.wait_ge(x_ple.hi, 2 * i + (x_ple.first + m + 1))
                        dve.scalar_tensor_tensor(xl[:, 2 * i + m, :], x, gains[:, bass.ds(2 * i + row, 1)],
                                                 xh[:, 2 * i + m, :].bitcast(F32), ALU.mult, ALU.subtract).then_inc(x_ple.lo, 1)
                        add_squares(n_ple, m, None if opening else i)

            with dve.Fori(0, FF2_HALF // RING) as i:
                mlp_up(FIRST["mlp_up_a"], 0, i)
            with dve.Fori(0, KC // 2) as i:
                mlp_down(FIRST["mlp_down_a"], ml_part, i, False)
            with dve.Fori(0, FF2_HALF // RING) as i:
                mlp_up(FIRST["mlp_up_b"], FF2_HALF, i)
            dve.wait_ge(ml_part, KC)
            mlp_down(FIRST["mlp_down_b"], h_mlp, 0, True, opening=True)
            with dve.Fori(1, KC // 2) as i:
                mlp_down(FIRST["mlp_down_b"], h_mlp, i, True)

            newton(n_ple, D)
            lay_out(n_ple)
            dve.wait_ge(norm.scale, n_ple.scale0 + 1)
            for m in range(KC):
                c = m % 2
                dve.wait_ge(unit_used, done(FIRST["ple_gate"] + m))
                dve.tensor_tensor(wa[:, c, :], bank[2 + c][:], scale[:], ALU.mult).then_inc(pg_x, 1)
                dve.wait_ge(pg_sig, m + 1)
                dve.wait_ge(ple_kept, m + 1)
                dve.tensor_tensor(wb[:, c, :], wa[:, c, :], ple[:, m, :], ALU.mult).then_inc(pg_term, 1)
                dve.wait_ge(pg_term, m + 1)
                dve.tensor_tensor(h[:, m, :], h[:, m, :], wb[:, c, :], ALU.add).then_inc(h_end, 1)
                if m >= 1:
                    add_squares(n_end, m - 1)
            add_squares(n_end, KC - 1)
            newton(n_end, D)
            lay_out(n_end)
            dve.wait_ge(norm.spread, n_end.expand0 + 1)
            for k in range(KC):
                dve.scalar_tensor_tensor(normed[:, k, :], h[:, k, :], gain("g_final_2", k), bank[SPREAD][:],
                                         ALU.mult, ALU.mult).then_inc(end_normed, 1)


INPUTS = ["x", "mem", "ffn1_pre_g", "ffn1_post_g", "ffn1_w1", "ffn1_w3", "ffn1_w2", "mix_pre_g", "mix_post_g", "w_in",
          "conv_w", "w_a_out", "w_b_out", "w_out", "mem_g", "xattn_pre_g", "xattn_post_g", "xattn_w_q", "xattn_w_kv",
          "xattn_w_o", "ffn2_pre_g", "ffn2_post_g", "ffn2_w1", "ffn2_w3", "ffn2_w2", "p_2", "g_mix_2", "w_in_2", "g_qa_2",
          "w_qb_2", "g_kva_2", "w_kvb_2", "g_qn_2", "g_kn_2", "w_oa_2", "w_ob_2", "w_o_2", "g_mlp_2", "w_up_2", "w_down_2",
          "g_ple_2", "w_ple_gate_2", "w_ple_2", "g_final_2"]


def kernel(**inputs):
    import concourse.bacc as bacc
    from concourse.bass_utils import run_bass_kernel_spmd

    nc = bacc.Bacc("TRN2", target_bir_lowering=False, num_devices=1)
    arrays = {f"in_{name}": np.ascontiguousarray(inputs[name]) for name in INPUTS}
    vectors = [inputs[name] for name in GAINS] + [inputs["g_qa_2"], inputs["g_kva_2"], inputs["conv_w"]]
    vectors += [inputs[name] for name in ("g_qn_2", "g_kn_2") for _ in range(2)]
    columns = np.concatenate([np.ravel(v) for v in vectors]).reshape(GAIN_ROWS, P).T
    arrays["in_gain_columns"] = np.ascontiguousarray(columns)
    mats, tabs = shape_constants()
    arrays["in_shape_mats"] = np.ascontiguousarray(mats.reshape(P, -1))
    arrays["in_shape_tabs"] = np.ascontiguousarray(tabs.reshape(P, -1))
    dram = {name[3:]: nc.dram_tensor(name, a.shape, mybir.dt.from_np(a.dtype), kind="ExternalInput").ap()
            for name, a in arrays.items()}
    out = nc.dram_tensor("out_0", (1, T, D), F32, kind="ExternalOutput").ap()
    build(nc, dram, out)
    result = run_bass_kernel_spmd(nc, [arrays], core_ids=[0])
    return result.results[0]["out_0"]
```

```python
from contextlib import ExitStack

import numpy as np

import concourse.bass as bass
from concourse import mybir

F32 = mybir.dt.float32
F32R = mybir.dt.float32r
I32 = mybir.dt.int32
ALU = mybir.AluOpType
ACT = mybir.ActivationFunctionType
AX = mybir.AxisListType

P = 128
T = 512
TB = T // P
D = 1024
KC = D // P
N_MEM = 256
MB = N_MEM // P
FF = 2816 // P
FF_A, FF_B = 16, 6
FF2 = 4096 // P
FF2_HALF = FF2 // 2
HEADS = 8
HD = 64
TOP_K = 128
LAT_Q, LAT_KV, ROPE_D, NOPE = 256, 128, 32, 64
QW = NOPE + ROPE_D
XH, XD = 4, 256
PLE = 256
EPS = 1e-6
RSQRT_SEED = float(0x5F3759DF)
NEWTON_COUNT = 9
RING = 4
LOOKAHEAD = 3
UNIT = 1024
REPLACED = -(2.0 ** 127)
NOT_CAUSAL = -(2.0 ** 126)
MASKED = -(2.0 ** 100)

C_QA, C_KA, C_VA, C_QI, C_KI, C_WI = 0, 512, 576, 640, 1152, 1216
C_GB, C_GC, C_CI, C_GA, C_GBB = 1224, 1736, 2248, 2760, 3784
Z_QL, Z_KVL, Z_KPE, Z_QB, Z_KB, Z_VB, Z_GA, Z_GB = 0, 256, 384, 416, 928, 1056, 1184, 2208

GAINS = ["ffn1_pre_g", "ffn1_post_g", "mix_pre_g", "mix_post_g", "mem_g", "xattn_pre_g", "xattn_post_g",
         "ffn2_pre_g", "ffn2_post_g", "g_mix_2", "g_mlp_2", "g_ple_2", "g_final_2"]
G_QA_ROW = len(GAINS) * KC
G_KVA_ROW = G_QA_ROW + LAT_Q // P
CONV_ROW = G_KVA_ROW + 1
G_QN_ROW = CONV_ROW + 3 * 4
G_KN_ROW = G_QN_ROW + 1
GAIN_ROWS = G_KN_ROW + 1

STEPS = [("ffn1_up_a", 2 * FF_A), ("ffn1_down_a", 2 * KC), ("ffn1_up_b", 2 * FF_B), ("ffn1_down_b", KC),
         ("index", 5), ("values", 1), ("queries", 5), ("conv", 12), ("merge_conv", 12), ("gate_a", 8),
         ("attn_out", 4), ("mix_out", 8),
         ("mem_k", 8), ("mem_v", 8), ("x_q", 8), ("x_out", 8),
         ("ffn2_up_a", 2 * FF_A), ("ffn2_down_a", 2 * KC), ("ffn2_up_b", 2 * FF_B), ("ffn2_down_b", KC),
         ("grouped", 7), ("gates", 8), ("latent", 4), ("latent_gates", 2), ("latent_heads", 10),
         ("merge", 8), ("out", 8),
         ("mlp_up_a", FF2_HALF), ("mlp_down_a", FF2_HALF), ("mlp_up_b", FF2_HALF), ("mlp_down_b", FF2_HALF),
         ("ple", 2), ("ple_gate", 8)]
FIRST = {}
UNITS = 0
for _name, _n in STEPS:
    FIRST[_name] = UNITS
    UNITS += _n
assert UNITS % RING == 0
HEAD_UNITS = (0, 3, 6, 8)
PAIR_GATE = (10, 12, 14, 15)
PAIR_GATE_2 = {0: 11, 1: 13}
TWO_PART = [FIRST["index"] + 4, FIRST["values"], FIRST["queries"] + 4, FIRST["grouped"] + 4, FIRST["grouped"] + 5,
            *[FIRST["latent_heads"] + n for n in HEAD_UNITS]]


def gate_unit(g):
    if g < 8:
        return FIRST["gates"] + g
    if g < 10:
        return FIRST["latent_gates"] + g - 8
    return FIRST["latent_heads"] + (1, 2, 4, 5, 7, 9)[g - 10]


def merge_conv_unit(p, q):
    return FIRST["merge_conv"] + MERGE_CONV.index((p, q))


def shape_constants():
    i = np.arange(P)
    ident = np.eye(P, dtype=np.float32)

    def rotation(half):
        m = np.zeros((P, P), np.float32)
        first = (i % (2 * half)) < half
        m[i[first] + half, i[first]] = -1.0
        m[i[~first] - half, i[~first]] = 1.0
        return m

    causal = np.where(i[None, :] <= i[:, None], 0.0, 1.0).astype(np.float32)
    heads = np.zeros((P, P), np.float32)
    heads[:HD, 0] = 1.0
    heads[HD:, 1] = 1.0
    mats = np.concatenate([ident, np.ones((P, P), np.float32), rotation(32), rotation(16), causal, heads], 1)

    def angles(pos, dim):
        inv = (10000.0 ** (-(np.arange(0, dim, 2, dtype=np.float32) / np.float32(dim)).astype(np.float64)))
        return pos.astype(np.float32)[:, None] * inv.astype(np.float32)[None, :]

    def tables(ang_rows):
        ang = np.stack(ang_rows).astype(np.float64)
        return np.cos(ang).astype(np.float32), np.sin(ang).astype(np.float32)

    t = np.arange(T)
    a64 = angles(t, 64)
    main = tables([a64[:, p % 32] for p in range(P)])
    a32 = angles(t, ROPE_D)
    lat = tables([a32[:, p % 16] if NOPE <= p < QW else np.zeros(T) for p in range(P)])
    row, col = angles(t // 64, 32), angles(t % 64, 32)
    grid = tables([(row if p % 64 < 32 else col)[:, p % 16] for p in range(P)])
    return mats, np.concatenate([np.stack(x, 1) for x in (main, lat, grid)], 1).reshape(P, 3, 2, T)


END_BANKS = (0, 1, 4, 5)
CONV_BANKS = ((6, 4, 5), (0, 2, 3))
ROUNDS = 3 * TOP_K // 8
SEARCHED = (ROUNDS // 3, ROUNDS // 2, 2 * ROUNDS // 3, 2 * ROUNDS // 3)
SEARCHED_2 = (19 * ROUNDS // 24, 11 * ROUNDS // 12, ROUNDS, ROUNDS)
MERGE_CONV = ((0, 0), (0, 1), (1, 0), (1, 1), (0, 2), (1, 2), (2, 0), (2, 1), (2, 2), (3, 0), (3, 1), (3, 2))
LATE_QUERIES = (1, 4, 7, 9)
GROUPED_ORDER = (4, 5, 0, 1, 2, 3)
IDX_SUM = [n // HEADS * (HEADS + 1) + n % HEADS + 1 for n in range(3 * HEADS)]


class Split:

    def __init__(self, sem, name):
        self.hi = sem(name + "_hi")
        self.lo = sem(name + "_lo")


class NormSems:

    def __init__(self, sem):
        self.squares = sem("norm_squares")
        self.added = sem("norm_added")
        self.summed = sem("norm_summed")
        self.newton = sem("norm_newton")
        self.spread = sem("norm_spread")
        self.scale = sem("norm_scale")


class Norm:

    def __init__(self, before, chunks, copies, spreads=1, heads=False, last_apart=False):
        self.before, self.chunks, self.copies, self.heads = before, chunks, copies, heads
        self.spreads = spreads
        self.adds, self.sums = (0, chunks) if heads else (chunks - 1 if last_apart else chunks, 1)
        self.add0 = before.add0 + before.adds if before else 0
        self.sum0 = before.sum0 + before.sums if before else 0
        self.chunk0 = before.chunk0 + before.chunks if before else 0
        self.spread0 = before.spread0 + before.spreads if before else 0
        self.scale0 = before.scale0 + before.copies if before else 0
        self.newton0 = before.newton0 + NEWTON_COUNT if before else 0

    def slot_user(self, k):
        norm, n = self, k - 2
        while n < 0:
            if norm.before is None:
                return None
            norm = norm.before
            n += norm.chunks
        if norm.heads:
            return "summed", norm.sum0 + n + 1
        return ("added", norm.add0 + n + 1) if n < norm.adds else ("summed", norm.sum0 + 1)


class Entry:

    def __init__(self, split, n):
        self.hi, self.lo, self.first = split.hi, split.lo, n * KC


class FfnSems:

    def __init__(self, sem):
        self.gate = sem("ffn_gate")
        self.silu = sem("ffn_silu")
        self.up = sem("ffn_up")
        self.prod = sem("ffn_prod")
        self.hid = Split(sem, "ffn_hid")
        self.part = sem("ffn_part")
        self.full = sem("ffn_full")


class Ffn:

    def __init__(self, n):
        self.hid0, self.out0 = n * FF, n * KC


class Residual:

    def __init__(self, term, h, n):
        self.term = term
        self.h = h
        self.first = n * KC


class Rope:
    def __init__(self, sem, name):
        self.x = sem(name + "_x")
        self.cos = sem(name + "_cos")
        self.rot = sem(name + "_rot")
        self.sin = sem(name + "_sin")
        self.sum = sem(name + "_sum")
        self.out = Split(sem, name + "_out")


class AttentionSems:

    def __init__(self, sem):
        self.logits = sem("att_logits")
        self.top = sem("att_top")
        self.exp = sem("att_exp")
        self.inv = sem("att_inv")
        self.probs = sem("att_probs")
        self.turned = sem("att_turned")
        self.pt = Split(sem, "att_pt")
        self.pv = sem("att_pv")
        self.out = Split(sem, "att_out")


class Attention:

    def __init__(self, block0, piece0):
        self.block0, self.half0, self.piece0 = block0, block0 // 2, piece0


def build(nc, dram, out):
    base = -(-nc.sbuf_base // 32) * 32
    place = [base]

    def fixed(name, shape, dt):
        words = int(np.prod(shape[1:]))
        t = nc.alloc_sbuf_tensor_at(name, shape, dt, offset=place[0])
        place[0] += -(-words * 4 // 32) * 32
        return t

    mats = fixed("mats", [P, 6, P], F32)
    ident, ones, rot32, rot16, after_query, head_sel = (mats[:, n, :] for n in range(6))
    gains = fixed("gains", [P, GAIN_ROWS], F32)
    tab = fixed("rope_tab", [P, 2, T], F32)
    scale = fixed("scale", [P, T], F32)
    n_x = fixed("newton_x", [P, 48], F32)
    n_y = fixed("newton_y", [P, 48], F32)
    n_t = fixed("newton_t", [P, 48], F32)
    top = fixed("top", [P, 4], F32)
    sums = fixed("sums", [P, 4], F32)
    invs = fixed("invs", [P, 4], F32)
    w_idx = fixed("w_idx", [P, TB, HEADS], F32)
    best8 = fixed("best8", [P, 8], F32)
    mem_sq = fixed("mem_sq", [P, MB], F32)
    h = fixed("h", [P, KC, T], F32)
    mem_rows = nc.alloc_sbuf_tensor_at("mem_rows", [P, MB, D], F32, offset=place[0] + 4 * T * 4)
    xh = fixed("xh", [P, KC, T], F32R)
    mem_squares = nc.alloc_sbuf_tensor_at("mem_squares", [P, D], F32, offset=place[0] + 4 * T * 4)
    xl = fixed("xl", [P, KC, T], F32R)
    raw = fixed("ring_raw", [P, RING, UNIT], F32)
    wh = fixed("ring_hi", [P, RING, UNIT], F32R)
    wl = fixed("ring_lo", [P, RING, UNIT], F32R)
    arena = place[0]
    K = 1024

    def at(name, kib, shape, dt):
        offset = arena + int(kib * K)
        assert offset + int(np.prod(shape[1:])) * 4 <= nc.sbuf_usable_end, name
        return nc.alloc_sbuf_tensor_at(name, shape, dt, offset=offset)

    f = at("f", 0, [P, KC, T], F32)
    squares = at("squares", 80, [P, 2, T], F32)
    wa = at("work_a", 84, [P, 2, T], F32)
    wb = at("work_b", 88, [P, 2, T], F32)
    square_sum = at("square_sum", 92, [P, T], F32)
    expand = square_sum[:].rearrange("p (b c) -> p b c", c=P)
    probs = at("probs", 94, [P, 3, T], F32)
    x_rows = at("x_rows", 16, [P, TB, D], F32)
    hid_h = at("hid_h", 16, [P, FF2_HALF, T], F32R)
    hid_l = at("hid_l", 48, [P, FF2_HALF, T], F32R)
    cz_h = at("cz_h", 67, [P, 4, T], F32R)
    cz_l = at("cz_l", 75, [P, 4, T], F32R)
    c_gb = at("c_gb", 32, [P, 2, T], F32)
    c_gc = at("c_gc", 36, [P, 2, T], F32)
    c_y = at("c_y", 40, [P, 2, T + 8], F32)
    c_z = at("c_z", 52, [P, 2, T], F32)
    mixed = at("mixed", 0, [P, KC, T], F32)
    qa_h = at("qa_h", 16, [P, 4, T], F32R)
    qa_l = at("qa_l", 24, [P, 4, T], F32R)
    qi_h = at("qi_h", 32, [P, 4, T], F32R)
    qi_l = at("qi_l", 40, [P, 4, T], F32R)
    a_pt_h = at("a_pt_h", 32, [P, 2, 4, 256], F32R)
    a_pt_l = at("a_pt_l", 40, [P, 2, 4, 256], F32R)
    ka_h = at("ka_h", 48, [P, T], F32R)
    ka_l = at("ka_l", 50, [P, T], F32R)
    ki_h = at("ki_h", 52, [P, T], F32R)
    ki_l = at("ki_l", 54, [P, T], F32R)
    va_h = at("va_h", 56, [P, TB, 192], F32R)
    va_l = at("va_l", 59, [P, TB, 192], F32R)
    v_cols = at("v_cols", 94, [P, T], F32)
    mask = at("mask", 62, [P, TB * (TB + 1) // 2 * P], F32)
    gate_a = at("gate_a", 67, [P, KC, T], F32)
    mm_h = at("mm_h", 32, [P, KC, T], F32R)
    mm_l = at("mm_l", 48, [P, KC, T], F32R)
    mg_h = at("mg_h", 16, [P, KC, T], F32R)
    mg_l = at("mg_l", 32, [P, KC, T], F32R)
    memt_h = at("memt_h", 16, [P, KC, N_MEM], F32R)
    memt_l = at("memt_l", 24, [P, KC, N_MEM], F32R)
    mk_h = at("mk_h", 32, [P, KC, N_MEM], F32R)
    mk_l = at("mk_l", 40, [P, KC, N_MEM], F32R)
    mv_h = at("mv_h", 48, [P, MB, D], F32R)
    mv_l = at("mv_l", 56, [P, MB, D], F32R)
    xq_h = at("xq_h", 64, [P, KC, T], F32R)
    xq_l = at("xq_l", 16, [P, KC, T], F32R)
    x_pt_h = at("x_pt_h", 0, [P, 2, MB, 256], F32R)
    x_pt_l = at("x_pt_l", 4, [P, 2, MB, 256], F32R)
    go_h = at("go_h", 0, [P, 4, T], F32R)
    go_l = at("go_l", 8, [P, 4, T], F32R)
    gq_h = at("gq_h", 16, [P, 4, T], F32R)
    gq_l = at("gq_l", 24, [P, 4, T], F32R)
    gk_h = at("gk_h", 32, [P, 2, T], F32R)
    gk_l = at("gk_l", 36, [P, 2, T], F32R)
    gv_h = at("gv_h", 40, [P, 2, TB, 192], F32R)
    gv_l = at("gv_l", 46, [P, 2, TB, 192], F32R)
    g_pt_h = at("g_pt_h", 52, [P, 2, 4, 256], F32R)
    g_pt_l = at("g_pt_l", 60, [P, 2, 4, 256], F32R)
    g_x = at("g_x", 68, [P, 6, T], F32)
    g_v = at("g_v", 94, [P, T], F32)
    cq_h = at("cq_h", 16, [P, 2, T], F32R)
    cq_l = at("cq_l", 20, [P, 2, T], F32R)
    ck_h = at("ck_h", 24, [P, T], F32R)
    ck_l = at("ck_l", 26, [P, T], F32R)
    lq_h = at("lq_h", 28, [P, 2, T], F32R)
    lq_l = at("lq_l", 32, [P, 2, T], F32R)
    lk_h = at("lk_h", 36, [P, 2, T], F32R)
    lk_l = at("lk_l", 40, [P, 2, T], F32R)
    lv_h = at("lv_h", 44, [P, TB, 192], F32R)
    lv_l = at("lv_l", 47, [P, TB, 192], F32R)
    l_pt_h = at("l_pt_h", 50, [P, 2, 4, 256], F32R)
    l_pt_l = at("l_pt_l", 58, [P, 2, 4, 256], F32R)
    l_x = at("l_x", 66, [P, 4, T], F32)
    l_q = at("l_q", 84, [P, 2, T], F32)
    lo_h = at("lo_h", 66, [P, 4, T], F32R)
    lo_l = at("lo_l", 74, [P, 4, T], F32R)
    gate_stage = at("gate_stage", 82, [P, T], F32)
    gates_back = at("gates_back", 48, [P, 4, 2, T], F32)
    gate_store = nc.dram_tensor("gate_store", (2 * KC, P, T), F32, kind="Internal").ap()
    p_rows = at("p_rows", 0, [P, TB, PLE], F32)
    pt_h = at("pt_h", 4, [P, 2, T], F32R)
    pt_l = at("pt_l", 8, [P, 2, T], F32R)
    ple = at("ple", 16, [P, KC, T], F32)
    gained = at("gained", 0, [P, KC, T], F32)
    out_rows = at("out_rows", 32, [P, TB, D], F32)

    def mask_of(b):
        lo = b * (b + 1) // 2 * P
        return mask[:, lo:lo + (b + 1) * P]

    def gain(name, k):
        row = GAINS.index(name) * KC + k
        return gains[:, row:row + 1]

    def gain_row(row):
        return gains[:, row:row + 1]

    with ExitStack() as ctx:
        def sem(name):
            return ctx.enter_context(nc.semaphore(name))

        bank = [ctx.enter_context(nc.psum_tensor(f"bank{n}", [P, T], F32)) for n in range(8)]
        SPREAD, SUMS = 6, 7

        raw_in = [sem(f"raw_in{s}") for s in range(RING)]
        hi_ready = sem("hi_ready")
        lo_ready = sem("lo_ready")
        unit_used = sem("unit_used")
        const_in = sem("const_in")
        x_in = [sem(f"x_in{n}") for n in range(2)]
        mem_in = sem("mem_in")
        p_in = sem("p_in")
        tab_in = sem("tab_in")
        out_sent = sem("out_sent")
        gains_in = sem("gains_in")
        x_turned = sem("x_turned")
        x_kept = sem("x_kept")
        norm = NormSems(sem)
        n_ffn1 = Norm(None, KC, 1)
        n_ffn1p = Norm(n_ffn1, KC, 0, last_apart=True)
        n_mix = Norm(n_ffn1p, KC, 1)
        n_mixp = Norm(n_mix, KC, 0, last_apart=True)
        n_xq = Norm(n_mixp, KC, 1)
        n_xp = Norm(n_xq, KC, 0, last_apart=True)
        n_ffn2 = Norm(n_xp, KC, 1)
        n_ffn2p = Norm(n_ffn2, KC, 0, last_apart=True)
        n_mix2 = Norm(n_ffn2p, KC, 1)
        n_heads = Norm(n_mix2, 6, 0, spreads=6, heads=True)
        n_cq = Norm(n_heads, LAT_Q // P, 0, last_apart=True)
        n_ckv = Norm(n_cq, 1, 0, last_apart=True)
        n_mlp = Norm(n_ckv, KC, 1)
        n_ple = Norm(n_mlp, KC, 1)
        n_end = Norm(n_ple, KC, 0, spreads=0, last_apart=True)
        n_mem = sem("n_mem")
        entry = Split(sem, "entry")
        x_ffn1, x_mix, x_x, x_ffn2, x_mix2, x_mlp, x_ple = (Entry(entry, n) for n in range(7))
        ffn = FfnSems(sem)
        ffn1, ffn2 = Ffn(0), Ffn(1)
        normed_term, h_added = sem("normed_term"), sem("h_added")
        r_ffn1, r_mix, r_x, r_ffn2 = (Residual(normed_term, h_added, n) for n in range(4))
        conv_step = sem("conv_step")
        conv_tap = sem("conv_tap")
        conv_out = Split(sem, "conv_out")
        mc_gate, mc_sig, mc_sum = sem("mc_gate"), sem("mc_sig"), sem("mc_sum")
        rope = Rope(sem, "rope")
        v_scaled, v_turned, v_split = sem("v_scaled"), sem("v_turned"), Split(sem, "v_split")
        v_zero = sem("v_zero")
        idx_raw, idx_relu, idx_sum = sem("idx_raw"), sem("idx_relu"), sem("idx_sum")
        taken = sem("taken")
        masked = sem("masked")
        ga_scaled, ga_sig = sem("ga_scaled"), sem("ga_sig")
        att = AttentionSems(sem)
        HB = HEADS * TB
        a_main, a_mem = Attention(0, 0), Attention(HB, HEADS)
        a_grp = Attention(HB + XH * TB, HEADS + 4 * XH)
        a_lat = Attention(2 * HB + XH * TB, 2 * HEADS + 4 * XH)
        ma_term, ma_sum, merged = sem("ma_term"), sem("ma_sum"), Split(sem, "merged")
        out_full = sem("out_full")
        mem_sum, mem_normed, mem_turned = sem("mem_sum"), sem("mem_normed"), sem("mem_turned")
        memt, mk, mv = Split(sem, "memt"), Split(sem, "mk"), Split(sem, "mv")
        xq_scaled, xq = sem("xq_scaled"), Split(sem, "xq")
        gx, gx_normed = Rope(sem, "gx"), sem("gx_normed")
        heads_laid = sem("heads_laid")
        gv_scaled, gv_turned, gv = sem("gv_scaled"), sem("gv_turned"), Split(sem, "gv")
        lx, l_normed, l_lat = sem("lx"), sem("l_normed"), Split(sem, "l_lat")
        kpe = Rope(sem, "kpe")
        lq, lk, lv = Rope(sem, "lq"), Split(sem, "lk"), Split(sem, "lv")
        lat_raw = sem("lat_raw")
        gate_scaled, gate_sig = sem("gate_scaled"), sem("gate_sig")
        gate_out = sem("gate_out")
        gate_in = [sem(f"gate_in{n}") for n in range(4)]
        me_term, me_sum = sem("me_term"), sem("me_sum")
        h_out = sem("h_out")
        p_turned, p_split = sem("p_turned"), Split(sem, "p_split")
        ml_x, ml_sq, ml_hid = sem("ml_x"), sem("ml_sq"), Split(sem, "ml_hid")
        ml_part, h_mlp = sem("ml_part"), sem("h_mlp")
        ple_kept, pg_x, pg_sig, pg_term, h_end = (sem(n) for n in ("ple_kept", "pg_x", "pg_sig", "pg_term", "h_end"))
        end_gained, end_turned, end_kept = sem("end_gained"), sem("end_turned"), sem("end_kept")
        end_scaled = sem("end_scaled")
        end_scaled_act = sem("end_scaled_act")

        block = ctx.enter_context(nc.Block())

        def landed(u):
            return 16 * (u // RING + 1 + sum(v <= u and v % RING == u % RING for v in TWO_PART))

        def done(u, i=None):
            return u + 2 if i is None else 4 * i + (u + 2)

        @block.sync
        def _(sp):
            def load(u, src, width, i=None, at_col=0):
                if i is not None:
                    sp.wait_ge(lo_ready, 4 * i + (u - RING + 1))
                elif u >= RING:
                    sp.wait_ge(lo_ready, u - RING + 1)
                dst = raw[:, u % RING, at_col:at_col + src.shape[1] * width].rearrange("p (k c) -> p k c", c=width)
                return sp.dma_start(dst, src)

            def rows(name, c0, width=P, k0=0, nk=KC):
                w = dram[name][0][k0 * P:(k0 + nk) * P]
                return w.rearrange("(k p) c -> p k c", p=P)[:, :, c0:c0 + width]

            def rows_at(name, c0, width=P, k0=0, nk=KC):
                w = dram[name][0][k0 * P:(k0 + nk) * P]
                return w.rearrange("(k p) c -> p k c", p=P)[:, :, bass.ds(c0, width)]

            def fetch(u, src, width):
                load(u, src, width).then_inc(raw_in[u % RING], 16)

            def loop(first, turns, source, peel=False):
                def turn(i, static):
                    for q in range(RING):
                        load(first + q, source(i, q), P, None if static else i).then_inc(raw_in[(first + q) % RING], 16)
                if peel:
                    turn(0, True)
                with sp.Fori(1 if peel else 0, turns) as i:
                    turn(i, False)

            def feed_forward(name):
                w1, w3, w2 = name + "_w1", name + "_w3", name + "_w2"

                def up(j0):
                    return lambda i, q: rows_at((w1, w3)[q % 2], i * (2 * P) + (j0 + q // 2) * P)
                loop(FIRST[name + "_up_a"], FF_A // 2, up(0), peel=FIRST[name + "_up_a"] == 0)
                loop(FIRST[name + "_down_a"], KC // 2, lambda i, q: rows_at(w2, i * (2 * P) + q // 2 * P, k0=q % 2 * KC))
                loop(FIRST[name + "_up_b"], FF_B // 2, up(FF_A))
                loop(FIRST[name + "_down_b"], KC // RING, lambda i, q: rows_at(w2, i * (4 * P) + q * P, k0=FF_A, nk=FF_B))

            for b in range(TB // 2, TB):
                sp.dma_start(x_rows[:, b, :], dram["x"][0, b * P:(b + 1) * P, :]).then_inc(x_in[1], 16)
            feed_forward("ffn1")
            def fetch_twin(u, name, c0):
                dst = raw[:, u % RING, :].rearrange("p (k c) -> p k c", c=P)
                sp.wait_ge(lo_ready, u - RING + 1)
                sp.dma_start(dst[:, :, 0:HD], rows(name, c0, HD)).then_inc(raw_in[u % RING], 16)
                sp.dma_start(dst[:, :, HD:P], rows(name, c0, HD)).then_inc(raw_in[u % RING], 16)

            u = FIRST["index"]
            for c in range(4):
                fetch(u + c, rows("w_in", C_QI + c * P), P)
            fetch_twin(u + 4, "w_in", C_KI)
            u = FIRST["values"]
            dst = raw[:, u % RING, :].rearrange("p (k c) -> p k c", c=P)
            sp.wait_ge(lo_ready, u - RING + 1)
            sp.dma_start(dst[:, :, 0:HD], rows("w_in", C_VA, HD)).then_inc(raw_in[u % RING], 16)
            sp.dma_start(dst[:, :, HD:HD + HEADS], rows("w_in", C_WI, HEADS)).then_inc(raw_in[u % RING], 16)
            u = FIRST["queries"]
            for c in range(4):
                fetch(u + c, rows("w_in", C_QA + c * P), P)
            fetch_twin(u + 4, "w_in", C_KA)
            u = FIRST["conv"]
            for j in range(4):
                for q, c in enumerate((C_GB, C_GC, C_CI)):
                    fetch(u + 3 * j + q, rows("w_in", c + j * P), P)
            for p, q in MERGE_CONV:
                if q < 2:
                    fetch(merge_conv_unit(p, q), rows("w_in", C_GBB + (2 * p + q) * P), P)
                else:
                    fetch(merge_conv_unit(p, q), rows("w_b_out", 2 * P * p, 2 * P, nk=4), 2 * P)
            for m in range(KC):
                fetch(FIRST["gate_a"] + m, rows("w_in", C_GA + m * P), P)
            for p in range(4):
                fetch(FIRST["attn_out"] + p, rows("w_a_out", 2 * P * p, 2 * P, nk=4), 2 * P)
            for m in range(KC):
                fetch(FIRST["mix_out"] + m, rows("w_out", m * P), P)
            for m in range(KC):
                fetch(FIRST["mem_k"] + m, rows("xattn_w_kv", m * P), P)
            for n in range(8):
                fetch(FIRST["mem_v"] + n, rows("xattn_w_kv", D + n // 4 * T, T, k0=2 * (n % 4), nk=2), T)
            for m in range(KC):
                fetch(FIRST["x_q"] + m, rows("xattn_w_q", m * P), P)
            for m in range(KC):
                fetch(FIRST["x_out"] + m, rows("xattn_w_o", m * P), P)
            feed_forward("ffn2")
            u = FIRST["grouped"]
            for c in range(4):
                fetch(u + c, rows("w_in_2", Z_QB + c * P), P)
            for kv in range(2):
                fetch_twin(u + 4 + kv, "w_in_2", Z_KB + kv * HD)
            fetch(u + 6, rows("w_in_2", Z_VB), P)
            def fetch_gate(g):
                fetch(gate_unit(g), rows("w_in_2", (Z_GA, Z_GB)[g % 2] + g // 2 * P), P)

            for g in range(8):
                fetch_gate(g)
            u = FIRST["latent"]
            for c in range(2):
                fetch(u + c, rows("w_in_2", Z_QL + c * P), P)
            fetch(u + 2, rows("w_in_2", Z_KVL), P)
            fetch(u + 3, rows("w_in_2", Z_KPE - NOPE), P)
            for g in (8, 9):
                fetch_gate(g)
            for c in range(4):
                u = FIRST["latent_heads"] + HEAD_UNITS[c]
                load(u, rows("w_qb_2", 2 * c * QW, 2 * QW, nk=2), 2 * QW).then_inc(raw_in[u % RING], 16)
                sp.dma_start(raw[:, u % RING, 4 * QW:4 * QW + 2 * P],
                             dram["w_kvb_2"][0][:, 2 * c * P:2 * (c + 1) * P]).then_inc(raw_in[u % RING], 16)
                fetch_gate(PAIR_GATE[c])
                if c in PAIR_GATE_2:
                    fetch_gate(PAIR_GATE_2[c])
            for p in range(4):
                u = FIRST["merge"] + 2 * p
                fetch(u, rows("w_oa_2", 2 * P * p, 2 * P, nk=4), 2 * P)
                fetch(u + 1, rows("w_ob_2", 2 * P * p, 2 * P, nk=4), 2 * P)
            for m in range(KC):
                fetch(FIRST["out"] + m, rows("w_o_2", m * P), P)
            for half in "ab":
                j0 = FF2_HALF * "ab".index(half)
                loop(FIRST["mlp_up_" + half], FF2_HALF // RING,
                     lambda i, q: rows_at("w_up_2", i * (4 * P) + (j0 + q) * P))
                loop(FIRST["mlp_down_" + half], KC // 2,
                     lambda i, q: rows_at("w_down_2", i * (2 * P) + q // 2 * P, k0=j0 + q % 2 * KC))
            for n in range(2):
                fetch(FIRST["ple"] + n, rows("w_ple_2", n * T, T, nk=2), T)
            for m in range(KC):
                fetch(FIRST["ple_gate"] + m, rows("w_ple_gate_2", m * P), P)
            for n, b in enumerate(range(0, TB, 2)):
                sp.wait_ge(end_scaled, n + 1)
                sp.dma_start(out[0, b * P:(b + 1) * P, :], out_rows[:, b, :]).then_inc(out_sent, 16)
            sp.wait_ge(out_sent, 16 * TB)

        @block.gpsimd
        def _(pool):
            with pool.Fori(0, UNITS // RING) as i:
                for s in range(RING):
                    pool.wait_ge(hi_ready, 4 * i + (s + 1))
                    pool.tensor_tensor(wl[:, s, :], raw[:, s, :], wh[:, s, :].bitcast(F32),
                                       ALU.subtract).then_inc(lo_ready, 1)

        @block.tensor
        def _(pe):
            def three(to, a_hi, a_lo, b_hi, b_lo, start, stop):
                pe.matmul(to, a_hi, b_hi, start=start, stop=False, skip_group_check=True)
                pe.matmul(to, a_hi, b_lo, start=False, stop=False, skip_group_check=True)
                return pe.matmul(to, a_lo, b_hi, start=False, stop=stop, skip_group_check=True)

            def unit(u, i=None):
                pe.wait_ge(lo_ready, u + 1 if i is None else 4 * i + (u + 1))
                return wh[:, u % RING, :], wl[:, u % RING, :]

            def columns(u, to, hi, lo, ks, i=None, start=True, stop=True, width=P, at_col=0, use=True, before=None):
                w_h, w_l = unit(u, i)
                for n, k in enumerate(ks):
                    if before is not None:
                        before(k)
                    c = n * width + at_col
                    last = three(to, w_h[:, c:c + P], w_l[:, c:c + P], hi[:, k, :], lo[:, k, :],
                                 start and n == 0, stop and n == len(ks) - 1)
                if use:
                    last.then_inc(unit_used, 1)

            def sum_squares(N, column=0):
                def add(x, first):
                    for b in range(TB):
                        last = pe.matmul(bank[SUMS][:, column + b:column + b + 1], x[:, b * P:(b + 1) * P], ones[:, 0:1],
                                         start=first and b == 0, stop=False, skip_group_check=True)
                    return last
                if N.adds:
                    pe.wait_ge(norm.added, N.add0 + N.adds)
                    last = add(square_sum, True)
                if N.adds < N.chunks:
                    pe.wait_ge(norm.squares, N.chunk0 + N.chunks)
                    last = add(squares[:, (N.chunk0 + N.chunks - 1) % 2, :], N.adds == 0)
                last.then_inc(norm.summed, 1)

            def spread(N, to=SPREAD):
                pe.wait_ge(norm.newton, N.newton0 + NEWTON_COUNT)
                for b in range(TB):
                    last = pe.matmul(bank[to][:, b * P:(b + 1) * P], n_y[:, b:b + 1].to_broadcast([P, P]), ident,
                                     start=True, stop=True)
                last.then_inc(norm.spread, 1)

            def entering(X):
                return lambda k: pe.wait_ge(X.lo, X.first + k + 1)

            def entry(X, N, u):
                weights = []

                def product(q, k):
                    if k == 0:
                        weights.append(unit(u + q))
                    c = slice(k * P, (k + 1) * P)
                    return three(bank[q][:], weights[q][0][:, c], weights[q][1][:, c], xh[:, k, :], xl[:, k, :],
                                 k == 0, k == KC - 1)
                for k in range(KC - 2):
                    pe.wait_ge(X.lo, X.first + k + 1)
                    for q in range(RING):
                        product(q, k)
                for q in range(RING):
                    if q == RING - 1:
                        spread(N)
                    for k in range(KC - 2, KC):
                        if q == 0:
                            pe.wait_ge(X.lo, X.first + k + 1)
                        last = product(q, k)
                    last.then_inc(unit_used, 1)
                    if q == 0:
                        sum_squares(N)

            def rotate(R, n, x, m, to, rows=slice(0, P)):
                pe.wait_ge(R.x, n + 1)
                pe.matmul(bank[to][rows, :], m[rows, rows], x, start=True, stop=True).then_inc(R.rot, 1)

            def feed_forward(name, S, X, N, NP):
                u = FIRST[name + "_up_a"]

                def up(u, j, i):
                    for q in range(RING):
                        pe.wait_ge((ffn.gate, ffn.up)[q % 2], 2 * i + (S.hid0 + j + q // 2 - 1))
                        columns(u + q, bank[q][:], xh, xl, range(KC), i)

                entry(X, N, u)
                with pe.Fori(1, FF_A // 2) as i:
                    up(u, 0, i)
                u = FIRST[name + "_down_a"]

                def down(i, first=False):
                    for q in range(RING):
                        if q % 2 == 0 and not first:
                            pe.wait_ge(ffn.part, 2 * i + (S.out0 + q // 2 - 1))
                        columns(u + q, bank[4 + q // 2][:], hid_h, hid_l, range(q % 2 * KC, q % 2 * KC + KC), i,
                                start=q % 2 == 0, stop=q % 2 == 1,
                                before=(lambda k: pe.wait_ge(ffn.hid.lo, S.hid0 + k + 1)) if first and q < 2 else None)
                down(None, first=True)
                with pe.Fori(1, KC // 2) as i:
                    down(i)
                with pe.Fori(0, FF_B // 2) as i:
                    up(FIRST[name + "_up_b"], FF_A, i)
                u = FIRST[name + "_down_b"]
                for m in range(KC):
                    if m == 0:
                        pe.wait_ge(ffn.part, S.out0 + KC)
                    elif m >= 2:
                        pe.wait_ge(ffn.full, S.out0 + m - 1)
                    columns(u + m, bank[4 + m % 2][:], hid_h, hid_l, range(FF_B),
                            before=(lambda k: pe.wait_ge(ffn.hid.lo, S.hid0 + FF_A + k + 1)) if m == 0 else None)
                sum_squares(NP)
                spread(NP)

            def attention(A, blocks, logits, blocks_of_keys, values, exp_reads_psum=True, lead=None):
                lo, hi = blocks
                for n in range(lo, hi + 6):
                    r = A.block0 + n
                    if lead is not None:
                        lead(n)
                    if n < hi:
                        if n >= lo + 3:
                            pe.wait_ge(att.exp if exp_reads_psum else att.top, r - 2)
                        logits(n, bank[n % 3]).then_inc(att.logits, 1)
                    m, r = n - 3, A.block0 + n - 3
                    if lo <= m < hi:
                        pe.wait_ge(att.probs, r + 1)
                        if m >= lo + 2:
                            pe.wait_ge(att.pt.lo, r - 1)
                        for s in range(blocks_of_keys(m)):
                            last = pe.transpose(bank[3 + m % 2][:, s * P:(s + 1) * P],
                                                probs[:, r % 3, s * P:(s + 1) * P], ident)
                        last.then_inc(att.turned, 1)
                    if (n - 6) % 2 == 0 and lo <= n - 6 < hi:
                        g = (n - 6) // 2
                        pe.wait_ge(att.pt.lo, A.block0 + 2 * g + 2)
                        values(g).then_inc(att.pv, 1)

            def paired_values(A, g, key_blocks, v_of, p_h, p_l, first_pair=0):
                head, half = g // 2, g % 2
                par, pair = head % 2, head // 2
                if par == 0 and pair > first_pair:
                    pe.wait_ge(att.out.lo, A.piece0 + 2 * (pair - 1) + half + 1)
                slot = (A.half0 + g) % 2
                n_s = key_blocks(2 * g + 1)
                for s in range(n_s):
                    c = max(0, (s - 2 * half) * P) if n_s != TB or key_blocks(2 * g) != TB else 0
                    v_h, v_l = v_of(head, s)
                    last = three(bank[5 + half][:, c:256], v_h[:, par * HD:par * HD + P], v_l[:, par * HD:par * HD + P],
                                 p_h[:, slot, s, c:256], p_l[:, slot, s, c:256],
                                 par == 0 and s == 0, par == 1 and s == n_s - 1)
                return last

            pe.wait_ge(const_in, 16)
            pe.transpose(bank[7][:, 0:P], ident, ident).then_inc(unit_used, 1)
            for x_part in x_in:
                pe.wait_ge(x_part, 16 * TB // 2)
            for k in range(KC):
                for b in range(TB):
                    last = pe.transpose(bank[k][:, b * P:(b + 1) * P], x_rows[:, b, k * P:(k + 1) * P], ident)
                last.then_inc(x_turned, 1)
            pe.wait_ge(x_kept, RING)

            feed_forward("ffn1", ffn1, x_ffn1, n_ffn1, n_ffn1p)

            def roped(r):
                if r > 4:
                    pe.wait_ge(rope.x, r - 3)
                u = FIRST["index"] + r if r < 5 else FIRST["queries"] + r - 5
                columns(u, bank[7 if r == 4 else r % 4][:], xh, xl, range(KC))

            def turn(r):
                if r >= 2:
                    pe.wait_ge(rope.sin, r - 1)
                rotate(rope, r, wa[:, r % 2, :], rot32, 4 + r % 2)

            def conv(n):
                j, q = n // 3, n % 3
                if q == 0 and j == 0:
                    pe.wait_ge(v_split.lo, 2)
                elif q == 0 and j >= 2:
                    pe.wait_ge(conv_step, 7 * (j - 2) + 3)
                columns(FIRST["conv"] + n, bank[CONV_BANKS[j % 2][q]][:], xh, xl, range(KC))

            entry(x_mix, n_mix, FIRST["index"])
            roped(4)
            turn(0)
            turn(1)
            width = HD + HEADS
            w_h, w_l = unit(FIRST["values"])
            pe.wait_ge(norm.scale, n_mix.scale0 + 1)
            for k in range(KC):
                w = slice(k * P, k * P + width)
                last = three(bank[6][0:width, :], w_h[:, w], w_l[:, w], xh[:, k, :], xl[:, k, :], k == 0, k == KC - 1)
            last.then_inc(unit_used, 1)
            turn(2)
            roped(5)
            pe.wait_ge(v_scaled, 1)
            for b in range(TB):
                last = pe.transpose(bank[6][:, b * width:(b + 1) * width], v_cols[0:width, b * P:(b + 1) * P],
                                    ident[0:width, 0:width])
            last.then_inc(v_turned, 1)
            for r in range(3, 8):
                turn(r)
                if r < 7:
                    roped(r + 3)
            conv(0)
            turn(8)
            turn(9)
            def conv_piece(n):
                q, k = 1 + n // KC, n % KC
                if k == 0:
                    pe.wait_ge(rope.sin, 8 + q)
                columns(FIRST["conv"] + q, bank[CONV_BANKS[0][q]][:], xh, xl, [k], at_col=k * P,
                        start=k == 0, stop=k == KC - 1, use=k == KC - 1)

            idx_bank = (0, 2, 3, 7)
            pe.wait_ge(rope.out.lo, 5)
            for n in range(3 * HEADS):
                b, head = n // HEADS + 1, n % HEADS
                if n >= 4:
                    pe.wait_ge(idx_relu, n - 3)
                half = slice(head % 2 * HD, head % 2 * HD + HD)
                q = slice(b * P, (b + 1) * P)
                three(bank[idx_bank[n % 4]][:, 0:(b + 1) * P], qi_h[half, head // 2, q], qi_l[half, head // 2, q],
                      ki_h[half, 0:(b + 1) * P], ki_l[half, 0:(b + 1) * P], True, True).then_inc(idx_raw, 1)
                if n < 2 * KC:
                    conv_piece(n)

            pe.wait_ge(idx_relu, 3 * HEADS)
            for n in range(3, 12):
                conv(n)
            for p, q in MERGE_CONV:
                u, b0 = merge_conv_unit(p, q), 4 * ((p + 1) % 2)
                if q == 0 and p <= 1:
                    pe.wait_ge(conv_step, 7 * (p + 2) + 3)
                elif q == 0:
                    pe.wait_ge(mc_sum, 2 * p - 2)
                if q < 2:
                    columns(u, bank[b0 + 2 + q][:], xh, xl, range(KC))
                    continue
                if p == 0:
                    pe.wait_ge(conv_out.lo, 4)
                for m in range(2):
                    columns(u, bank[b0 + m][:], cz_h, cz_l, range(4), width=2 * P, at_col=m * P, use=m == 1)

            def main_logits(n, to):
                head, b = n // TB, n % TB
                half = slice(head % 2 * HD, head % 2 * HD + HD)
                q = slice(b * P, (b + 1) * P)
                return three(to[:, 0:(b + 1) * P], qa_h[half, head // 2, q], qa_l[half, head // 2, q],
                             ka_h[half, 0:(b + 1) * P], ka_l[half, 0:(b + 1) * P], True, True)

            def main_gate(n):
                if n < HB and n % TB < 3:
                    m, ks = n // TB, ((0, 1, 2), (3, 4, 5), (6, 7))[n % TB]
                    if n % TB == 0 and m:
                        pe.wait_ge(ga_scaled, m)
                    columns(FIRST["gate_a"] + m, bank[7][:], xh, xl, ks, at_col=ks[0] * P,
                            start=ks[0] == 0, stop=ks[-1] == KC - 1, use=ks[-1] == KC - 1)

            pe.wait_ge(mc_sum, KC)
            pe.wait_ge(rope.out.lo, 10)
            pe.wait_ge(v_split.lo, 2)
            attention(a_main, (0, HB), main_logits, lambda n: n % TB + 1,
                      lambda g: paired_values(a_main, g, lambda n: n % TB + 1,
                                              lambda head, s: (va_h[:, s, :], va_l[:, s, :]), a_pt_h, a_pt_l),
                      exp_reads_psum=False, lead=main_gate)
            pe.wait_ge(att.out.lo, a_main.piece0 + HEADS)
            for p in range(4):
                for q in range(2):
                    if p == 3 and q == 0:
                        pe.wait_ge(ga_scaled, KC)
                    columns(FIRST["attn_out"] + p, bank[2 * p + q][:], qa_h, qa_l, range(4), width=2 * P, at_col=q * P,
                            use=q == 1)

            pe.wait_ge(mem_normed, MB)
            for c in range(4):
                pe.wait_ge(ma_term, c + 1)
                for k in (2 * c, 2 * c + 1):
                    for b in range(MB):
                        last = pe.transpose(bank[c][:, (k % 2) * N_MEM + b * P:(k % 2) * N_MEM + (b + 1) * P],
                                            mem_rows[:, b, k * P:(k + 1) * P], ident)
                last.then_inc(mem_turned, 1)

            def out_projection(u, full0, hi, lo, ready):
                for m in range(KC):
                    if m >= 2:
                        pe.wait_ge(out_full, full0 + m - 1)
                    columns(u + m, bank[4 + m % 2][:], hi, lo, range(KC), before=ready if m == 0 else None)

            pe.wait_ge(ma_term, 6)
            out_projection(FIRST["mix_out"], 0, mm_h, mm_l, lambda k: pe.wait_ge(merged.lo, k + 1))

            pe.wait_ge(memt.lo, KC)
            for m in range(KC):
                if m >= 4:
                    pe.wait_ge(mk.lo, m - 3)
                columns(FIRST["mem_k"] + m, bank[m % 4][:, 0:N_MEM], memt_h, memt_l, range(KC))
                if m == 0:
                    pe.wait_ge(ma_term, KC)
                    sum_squares(n_mixp)
                if m == 2:
                    spread(n_mixp)
            for n in range(8):
                c, q = n // 4, n % 4
                if n == 0:
                    pe.wait_ge(out_full, KC)
                elif n == 4:
                    pe.wait_ge(mk.lo, KC)
                w_h, w_l = unit(FIRST["mem_v"] + n)
                for kk in range(2):
                    k = 2 * q + kk
                    for b in range(MB):
                        last = three(bank[(4, 0)[c] + b][:], memt_h[:, k, b * P:(b + 1) * P], memt_l[:, k, b * P:(b + 1) * P],
                                     w_h[:, kk * T:(kk + 1) * T], w_l[:, kk * T:(kk + 1) * T], k == 0, k == KC - 1)
                last.then_inc(unit_used, 1)
            for m in range(4):
                if m == 2:
                    pe.wait_ge(mv.lo, 2 * MB)
                columns(FIRST["x_q"] + m, bank[(2 + m) % 4][:], xh, xl, range(KC),
                        before=entering(x_x) if m == 0 else None)
                if m == 0:
                    sum_squares(n_xq)
                if m == 1:
                    spread(n_xq)

            def mem_logits(n, to):
                head, b = n // TB, n % TB
                q = slice(b * P, (b + 1) * P)
                if b == 0:
                    pe.wait_ge(xq.lo, 2 * head + 2)
                for k in (2 * head, 2 * head + 1):
                    last = three(to[:, 0:N_MEM], xq_h[:, k, q], xq_l[:, k, q], mk_h[:, k, :], mk_l[:, k, :],
                                 k % 2 == 0, k % 2 == 1)
                return last

            def mem_values(g):
                head, slot = g // 2, (a_mem.half0 + g) % 2
                if g >= 1:
                    pe.wait_ge(att.out.lo, a_mem.piece0 + 2 * g)
                for c in range(2):
                    f0 = head * XD + c * P
                    for s in range(MB):
                        last = three(bank[5 + c][:, 0:256], mv_h[:, s, f0:f0 + P], mv_l[:, s, f0:f0 + P],
                                     x_pt_h[:, slot, s, :], x_pt_l[:, slot, s, :], s == 0, s == MB - 1)
                return last

            def late_queries(n):
                if n in LATE_QUERIES:
                    m = 4 + LATE_QUERIES.index(n)
                    if m > 4:
                        pe.wait_ge(xq_scaled, m)
                    columns(FIRST["x_q"] + m, bank[7][:], xh, xl, range(KC))

            pe.wait_ge(xq_scaled, 4)
            attention(a_mem, (0, XH * TB), mem_logits, lambda n: MB, mem_values, lead=late_queries)
            pe.wait_ge(att.out.lo, a_mem.piece0 + 4 * XH)
            out_projection(FIRST["x_out"], KC, xq_h, xq_l, None)
            sum_squares(n_xp)
            spread(n_xp)

            feed_forward("ffn2", ffn2, x_ffn2, n_ffn2, n_ffn2p)

            def turn_grouped(n):
                if n >= 2:
                    pe.wait_ge(gx.sin, n - 1)
                pe.wait_ge(gx_normed, n + 1)
                pe.matmul(bank[n % 2][:], rot16, g_x[:, GROUPED_ORDER[n], :], start=True, stop=True).then_inc(gx.rot, 1)

            def gate(g, to, banks=1):
                if g >= banks:
                    pe.wait_ge(gate_scaled, g - banks + 1)
                columns(gate_unit(g), bank[to][:], xh, xl, range(KC))

            def gate_piece(g, n):
                ks = {3: (0, 1, 2), 4: (3, 4, 5), 5: (6, 7)}.get(n, ())
                if ks:
                    if n == 3:
                        pe.wait_ge(gate_scaled, g)
                    columns(gate_unit(g), bank[7][:], xh, xl, ks, at_col=ks[0] * P,
                            start=ks[0] == 0, stop=ks[-1] == KC - 1, use=ks[-1] == KC - 1)

            def head_squares(r):
                c = n_heads.chunk0 + r
                pe.wait_ge(norm.squares, c + 1)
                for b in range(TB):
                    to = bank[SUMS][:, 12 * b + 2 * r:12 * b + 2 * r + 2]
                    last = pe.matmul(to, squares[:, c % 2, b * P:(b + 1) * P], head_sel[:, 0:2],
                                     start=r == 0 and b == 0, stop=False, skip_group_check=True)
                last.then_inc(norm.summed, 1)

            entry(x_mix2, n_mix2, FIRST["grouped"])
            for r in (4, 5):
                pe.wait_ge(gx.x, r - 3)
                columns(FIRST["grouped"] + r, bank[r % 4][:], xh, xl, range(KC))
                head_squares(2 * r - 8)
                head_squares(2 * r - 7)
            pe.wait_ge(norm.scale, n_mix2.scale0 + 1)
            columns(FIRST["grouped"] + 6, bank[6][:], xh, xl, range(KC))
            head_squares(4)
            head_squares(5)
            pe.wait_ge(gx.x, 4)
            gate(0, 2)
            pe.wait_ge(gv_scaled, 1)
            for b in range(TB):
                last = pe.transpose(bank[6][:, b * P:(b + 1) * P], g_v[:, b * P:(b + 1) * P], ident)
            last.then_inc(gv_turned, 1)
            for n in range(6):
                if n >= 2:
                    pe.wait_ge(gx_normed, n - 1)
                pe.wait_ge(heads_laid, n + 1)
                for b in range(TB):
                    last = pe.matmul(bank[4 + n % 2][:, b * P:(b + 1) * P], expand[:, b, :], ident, start=True, stop=True)
                last.then_inc(norm.spread, 1)
                if n + 1 < 6:
                    gate(n + 1, 3 - n % 2, 2)
                if n >= 1:
                    turn_grouped(n - 1)
            turn_grouped(5)
            pe.wait_ge(gate_scaled, 6)

            def grp_logits(n, to):
                head, b = n // TB, n % TB
                half = slice(head % 2 * HD, head % 2 * HD + HD)
                q, kv = slice(b * P, (b + 1) * P), head // 4
                return three(to[:], gq_h[half, head // 2, q], gq_l[half, head // 2, q],
                             gk_h[half, kv, :], gk_l[half, kv, :], True, True)

            gate(6, 7)
            pe.wait_ge(gx.out.lo, 6)
            pe.wait_ge(gv.lo, 4)
            attention(a_grp, (0, HB), grp_logits, lambda n: TB,
                      lambda g: paired_values(a_grp, g, lambda n: TB,
                                              lambda head, s: (gv_h[:, head // 4, s, :], gv_l[:, head // 4, s, :]),
                                              g_pt_h, g_pt_l),
                      lead=lambda n: gate_piece(7, n))

            u = FIRST["latent"]
            pe.wait_ge(att.exp, a_grp.block0 + HB)
            for r in range(4):
                if r == 3:
                    pe.wait_ge(att.pt.lo, a_grp.block0 + HB)
                columns(u + r, bank[r][:], xh, xl, range(KC))
            pe.wait_ge(gate_scaled, 8)
            sum_squares(n_cq)
            pe.wait_ge(kpe.x, 1)
            gate(8, 2)
            spread(n_cq)
            sum_squares(n_ckv, 8)
            rotate(kpe, 0, l_x[:, 3, :], rot16, 4)
            pe.wait_ge(att.out.lo, a_grp.piece0 + HEADS)
            spread(n_ckv, 5)
            gate(9, 3, 2)

            kv0 = 4 * QW

            def lat_key(c, q, w_h, w_l):
                w = slice(kv0 + q * P, kv0 + (q + 1) * P)
                return three(bank[2 + q][:], w_h[:, w], w_l[:, w], ck_h[:], ck_l[:], True, True)

            def lat_queries(c):
                w_h, w_l = unit(FIRST["latent_heads"] + HEAD_UNITS[c])
                if c >= 1:
                    pe.wait_ge(att.exp, a_lat.block0 + 2 * TB * c)
                else:
                    pe.wait_ge(gate_scaled, 9)
                for q in range(2):
                    for k in range(2):
                        w = slice(k * 2 * QW + q * QW, k * 2 * QW + (q + 1) * QW)
                        three(bank[q][0:QW, :], w_h[:, w], w_l[:, w], cq_h[:, k, :], cq_l[:, k, :], k == 0, k == 1)
                lat_key(c, 0, w_h, w_l).then_inc(lat_raw, 1)

            def lat_turns(c):
                for q in range(2):
                    rotate(lq, 2 * c + q, l_q[0:QW, q, :], rot16, q, slice(0, QW))

            def lat_values(c):
                w_h, w_l = unit(FIRST["latent_heads"] + HEAD_UNITS[c])
                if c >= 1:
                    pe.wait_ge(att.pt.lo, a_lat.block0 + 2 * TB * c)
                else:
                    pe.wait_ge(gate_scaled, 10)
                lat_key(c, 1, w_h, w_l)
                if c >= 1:
                    pe.wait_ge(att.out.lo, a_lat.piece0 + 2 * c)
                v_h, v_l = (w[:, kv0:kv0 + 2 * P].rearrange("p (h c) -> p h c", c=P)[:, :, NOPE:P] for w in (w_h, w_l))
                for b in range(TB):
                    last = three(bank[6][:, b * P:(b + 1) * P].rearrange("p (h c) -> p h c", c=HD),
                                 ck_h[:, b * P:(b + 1) * P], ck_l[:, b * P:(b + 1) * P], v_h, v_l, True, True)
                last.then_inc(unit_used, 1)
                if c == 0:
                    lat_turns(0)
                gate(PAIR_GATE[c], 7)

            def lat_lead(c, n):
                if c in PAIR_GATE_2:
                    gate_piece(PAIR_GATE_2[c], n)
                if n == 2 * TB + 1 and c < 3:
                    lat_queries(c + 1)
                if n == 2 * TB + 4 and c < 3:
                    lat_turns(c + 1)

            def lat_logits(n, to):
                head, b = n // TB, n % TB
                q = slice(b * P, (b + 1) * P)
                return three(to[:], lq_h[0:QW, head % 2, q], lq_l[0:QW, head % 2, q],
                             lk_h[0:QW, head % 2, :], lk_l[0:QW, head % 2, :], True, True)

            pe.wait_ge(l_lat.lo, 3)
            lat_queries(0)
            for c in range(4):
                lat_values(c)
                pe.wait_ge(lq.out.lo, 2 * c + 2)
                pe.wait_ge(lk.lo, 2 * c + 2)
                if c == 0:
                    pe.wait_ge(kpe.out.lo, 2)
                pe.wait_ge(lv.lo, 2 * c + 2)
                attention(a_lat, (2 * TB * c, 2 * TB * (c + 1)), lat_logits, lambda n: TB,
                          lambda g: paired_values(a_lat, g, lambda n: TB,
                                                  lambda head, s: (lv_h[:, s, :], lv_l[:, s, :]), l_pt_h, l_pt_l,
                                                  first_pair=c),
                          lead=lambda n: lat_lead(c, n - 2 * TB * c))

            pe.wait_ge(att.out.lo, a_lat.piece0 + HEADS)
            for p in range(4):
                u, b0 = FIRST["merge"] + 2 * p, 4 * (p % 2)
                if p >= 2:
                    pe.wait_ge(me_term, 4 * (p - 1))
                for branch, (o_h, o_l) in enumerate(((lo_h, lo_l), (go_h, go_l))):
                    for q in range(2):
                        columns(u + branch, bank[b0 + 2 * branch + q][:], o_h, o_l, range(4), width=2 * P, at_col=q * P,
                                use=q == 1)
            u = FIRST["out"]
            for m in range(KC):
                if m >= 3:
                    pe.wait_ge(h_out, m - 2)
                elif m == 0:
                    pe.wait_ge(me_term, 3 * KC // 2)
                columns(u + m, bank[1 + m % 3][:], mg_h, mg_l, range(KC),
                        before=(lambda k: pe.wait_ge(merged.lo, KC + k + 1)) if m == 0 else None)

            pe.wait_ge(p_in, 16)
            pe.wait_ge(me_sum, KC)
            for k in range(2):
                for b in range(TB):
                    last = pe.transpose(bank[4 + k][:, b * P:(b + 1) * P], p_rows[:, b, k * P:(k + 1) * P], ident)
                last.then_inc(p_turned, 1)

            def mlp_up(first, j0, i, opening=False):
                for q in range(RING):
                    if not opening:
                        pe.wait_ge(ml_x, 4 * i + (j0 + q - 3))
                    columns(first + q, bank[q][:], xh, xl, range(KC), i,
                            before=entering(x_mlp) if opening and q == 0 else None)
                    if opening and q == 0:
                        sum_squares(n_mlp)
                    if opening and q == 1:
                        spread(n_mlp)

            def mlp_down(first, kept, k0, i, opening=False):
                for q in range(RING):
                    m = q // 2
                    if q % 2 == 0 and not opening:
                        pe.wait_ge(kept, 2 * i + (m - 1))
                    columns(first + q, bank[4 + m][:], hid_h, hid_l, range(q % 2 * KC, q % 2 * KC + KC), i,
                            start=q % 2 == 0, stop=q % 2 == 1,
                            before=(lambda k: pe.wait_ge(ml_hid.lo, k0 + k + 1)) if opening and m == 0 else None)

            mlp_up(FIRST["mlp_up_a"], 0, None, opening=True)
            with pe.Fori(1, FF2_HALF // RING) as i:
                mlp_up(FIRST["mlp_up_a"], 0, i)
            pe.wait_ge(p_split.lo, 2)
            mlp_down(FIRST["mlp_down_a"], ml_part, 0, None, opening=True)
            with pe.Fori(1, KC // 2) as i:
                mlp_down(FIRST["mlp_down_a"], ml_part, 0, i)
            with pe.Fori(0, FF2_HALF // RING) as i:
                mlp_up(FIRST["mlp_up_b"], FF2_HALF, i)
            pe.wait_ge(ml_part, KC)
            mlp_down(FIRST["mlp_down_b"], h_mlp, FF2_HALF, None, opening=True)
            with pe.Fori(1, KC // 2) as i:
                mlp_down(FIRST["mlp_down_b"], h_mlp, FF2_HALF, i)

            for n in range(2):
                w_h, w_l = unit(FIRST["ple"] + n)
                for m in range(4):
                    if n == 1 and m == 0:
                        pe.wait_ge(h_mlp, KC)
                    if n == 1 and m == 2:
                        pe.wait_ge(ple_kept, 2)
                    if n == 0 and m == 0:
                        pe.wait_ge(ml_x, FF2)
                    to = bank[m if n == 0 else (4, 5, 0, 1)[m]]
                    for k in range(2):
                        w = slice(k * T + m * P, k * T + (m + 1) * P)
                        last = three(to[:], w_h[:, w], w_l[:, w], pt_h[:, k, :], pt_l[:, k, :], k == 0, k == 1)
                last.then_inc(unit_used, 1)
                if n == 0:
                    sum_squares(n_ple)
                else:
                    spread(n_ple)
            def turn_end(k):
                pe.wait_ge(end_gained, k + 1)
                if k >= 4:
                    pe.wait_ge(end_kept, k - 3)
                for b in range(TB):
                    last = pe.transpose(bank[END_BANKS[k % 4]][:, b * P:(b + 1) * P], gained[:, k, b * P:(b + 1) * P], ident)
                last.then_inc(end_turned, 1)

            for m in range(KC):
                if m == 0:
                    pe.wait_ge(ple_kept, 4)
                elif m >= 2:
                    pe.wait_ge(pg_x, m - 1)
                columns(FIRST["ple_gate"] + m, bank[2 + m % 2][:], xh, xl, range(KC),
                        before=entering(x_ple) if m == 0 else None)
                if m == 2:
                    pe.wait_ge(ple_kept, KC)
                if m >= 2:
                    turn_end(m - 2)
            turn_end(KC - 2)
            turn_end(KC - 1)
            sum_squares(n_end)

        @block.scalar
        def _(act):
            def hi(u, i=None):
                if u >= UNITS:
                    return
                s = u % RING
                act.wait_ge(raw_in[s], landed(u) if i is None else 16 * i + landed(u))
                if i is not None:
                    act.wait_ge(unit_used, 4 * i + done(u - RING))
                elif u >= RING:
                    act.wait_ge(unit_used, done(u - RING))
                act.activation(wh[:, s, :], raw[:, s, :], ACT.Copy).then_inc(hi_ready, 1)

            def ahead(u, i=None):
                hi(u + LOOKAHEAD, i)

            def square(N, k, src, free=False):
                r, user = N.chunk0 + k, N.slot_user(k)
                if user is not None and not free:
                    act.wait_ge(norm.summed if user[0] == "summed" else norm.added, user[1])
                act.activation(squares[:, r % 2, :], src, ACT.Square).then_inc(norm.squares, 1)

            def scaled(X, name, k):
                act.activation(xh[:, k, :], h[:, k, :], ACT.Copy, scale=gain(name, k)).then_inc(X.hi, 1)

            def keep_scale(N):
                act.wait_ge(norm.spread, N.spread0 + 1)
                act.activation(scale[:], bank[SPREAD][:], ACT.Copy).then_inc(norm.scale, 1)

            def enter(X, N, name, updated, first):
                for k in range(KC):
                    act.wait_ge(updated, first + k + 1)
                    scaled(X, name, k)
                    square(N, k, h[:, k, :])

            def feed_forward(name, S, X, N, NP, updated, first):
                u = FIRST[name + "_up_a"]

                def pair(u, j, i, n, opening=False):
                    c = n % 2
                    ahead(u, i)
                    if opening:
                        enter(X, N, name + "_pre_g", updated, first)
                    ahead(u + 1, i)
                    if opening:
                        keep_scale(N)
                    act.wait_ge(ffn.gate, S.hid0 + j + 1 if i is None else 2 * i + (S.hid0 + j + 1))
                    act.activation(wa[:, c, :], wa[:, c, :], ACT.Silu).then_inc(ffn.silu, 1)
                    act.wait_ge(ffn.prod, S.hid0 + j + 1 if i is None else 2 * i + (S.hid0 + j + 1))
                    dst = hid_h[:, n, :] if i is None else hid_h[:, 2 * i + n, :]
                    act.activation(dst, wb[:, c, :], ACT.Copy).then_inc(ffn.hid.hi, 1)

                pair(u, 0, None, 0, opening=True)
                pair(u + 2, 1, None, 1)
                with act.Fori(1, FF_A // 2) as i:
                    for c in range(2):
                        pair(u + 2 * c, c, i, c)
                u = FIRST[name + "_down_a"]
                with act.Fori(0, KC // 2) as i:
                    for q in range(RING):
                        ahead(u + q, i)
                u = FIRST[name + "_up_b"]
                with act.Fori(0, FF_B // 2) as i:
                    for c in range(2):
                        pair(u + 2 * c, FF_A + c, i, c)
                u = FIRST[name + "_down_b"]
                for m in range(KC):
                    ahead(u + m)
                    act.wait_ge(ffn.full, S.out0 + m + 1)
                    square(NP, m, f[:, m, :])

            def attention(A, blocks, source, exp_scale, blocks_of_keys, p_h, outputs, lead=None):
                lo, hi_ = blocks
                for n in range(lo, hi_ + 6):
                    r = A.block0 + n
                    if lead is not None:
                        lead(n)
                    if n < hi_:
                        act.wait_ge(att.top, r + 1)
                        if r >= 3:
                            act.wait_ge(att.turned, r - 2)
                        src = source(n)
                        act.activation(probs[:, r % 3, 0:src.shape[1]], src, ACT.Exp, bias=top[:, r % 4:r % 4 + 1],
                                       scale=exp_scale, accum_out=sums[:, r % 4:r % 4 + 1]).then_inc(att.exp, 1)
                    m, r = n - 1, A.block0 + n - 1
                    if lo <= m < hi_:
                        act.wait_ge(att.inv, r + 1)
                        p = probs[:, r % 3, 0:blocks_of_keys(m) * P]
                        act.activation(p, p, ACT.Copy, scale=invs[:, r % 4:r % 4 + 1]).then_inc(att.probs, 1)
                    m, r = n - 3, A.block0 + n - 3
                    if lo <= m < hi_:
                        g = A.half0 + m // 2
                        act.wait_ge(att.turned, r + 1)
                        if g >= 2:
                            act.wait_ge(att.pv, g - 1)
                        w = blocks_of_keys(m)
                        act.activation(p_h[:, g % 2, 0:w, m % 2 * P:(m % 2 + 1) * P],
                                       bank[3 + m % 2][:, 0:w * P].rearrange("p (s q) -> p s q", q=P),
                                       ACT.Copy).then_inc(att.pt.hi, 1)
                    if (n - 7) % 2 == 0 and lo <= n - 7 < hi_:
                        output(A, (n - 7) // 2, outputs)

            def output(A, g, outputs):
                for dst, src in outputs(g):
                    act.wait_ge(att.pv, A.half0 + g + 1)
                    act.activation(dst, src, ACT.Copy).then_inc(att.out.hi, 1)

            def paired(o_h):
                def outputs(g):
                    head, half = g // 2, g % 2
                    if head % 2 == 0:
                        return []
                    return [(o_h[:, head // 2, half * 256:(half + 1) * 256], bank[5 + half][:, 0:256])]
                return outputs

            act.dma_start(mats[:], dram["shape_mats"].rearrange("p (n c) -> p n c", c=P)).then_inc(const_in, 16)
            for b in range(TB // 2):
                act.dma_start(x_rows[:, b, :], dram["x"][0, b * P:(b + 1) * P, :]).then_inc(x_in[0], 16)
            act.dma_start(gains[:], dram["gain_columns"]).then_inc(gains_in, 16)
            tabs = dram["shape_tabs"].rearrange("p (n c t) -> p n c t", n=3, c=2)
            act.dma_start(tab[:], tabs[:, 0]).then_inc(tab_in, 16)
            for u in range(LOOKAHEAD):
                hi(u)
            act.wait_ge(gains_in, 16)
            feed_forward("ffn1", ffn1, x_ffn1, n_ffn1, n_ffn1p, x_kept, 0)

            def rope_hi(r):
                dst = (qi_h[:, r, :] if r < 4 else ki_h[:] if r == 4 else qa_h[:, r - 5, :] if r < 9 else ka_h[:])
                act.wait_ge(rope.sum, r + 1)
                act.activation(dst, wb[:, r % 2, :], ACT.Copy, scale=HD ** -0.5 if 5 <= r < 9 else 1.0).then_inc(rope.out.hi, 1)

            u = FIRST["index"]
            ahead(u)
            enter(x_mix, n_mix, "mix_pre_g", r_ffn1.h, r_ffn1.first)
            ahead(u + 1)
            keep_scale(n_mix)
            for n in (2, 3, 4, 5):
                ahead(u + n)
            rope_hi(0)
            rope_hi(1)
            ahead(u + 6)
            rope_hi(2)
            ahead(u + 7)
            act.wait_ge(v_turned, 1)
            turned = bank[6][:, 0:TB * (HD + HEADS)].rearrange("p (b c) -> p b c", c=HD + HEADS)
            for par in range(2):
                act.activation(va_h[:, :, par * P:par * P + HD], turned[:, :, 0:HD], ACT.Copy).then_inc(v_split.hi, 1)
            for r in range(3, 10):
                rope_hi(r)
                if r < 8:
                    ahead(u + r + 5)
            for n in range(3 * HEADS):
                w = (n // HEADS + 2) * P
                act.wait_ge(idx_raw, n + 1)
                if n >= 3:
                    act.wait_ge(idx_sum, IDX_SUM[n - 3])
                act.activation(probs[:, n % 3, 0:w], bank[(0, 2, 3, 7)[n % 4]][:, 0:w], ACT.Relu).then_inc(idx_relu, 1)
                if n in (KC + 2, 2 * KC + 2):
                    ahead(FIRST["conv"] + 1 + n // KC)

            u = FIRST["conv"]
            for j in range(4):
                c = j % 2
                if j >= 1:
                    ahead(u + 3 * j + 3)
                act.wait_ge(conv_step, 7 * j + 4)
                act.activation(c_z[:, c, :], c_y[:, c, 2:2 + T], ACT.Copy,
                               scale=gain_row(CONV_ROW + 8 + j)).then_inc(conv_tap, 1)
                act.wait_ge(conv_step, 7 * j + 7)
                act.activation(cz_h[:, j, :], c_z[:, c, :], ACT.Copy).then_inc(conv_out.hi, 1)
                if j < 3:
                    ahead(u + 3 * j + 4)
                    ahead(u + 3 * j + 5)
            def merge_gate(m):
                act.wait_ge(mc_gate, m + 1)
                act.activation(wa[:, m % 2, :], wa[:, m % 2, :], ACT.Sigmoid).then_inc(mc_sig, 1)

            for n in range(1, len(MERGE_CONV)):
                ahead(FIRST["merge_conv"] + n)
                for m in {3: (0, 1), 5: (2, 3), 7: (4,), 8: (5,), 10: (6,), 11: (7,)}.get(n, ()):
                    merge_gate(m)

            act.wait_ge(rope.sin, 10)
            act.dma_start(tab[:], tabs[:, 2]).then_inc(tab_in, 16)

            def main_gate(n):
                if n < HB and n % TB == TB - 1:
                    ahead(FIRST["gate_a"] + n // TB)
                if n == HB + 2:
                    act.wait_ge(unit_used, done(FIRST["gate_a"] + KC - 1))
                    act.dma_start(mem_rows[:], dram["mem"][0].rearrange("(b p) c -> p b c", p=P)).then_inc(mem_in, 16)

            attention(a_main, (0, HB), lambda n: wb[:, n % 2, 0:(n % TB + 1) * P], -1.0, lambda n: n % TB + 1, a_pt_h,
                      paired(qa_h), main_gate)
            for m in range(KC):
                act.wait_ge(ga_scaled, m + 1)
                act.activation(gate_a[:, m, :], gate_a[:, m, :], ACT.Sigmoid).then_inc(ga_sig, 1)
            act.wait_ge(mem_in, 16)
            for b in range(MB):
                if b:
                    act.wait_ge(mem_sum, b)
                act.activation(mem_squares[:], mem_rows[:, b, :], ACT.Square,
                               accum_out=mem_sq[:, b:b + 1]).then_inc(mem_sum, 1)
            for p in range(4):
                ahead(FIRST["attn_out"] + p)
                for m in (2 * p, 2 * p + 1):
                    act.wait_ge(ma_sum, m + 1)
                    act.activation(mm_h[:, m, :], mixed[:, m, :], ACT.Copy).then_inc(merged.hi, 1)
            for k in range(KC):
                act.wait_ge(mem_turned, k // 2 + 1)
                act.activation(memt_h[:, k, :], bank[k // 2][:, k % 2 * N_MEM:(k % 2 + 1) * N_MEM], ACT.Copy,
                               scale=gain("mem_g", k)).then_inc(memt.hi, 1)
            for m in range(KC):
                ahead(FIRST["mix_out"] + m)
                act.wait_ge(out_full, m + 1)
                square(n_mixp, m, f[:, m, :])

            def enter_mem(k):
                act.wait_ge(r_mix.h, r_mix.first + k + 1)
                scaled(x_x, "xattn_pre_g", k)
                square(n_xq, k, h[:, k, :])

            for m in range(KC):
                ahead(FIRST["mem_k"] + m)
                act.wait_ge(unit_used, done(FIRST["mem_k"] + m))
                act.activation(mk_h[:, m, :], bank[m % 4][:, 0:N_MEM], ACT.Copy).then_inc(mk.hi, 1)
                if m >= 3:
                    enter_mem(m - 3)
            for n in range(8):
                ahead(FIRST["mem_v"] + n)
                if n < 3:
                    enter_mem(n + 5)
                if n % 4 == 3:
                    c = n // 4
                    act.wait_ge(unit_used, done(FIRST["mem_v"] + n))
                    for b in range(MB):
                        act.activation(mv_h[:, b, c * T:(c + 1) * T], bank[(4, 0)[c] + b][:], ACT.Copy).then_inc(mv.hi, 1)
            def query_hi(m):
                act.wait_ge(xq_scaled, m + 1)
                act.activation(xq_h[:, m, :], wb[:, m % 2, :], ACT.Copy).then_inc(xq.hi, 1)

            for m in range(5):
                if m < 4:
                    ahead(FIRST["x_q"] + m)
                if m == 1:
                    keep_scale(n_xq)
                if m >= 1:
                    query_hi(m - 1)

            def late_queries(n):
                if n in LATE_QUERIES:
                    ahead(FIRST["x_q"] + 4 + LATE_QUERIES.index(n))
                if n - 1 in LATE_QUERIES:
                    query_hi(4 + LATE_QUERIES.index(n - 1))

            attention(a_mem, (0, XH * TB), lambda n: bank[n % 3][:, 0:N_MEM], 1.0, lambda n: MB, x_pt_h,
                      lambda g: [(xq_h[:, g // 2 * 2 + c, g % 2 * 256:(g % 2 + 1) * 256], bank[5 + c][:, 0:256]) for c in range(2)],
                      late_queries)
            for m in range(KC):
                ahead(FIRST["x_out"] + m)
                act.wait_ge(out_full, KC + m + 1)
                square(n_xp, m, f[:, m, :])

            feed_forward("ffn2", ffn2, x_ffn2, n_ffn2, n_ffn2p, r_x.h, r_x.first)

            for r in range(6):
                ahead(FIRST["grouped"] + r)
                if r == 0:
                    enter(x_mix2, n_mix2, "g_mix_2", r_ffn2.h, r_ffn2.first)
                elif r == 1:
                    keep_scale(n_mix2)
                else:
                    act.wait_ge(gx.x, r - 1)
                    square(n_heads, r - 2, g_x[:, r - 2, :])
            ahead(FIRST["grouped"] + 6)
            for r in (4, 5):
                act.wait_ge(gx.x, r + 1)
                square(n_heads, r, g_x[:, r, :])
            act.wait_ge(gv_turned, 1)
            turned_g = bank[6][:].rearrange("p (b c) -> p b c", c=P)
            for kv in range(2):
                for par in range(2):
                    act.activation(gv_h[:, kv, :, par * P:par * P + HD], turned_g[:, :, kv * HD:(kv + 1) * HD],
                                   ACT.Copy).then_inc(gv.hi, 1)
            def gate(g):
                act.wait_ge(gate_scaled, g + 1)
                act.dma_start(gate_store[g], gate_stage[:]).then_inc(gate_out, 16)

            for n, r in enumerate(GROUPED_ORDER):
                ahead(gate_unit(n))
                gate(n)
                act.wait_ge(gx.sum, n + 1)
                act.activation(gq_h[:, r, :] if r < 4 else gk_h[:, r - 4, :], wb[:, n % 2, :], ACT.Copy,
                               scale=HD ** -0.5 if r < 4 else 1.0).then_inc(gx.out.hi, 1)
            ahead(gate_unit(6))
            act.wait_ge(gx.sin, 6)
            act.dma_start(tab[:], tabs[:, 1]).then_inc(tab_in, 16)
            act.wait_ge(gv.lo, 4)

            def grouped_gates(n):
                if n == 2:
                    gate(6)
                if n == 3:
                    ahead(gate_unit(7))
                if n == 8:
                    gate(7)

            attention(a_grp, (0, HB), lambda n: bank[n % 3][:], 1.0, lambda n: TB, g_pt_h, paired(go_h), grouped_gates)

            act.wait_ge(gate_out, 16 * 8)
            for r in range(4):
                ahead(FIRST["latent"] + r)
                if r >= 1:
                    act.wait_ge(lx, r)
                    N, k = ((n_cq, 0), (n_cq, 1), (n_ckv, 0))[r - 1]
                    square(N, k, l_x[:, r - 1, :])
            for k in range(3):
                act.wait_ge(l_normed, k + 1)
                act.activation((cq_h[:, 0, :], cq_h[:, 1, :], ck_h[:])[k], (wb[:, 0, :], wb[:, 1, :], wa[:, 0, :])[k],
                               ACT.Copy).then_inc(l_lat.hi, 1)
            act.wait_ge(kpe.sum, 1)
            for q in range(2):
                act.activation(lk_h[NOPE:QW, q, :], wa[NOPE:QW, 1, :], ACT.Copy).then_inc(kpe.out.hi, 1)
            act.wait_ge(kpe.out.lo, 2)
            for g in (8, 9):
                ahead(gate_unit(g))
                gate(g)

            def pair_gates(c, n):
                if n == 2:
                    gate(PAIR_GATE[c])
                if c in PAIR_GATE_2 and n == 3:
                    ahead(gate_unit(PAIR_GATE_2[c]))
                if c in PAIR_GATE_2 and n == 8:
                    gate(PAIR_GATE_2[c])
                if n == 2 * TB + 3 and c < 3:
                    pair_queries(c + 1)

            def pair_key(q):
                act.activation(lk_h[0:NOPE, q, :], bank[2 + q][0:NOPE, :], ACT.Copy).then_inc(lk.hi, 1)

            def pair_queries(c):
                ahead(FIRST["latent_heads"] + HEAD_UNITS[c])
                act.wait_ge(lat_raw, c + 1)
                for q in range(2):
                    act.activation(l_q[0:QW, q, :], bank[q][0:QW, :], ACT.Copy).then_inc(lq.x, 1)
                pair_key(0)

            pair_queries(0)
            for c in range(4):
                u = FIRST["latent_heads"] + HEAD_UNITS[c]
                act.wait_ge(unit_used, done(u))
                pair_key(1)
                for q in range(2):
                    act.activation(lv_h[:, :, q * P:q * P + HD],
                                   bank[6][:].rearrange("p (s c) -> p s c", c=P)[:, :, q * HD:(q + 1) * HD],
                                   ACT.Copy).then_inc(lv.hi, 1)
                for q in range(2):
                    act.wait_ge(lq.sum, 2 * c + q + 1)
                    act.activation(lq_h[0:QW, q, :], wb[0:QW, q, :], ACT.Copy, scale=QW ** -0.5).then_inc(lq.out.hi, 1)
                ahead(u + 1)
                attention(a_lat, (2 * TB * c, 2 * TB * (c + 1)), lambda n: bank[n % 3][:], 1.0, lambda n: TB, l_pt_h,
                          paired(lo_h), lambda n: pair_gates(c, n - 2 * TB * c))

            def gates_from_dram(m):
                act.dma_start(gates_back[:, m % 4], gate_store[2 * m:2 * m + 2].rearrange("g p t -> p g t")
                              ).then_inc(gate_in[m % 4], 16)

            act.wait_ge(gate_out, 16 * 2 * KC)
            act.wait_ge(att.pv, a_lat.half0 + HB // 2)
            for m in range(4):
                gates_from_dram(m)
            for m in range(KC + 1):
                if m < KC:
                    ahead(FIRST["merge"] + m)
                    act.wait_ge(gate_in[m % 4], 16 * (m // 4 + 1))
                    act.activation(gates_back[:, m % 4], gates_back[:, m % 4], ACT.Sigmoid).then_inc(gate_sig, 1)
                if m >= 1:
                    act.wait_ge(me_sum, m)
                    act.activation(mg_h[:, m - 1, :], wa[:, (m - 1) % 2, :], ACT.Copy).then_inc(merged.hi, 1)
                    if m <= 4:
                        gates_from_dram(m + 3)
            act.wait_ge(unit_used, done(FIRST["merge"] + 7))
            act.dma_start(p_rows[:], dram["p_2"][0, 0].rearrange("(b p) c -> p b c", p=P)).then_inc(p_in, 16)
            for m in range(KC):
                ahead(FIRST["out"] + m)
                act.wait_ge(h_out, m + 1)
                scaled(x_mlp, "g_mlp_2", m)
                square(n_mlp, m, h[:, m, :])
            for k in range(2):
                act.wait_ge(p_turned, k + 1)
                act.activation(pt_h[:, k, :], bank[4 + k][:], ACT.Copy).then_inc(p_split.hi, 1)

            def mlp_chunk(j, i, n):
                act.wait_ge(ml_sq, j + 1 if i is None else 4 * i + (j + 1))
                act.activation(hid_h[:, n, :] if i is None else hid_h[:, 4 * i + n, :], wb[:, n % 2, :],
                               ACT.Copy).then_inc(ml_hid.hi, 1)

            def mlp_up(u, j0, i):
                for q in range(RING):
                    ahead(u + q, i)
                    mlp_chunk(j0 + q, i, q)

            u = FIRST["mlp_up_a"]
            ahead(u)
            ahead(u + 1)
            keep_scale(n_mlp)
            mlp_chunk(0, None, 0)
            mlp_chunk(1, None, 1)
            for q in (2, 3):
                ahead(u + q)
                mlp_chunk(q, None, q)
            with act.Fori(1, FF2_HALF // RING) as i:
                mlp_up(u, 0, i)
            with act.Fori(0, KC // 2) as i:
                for q in range(RING):
                    ahead(FIRST["mlp_down_a"] + q, i)
            with act.Fori(0, FF2_HALF // RING) as i:
                mlp_up(FIRST["mlp_up_b"], FF2_HALF, i)

            def leave_mlp(i):
                for q in range(RING):
                    ahead(FIRST["mlp_down_b"] + q, i)
                    if q % 2 == 1:
                        m = q // 2
                        if i is not None:
                            act.wait_ge(norm.added, 2 * i + (n_ple.add0 + m - 1))
                        act.wait_ge(h_mlp, m + 1 if i is None else 2 * i + (m + 1))
                        row = GAINS.index("g_ple_2") * KC + m
                        if i is None:
                            g, x, to = gains[:, row:row + 1], h[:, m, :], xh[:, m, :]
                        else:
                            g, x, to = gains[:, bass.ds(2 * i + row, 1)], h[:, 2 * i + m, :], xh[:, 2 * i + m, :]
                        act.activation(to, x, ACT.Copy, scale=g).then_inc(x_ple.hi, 1)
                        square(n_ple, m, x, free=i is not None)

            leave_mlp(None)
            with act.Fori(1, KC // 2) as i:
                leave_mlp(i)

            for n in range(2):
                ahead(FIRST["ple"] + n)
                if n == 1:
                    keep_scale(n_ple)
                act.wait_ge(unit_used, done(FIRST["ple"] + n))
                for m in range(4):
                    act.activation(ple[:, 4 * n + m, :], bank[m if n == 0 else (4, 5, 0, 1)[m]][:], ACT.Copy).then_inc(ple_kept, 1)
            for m in range(KC + 3):
                if m < KC:
                    ahead(FIRST["ple_gate"] + m)
                    act.wait_ge(pg_x, m + 1)
                    act.activation(wa[:, m % 2, :], wa[:, m % 2, :], ACT.Sigmoid).then_inc(pg_sig, 1)
                if 1 <= m <= KC:
                    act.wait_ge(h_end, m)
                    square(n_end, m - 1, h[:, m - 1, :])
                    act.activation(gained[:, m - 1, :], h[:, m - 1, :], ACT.Copy, scale=gain("g_final_2", m - 1)
                                   ).then_inc(end_gained, 1)
                if m >= 3:
                    k = m - 3
                    act.wait_ge(end_turned, k + 1)
                    act.activation(out_rows[:, :, k * P:(k + 1) * P], bank[END_BANKS[k % 4]][:].rearrange("p (b c) -> p b c", c=P),
                                   ACT.Copy).then_inc(end_kept, 1)
            act.wait_ge(end_kept, KC)
            act.wait_ge(norm.newton, n_end.newton0 + NEWTON_COUNT)
            for n, b in enumerate(range(1, TB, 2)):
                act.activation(out_rows[:, b, :], out_rows[:, b, :], ACT.Copy, scale=n_y[:, b:b + 1]).then_inc(end_scaled_act, 1)
                act.wait_ge(end_scaled_act, n + 1)
                act.dma_start(out[0, b * P:(b + 1) * P, :], out_rows[:, b, :]).then_inc(out_sent, 16)

        @block.vector
        def _(dve):
            def rsqrt(x, y, t, mean_sq, d, steps, before):
                c = 3 / 8
                dve.tensor_scalar(x, mean_sq, 1.0 / d, EPS, ALU.mult, ALU.add).then_inc(steps, 1)
                dve.wait_ge(steps, before + 1)
                dve.tensor_scalar(y.bitcast(I32), x.bitcast(I32), -0.5, RSQRT_SEED, ALU.mult, ALU.add).then_inc(steps, 1)
                dve.wait_ge(steps, before + 2)
                dve.tensor_tensor(t, x, y, ALU.mult).then_inc(steps, 1)
                dve.wait_ge(steps, before + 3)
                dve.tensor_tensor(t, t, y, ALU.mult).then_inc(steps, 1)
                dve.wait_ge(steps, before + 4)
                dve.scalar_tensor_tensor(t, t, -10 / 3, t, ALU.add, ALU.mult).then_inc(steps, 1)
                dve.wait_ge(steps, before + 5)
                dve.scalar_tensor_tensor(y, t, 5.0, y, ALU.add, ALU.mult).then_inc(steps, 1)
                dve.wait_ge(steps, before + 6)
                dve.scalar_tensor_tensor(t, x, -0.5 * c ** 3, y, ALU.mult, ALU.mult).then_inc(steps, 1)
                dve.wait_ge(steps, before + 7)
                dve.tensor_tensor(t, t, y, ALU.mult).then_inc(steps, 1)
                dve.wait_ge(steps, before + 8)
                dve.scalar_tensor_tensor(y, t, 1.5 * c, y, ALU.add, ALU.mult).then_inc(steps, 1)
                dve.wait_ge(steps, before + NEWTON_COUNT)

            def zero(middle):
                return dve.tensor_scalar(middle, ones[:, 0:HD].unsqueeze(1).to_broadcast([P, TB, HD]), 0.0, None, ALU.mult)

            def newton(N, d, columns=slice(0, TB)):
                n = columns.stop - columns.start
                dve.wait_ge(norm.summed, N.sum0 + N.sums)
                rsqrt(n_x[:, 0:n], n_y[:, 0:n], n_t[:, 0:n], bank[SUMS][:, columns], d, norm.newton, N.newton0)

            def remainder(X, k, name):
                dve.wait_ge(X.hi, X.first + k + 1)
                dve.scalar_tensor_tensor(xl[:, k, :], h[:, k, :], gain(name, k), xh[:, k, :].bitcast(F32),
                                         ALU.mult, ALU.subtract).then_inc(X.lo, 1)

            def add_squares(N, k, i=None):
                r = N.chunk0 + k
                dve.wait_ge(norm.squares, r + 1 if i is None else 2 * i + (r + 1))
                if k == 0 and i is None:
                    dve.tensor_copy(square_sum[:], squares[:, r % 2, :]).then_inc(norm.added, 1)
                else:
                    dve.wait_ge(norm.added, N.add0 + k if i is None else 2 * i + (N.add0 + k))
                    dve.tensor_tensor(square_sum[:], square_sum[:], squares[:, r % 2, :], ALU.add).then_inc(norm.added, 1)

            def residual_term(R, NP, post, k):
                if k == 0:
                    dve.wait_ge(norm.spread, NP.spread0 + 1)
                dve.scalar_tensor_tensor(wa[:, k % 2, :], f[:, k, :], gain(post, k), bank[SPREAD][:],
                                         ALU.mult, ALU.mult).then_inc(R.term, 1)

            def residual_sum(R, factor, k):
                dve.wait_ge(R.term, R.first + k + 1)
                dve.scalar_tensor_tensor(h[:, k, :], wa[:, k % 2, :], factor, h[:, k, :], ALU.mult, ALU.add).then_inc(R.h, 1)

            def residual(R, NP, post, factor, X, pre, N):
                newton(NP, D)
                for k in range(KC):
                    residual_term(R, NP, post, k)
                    if k >= 1:
                        remainder(X, k - 1, pre)
                    residual_sum(R, factor, k)
                    if k >= 1:
                        add_squares(N, k - 1)
                remainder(X, KC - 1, pre)
                add_squares(N, KC - 1)

            def feed_forward(name, S, N, NP):
                newton(N, D)
                dve.wait_ge(norm.scale, N.scale0 + 1)
                u = FIRST[name + "_up_a"]

                def pair(u, j, i, n):
                    c = n % 2

                    def at(v):
                        return 2 * i + (S.hid0 + v)
                    dve.wait_ge(unit_used, done(u, i))
                    dve.tensor_tensor(wa[:, c, :], bank[2 * c][:], scale[:], ALU.mult).then_inc(ffn.gate, 1)
                    dve.wait_ge(unit_used, done(u + 1, i))
                    dve.tensor_tensor(wb[:, c, :], bank[2 * c + 1][:], scale[:], ALU.mult).then_inc(ffn.up, 1)
                    dve.wait_ge(ffn.silu, at(j + 1))
                    dve.wait_ge(ffn.up, at(j + 1))
                    dve.tensor_tensor(wb[:, c, :], wb[:, c, :], wa[:, c, :], ALU.mult).then_inc(ffn.prod, 1)
                    dve.wait_ge(ffn.hid.hi, at(j + 1))
                    h_, l_ = (hid_h[:, n, :], hid_l[:, n, :]) if i is None else (hid_h[:, 2 * i + n, :], hid_l[:, 2 * i + n, :])
                    dve.tensor_tensor(l_, wb[:, c, :], h_.bitcast(F32), ALU.subtract).then_inc(ffn.hid.lo, 1)

                with dve.Fori(0, FF_A // 2) as i:
                    for c in range(2):
                        pair(u + 2 * c, c, i, c)
                u = FIRST[name + "_down_a"]
                with dve.Fori(0, KC // 2) as i:
                    for m in range(2):
                        dve.wait_ge(unit_used, done(u + 2 * m + 1, i))
                        dve.tensor_copy(f[:, 2 * i + m, :], bank[4 + m][:]).then_inc(ffn.part, 1)
                u = FIRST[name + "_up_b"]
                with dve.Fori(0, FF_B // 2) as i:
                    for c in range(2):
                        pair(u + 2 * c, FF_A + c, i, c)
                u = FIRST[name + "_down_b"]
                dve.wait_ge(ffn.part, S.out0 + KC)
                for m in range(KC):
                    if m >= 1:
                        add_squares(NP, m - 1)
                    dve.wait_ge(unit_used, done(u + m))
                    dve.tensor_tensor(f[:, m, :], bank[4 + m % 2][:], f[:, m, :], ALU.add).then_inc(ffn.full, 1)

            def attention(A, blocks, find_top, blocks_of_keys, p_h, p_l, outputs, lead=None):
                lo, hi_ = blocks
                for n in range(lo, hi_ + 6):
                    if lead is not None:
                        lead(n)
                    if n < hi_:
                        r = A.block0 + n
                        dve.wait_ge(att.logits, r + 1)
                        find_top(n, r).then_inc(att.top, 1)
                    m, r = n - 1, A.block0 + n - 1
                    if lo <= m < hi_:
                        c = slice(r % 4, r % 4 + 1)
                        dve.wait_ge(att.exp, r + 1)
                        dve.reciprocal(invs[:, c], sums[:, c]).then_inc(att.inv, 1)
                    m, r = n - 4, A.block0 + n - 4
                    if lo <= m < hi_:
                        w, g = blocks_of_keys(m), A.half0 + m // 2
                        part = (slice(None), g % 2, slice(0, w), slice(m % 2 * P, (m % 2 + 1) * P))
                        dve.wait_ge(att.pt.hi, r + 1)
                        dve.tensor_tensor(p_l[part], bank[3 + m % 2][:, 0:w * P].rearrange("p (s q) -> p s q", q=P),
                                          p_h[part].bitcast(F32), ALU.subtract).then_inc(att.pt.lo, 1)
                    if (n - 7) % 2 == 0 and lo <= n - 7 < hi_:
                        for piece, to, src, top_ in outputs((n - 7) // 2):
                            dve.wait_ge(att.out.hi, A.piece0 + piece + 1)
                            dve.tensor_tensor(to, src, top_.bitcast(F32), ALU.subtract).then_inc(att.out.lo, 1)

            def plain_top(width):
                return lambda n, r: dve.tensor_reduce(top[:, r % 4:r % 4 + 1], bank[n % 3][:, 0:width], AX.X, ALU.max, negate=True)

            def paired(o_h, o_l):
                def outputs(g):
                    head, half = g // 2, g % 2
                    if head % 2 == 0:
                        return []
                    part = (slice(None), head // 2, slice(half * 256, (half + 1) * 256))
                    return [(head // 2 * 2 + half, o_l[part], bank[5 + half][:, 0:256], o_h[part])]
                return outputs

            dve.wait_ge(gains_in, 16)
            for k in range(KC):
                dve.wait_ge(x_turned, k + 1)
                dve.tensor_copy(h[:, k, :], bank[k][:]).then_inc(x_kept, 1)
            for k in range(KC):
                remainder(x_ffn1, k, "ffn1_pre_g")
                add_squares(n_ffn1, k)
            feed_forward("ffn1", ffn1, n_ffn1, n_ffn1p)
            residual(r_ffn1, n_ffn1p, "ffn1_post_g", 0.5, x_mix, "mix_pre_g", n_mix)

            def rope_x(r):
                if r >= 2:
                    dve.wait_ge(rope.rot, r - 1)
                u = FIRST["index"] + r if r < 5 else FIRST["queries"] + r - 5
                dve.wait_ge(unit_used, done(u))
                dve.tensor_tensor(wa[:, r % 2, :], bank[7 if r == 4 else r % 4][:], scale[:], ALU.mult).then_inc(rope.x, 1)
                dve.wait_ge(rope.x, r + 1)
                dve.tensor_tensor(wb[:, r % 2, :], wa[:, r % 2, :], tab[:, 0, :], ALU.mult).then_inc(rope.cos, 1)

            def rope_sum(r):
                dve.wait_ge(rope.rot, r + 1)
                dve.wait_ge(rope.cos, r + 1)
                dve.tensor_tensor(wa[:, r % 2, :], bank[4 + r % 2][:], tab[:, 1, :], ALU.mult).then_inc(rope.sin, 1)
                dve.wait_ge(rope.sin, r + 1)
                dve.tensor_tensor(wb[:, r % 2, :], wb[:, r % 2, :], wa[:, r % 2, :], ALU.add).then_inc(rope.sum, 1)

            def rope_lo(r):
                if r < 4:
                    a, b, s = qi_l[:, r, :], qi_h[:, r, :], 1.0
                elif r == 4:
                    a, b, s = ki_l[:], ki_h[:], 1.0
                elif r < 9:
                    a, b, s = qa_l[:, r - 5, :], qa_h[:, r - 5, :], HD ** -0.5
                else:
                    a, b, s = ka_l[:], ka_h[:], 1.0
                dve.wait_ge(rope.out.hi, r + 1)
                dve.scalar_tensor_tensor(a, wb[:, r % 2, :], s, b.bitcast(F32), ALU.mult, ALU.subtract).then_inc(rope.out.lo, 1)

            newton(n_mix, D)
            dve.wait_ge(norm.scale, n_mix.scale0 + 1)
            dve.wait_ge(tab_in, 16)
            width = HD + HEADS
            turned = bank[6][:, 0:TB * width].rearrange("p (b c) -> p b c", c=width)
            for r in range(10):
                if r >= 2:
                    rope_lo(r - 2)
                rope_x(r)
                if r == 3:
                    dve.wait_ge(unit_used, done(FIRST["values"]))
                    dve.tensor_tensor(v_cols[0:width, :], bank[6][0:width, :], scale[0:width, :], ALU.mult).then_inc(v_scaled, 1)
                if r >= 1:
                    rope_sum(r - 1)
                if r == 4:
                    zero(va_h[:, :, HD:P])
                    zero(va_l[:, :, HD:P]).then_inc(v_zero, 1)
                    dve.wait_ge(v_split.hi, 2)
                    dve.tensor_scalar(w_idx[:], turned[:, :, HD:width], HEADS ** -0.5 * HD ** -0.5, None,
                                      ALU.mult).then_inc(v_scaled, 1)
                    for par in range(2):
                        part = (slice(None), slice(None), slice(par * P, par * P + HD))
                        dve.tensor_tensor(va_l[part], turned[:, :, 0:HD], va_h[part].bitcast(F32),
                                          ALU.subtract).then_inc(v_split.lo, 1)
            rope_lo(8)
            rope_sum(9)
            rope_lo(9)

            dve.wait_ge(v_scaled, 2)
            for n in range(3 * HEADS):
                b, head = n // HEADS + 1, n % HEADS
                score, relu, w = mask_of(b), probs[:, n % 3, 0:(b + 1) * P], w_idx[:, b, head:head + 1]
                dve.wait_ge(idx_relu, n + 1)
                if head == 0:
                    dve.tensor_scalar(score, relu, w, None, ALU.mult).then_inc(idx_sum, 1)
                else:
                    dve.wait_ge(idx_sum, IDX_SUM[n] - 1)
                    dve.scalar_tensor_tensor(score, relu, w, score, ALU.mult, ALU.add).then_inc(idx_sum, 1)
                if head == HEADS - 1:
                    dve.wait_ge(idx_sum, IDX_SUM[n])
                    own = score[:, b * P:(b + 1) * P]
                    dve.scalar_tensor_tensor(own, after_query, NOT_CAUSAL, own, ALU.mult, ALU.add).then_inc(idx_sum, 1)
            dve.tensor_scalar(mask_of(0), after_query, MASKED, None, ALU.mult).then_inc(masked, 1)

            def search(n):
                score = mask_of(n // (TOP_K // 8) + 1)
                if n:
                    dve.wait_ge(taken, 2 * n)
                else:
                    dve.wait_ge(idx_sum, 3 * (HEADS + 1))
                dve.max(best8[:], score).then_inc(taken, 1)
                dve.wait_ge(taken, 2 * n + 1)
                dve.match_replace(score, best8[:], score, REPLACED).then_inc(taken, 1)
                if (n + 1) % (TOP_K // 8) == 0:
                    dve.wait_ge(taken, 2 * n + 2)
                    dve.tensor_scalar(score, score, REPLACED, MASKED, ALU.not_equal, ALU.mult).then_inc(masked, 1)

            dve.memset(c_y[:, :, 0:2], 0.0).then_inc(v_zero, 1)
            dve.wait_ge(v_zero, 2)
            u = FIRST["conv"]
            for j in range(4):
                c, banks, s0 = j % 2, CONV_BANKS[j % 2], 7 * j
                y, z = c_y[:, c, :], c_z[:, c, :]
                for q, to in enumerate((c_gb[:, c, :], c_gc[:, c, :], y[:, 2:2 + T])):
                    dve.wait_ge(unit_used, done(u + 3 * j + q))
                    dve.tensor_tensor(to, bank[banks[q]][:], scale[:], ALU.mult).then_inc(conv_step, 1)
                dve.wait_ge(conv_step, s0 + 3)
                dve.tensor_tensor(y[:, 2:2 + T], y[:, 2:2 + T], c_gc[:, c, :], ALU.mult).then_inc(conv_step, 1)
                dve.wait_ge(conv_step, s0 + 4)
                dve.wait_ge(conv_tap, j + 1)
                for n, tap in enumerate((1, 0)):
                    dve.scalar_tensor_tensor(z, y[:, tap:tap + T], gain_row(CONV_ROW + 4 * tap + j), z,
                                             ALU.mult, ALU.add).then_inc(conv_step, 1)
                    dve.wait_ge(conv_step, s0 + 5 + n)
                dve.tensor_tensor(z, z, c_gb[:, c, :], ALU.mult).then_inc(conv_step, 1)
                dve.wait_ge(conv_out.hi, j + 1)
                dve.tensor_tensor(cz_l[:, j, :], z, cz_h[:, j, :].bitcast(F32), ALU.subtract).then_inc(conv_out.lo, 1)
                for n in range(SEARCHED[j - 1] if j else 0, SEARCHED[j]):
                    search(n)
            for p in range(4):
                b0 = 4 * ((p + 1) % 2)
                for q in range(2):
                    dve.wait_ge(unit_used, done(merge_conv_unit(p, q)))
                    if p >= 1:
                        dve.wait_ge(mc_sum, 2 * p)
                    dve.tensor_tensor(wa[:, q, :], bank[b0 + 2 + q][:], scale[:], ALU.mult).then_inc(mc_gate, 1)
                dve.wait_ge(unit_used, done(merge_conv_unit(p, 2)))
                for q in range(2):
                    m = 2 * p + q
                    dve.wait_ge(mc_sig, m + 1)
                    dve.tensor_tensor(mixed[:, m, :], bank[b0 + q][:], wa[:, q, :], ALU.mult).then_inc(mc_sum, 1)
                for n in range(SEARCHED_2[p - 1] if p else SEARCHED[-1], SEARCHED_2[p]):
                    search(n)

            def masked_top(n, r):
                b = n % TB
                if n >= 2:
                    dve.wait_ge(att.exp, r - 1)
                w = (b + 1) * P
                return dve.tensor_tensor_reduce(wb[:, n % 2, 0:w], bank[n % 3][:, 0:w], mask_of(b), -1.0, 3.0e38,
                                                ALU.add, ALU.min, top[:, r % 4:r % 4 + 1])

            dve.wait_ge(masked, TB)
            def main_gate(n):
                if n % TB == TB - 1 and n < HB:
                    m = n // TB
                    dve.wait_ge(unit_used, done(FIRST["gate_a"] + m))
                    dve.tensor_tensor(gate_a[:, m, :], bank[7][:], scale[:], ALU.mult).then_inc(ga_scaled, 1)

            attention(a_main, (0, HB), masked_top, lambda n: n % TB + 1, a_pt_h, a_pt_l, paired(qa_h, qa_l), main_gate)

            def mixed_lo(m):
                dve.wait_ge(merged.hi, m + 1)
                dve.tensor_tensor(mm_l[:, m, :], mixed[:, m, :], mm_h[:, m, :].bitcast(F32), ALU.subtract).then_inc(merged.lo, 1)

            dve.wait_ge(mem_sum, MB)
            rsqrt(n_x[:, 0:MB], n_y[:, 0:MB], n_t[:, 0:MB], mem_sq[:], D, n_mem, 0)
            for b in range(MB):
                dve.tensor_scalar(mem_rows[:, b, :], mem_rows[:, b, :], n_y[:, b:b + 1], None, ALU.mult).then_inc(mem_normed, 1)
            for m in range(KC):
                c = m % 2
                dve.wait_ge(unit_used, done(FIRST["attn_out"] + m // 2))
                dve.wait_ge(ga_sig, m + 1)
                dve.tensor_tensor(wa[:, c, :], bank[m][:], gate_a[:, m, :], ALU.mult).then_inc(ma_term, 1)
                dve.wait_ge(ma_term, m + 1)
                dve.tensor_tensor(mixed[:, m, :], mixed[:, m, :], wa[:, c, :], ALU.add).then_inc(ma_sum, 1)
                if m >= 1:
                    mixed_lo(m - 1)
            mixed_lo(KC - 1)
            for k in range(KC):
                dve.wait_ge(memt.hi, k // 2 * 2 + 2)
                dve.scalar_tensor_tensor(memt_l[:, k, :], bank[k // 2][:, k % 2 * N_MEM:(k % 2 + 1) * N_MEM], gain("mem_g", k),
                                         memt_h[:, k, :].bitcast(F32), ALU.mult, ALU.subtract).then_inc(memt.lo, 1)

            def out_chunks(u, NP):
                for m in range(KC):
                    if m >= 1:
                        add_squares(NP, m - 1)
                    dve.wait_ge(unit_used, done(u + m))
                    dve.tensor_copy(f[:, m, :], bank[4 + m % 2][:]).then_inc(out_full, 1)

            out_chunks(FIRST["mix_out"], n_mixp)

            def mem_key(m):
                dve.wait_ge(mk.hi, m + 1)
                dve.tensor_tensor(mk_l[:, m, :], bank[m % 4][:, 0:N_MEM], mk_h[:, m, :].bitcast(F32), ALU.subtract).then_inc(mk.lo, 1)

            newton(n_mixp, D)
            for m in range(3):
                mem_key(m)
            for k in range(KC):
                residual_term(r_mix, n_mixp, "mix_post_g", k)
                if k >= 1:
                    remainder(x_x, k - 1, "xattn_pre_g")
                residual_sum(r_mix, 1.0, k)
                if k + 3 < KC:
                    mem_key(k + 3)
                if k >= 1:
                    add_squares(n_xq, k - 1)
            remainder(x_x, KC - 1, "xattn_pre_g")
            add_squares(n_xq, KC - 1)
            for c in range(2):
                for b in range(MB):
                    part = (slice(None), b, slice(c * T, (c + 1) * T))
                    dve.wait_ge(mv.hi, 2 * c + b + 1)
                    dve.tensor_tensor(mv_l[part], bank[(4, 0)[c] + b][:], mv_h[part].bitcast(F32), ALU.subtract).then_inc(mv.lo, 1)
            newton(n_xq, D)
            dve.wait_ge(norm.scale, n_xq.scale0 + 1)
            def query_scaled(m, source):
                dve.wait_ge(unit_used, done(FIRST["x_q"] + m))
                if m >= 2:
                    dve.wait_ge(xq.lo, m - 1)
                dve.scalar_tensor_tensor(wb[:, m % 2, :], source[:], XD ** -0.5, scale[:], ALU.mult, ALU.mult).then_inc(xq_scaled, 1)

            def query_lo(m):
                dve.wait_ge(xq.hi, m + 1)
                dve.tensor_tensor(xq_l[:, m, :], wb[:, m % 2, :], xq_h[:, m, :].bitcast(F32), ALU.subtract).then_inc(xq.lo, 1)

            for m in range(5):
                if m < 4:
                    query_scaled(m, bank[(2 + m) % 4])
                if m >= 1:
                    query_lo(m - 1)

            def mem_pieces(g):
                out = []
                for c in range(2):
                    part = (slice(None), g // 2 * 2 + c, slice(g % 2 * 256, (g % 2 + 1) * 256))
                    out.append((2 * g + c, xq_l[part], bank[5 + c][:, 0:256], xq_h[part]))
                return out

            def late_queries(n):
                if n - 1 in LATE_QUERIES:
                    query_scaled(4 + LATE_QUERIES.index(n - 1), bank[7])
                if n - 2 in LATE_QUERIES:
                    query_lo(4 + LATE_QUERIES.index(n - 2))

            attention(a_mem, (0, XH * TB), plain_top(N_MEM), lambda n: MB, x_pt_h, x_pt_l, mem_pieces, late_queries)
            out_chunks(FIRST["x_out"], n_xp)
            residual(r_x, n_xp, "xattn_post_g", 1.0, x_ffn2, "ffn2_pre_g", n_ffn2)

            feed_forward("ffn2", ffn2, n_ffn2, n_ffn2p)
            residual(r_ffn2, n_ffn2p, "ffn2_post_g", 0.5, x_mix2, "g_mix_2", n_mix2)

            newton(n_mix2, D)
            dve.wait_ge(norm.scale, n_mix2.scale0 + 1)
            for r in range(6):
                dve.wait_ge(unit_used, done(FIRST["grouped"] + r))
                dve.tensor_tensor(g_x[:, r, :], bank[r % 4][:], scale[:], ALU.mult).then_inc(gx.x, 1)
            for kv in range(2):
                zero(gv_h[:, kv, :, HD:P])
                zero(gv_l[:, kv, :, HD:P]).then_inc(v_zero, 1)
            dve.wait_ge(unit_used, done(FIRST["grouped"] + 6))
            dve.tensor_tensor(g_v[:], bank[6][:], scale[:], ALU.mult).then_inc(gv_scaled, 1)
            newton(n_heads, HD, slice(0, 12 * TB))
            by_head = n_y[:, 0:12 * TB].rearrange("p (b c) -> p b c", c=12)

            def lay_out_heads(n):
                r = GROUPED_ORDER[n]
                dve.tensor_copy(expand.rearrange("p b (h c) -> p b h c", c=HD),
                                by_head[:, :, 2 * r:2 * r + 2].unsqueeze(3).to_broadcast([P, TB, 2, HD])).then_inc(heads_laid, 1)

            lay_out_heads(0)
            turned_g = bank[6][:].rearrange("p (b c) -> p b c", c=P)

            def grouped_value_lo(n):
                kv, par = n // 2, n % 2
                part = (slice(None), kv, slice(None), slice(par * P, par * P + HD))
                dve.wait_ge(gv.hi, 4)
                dve.tensor_tensor(gv_l[part], turned_g[:, :, kv * HD:(kv + 1) * HD], gv_h[part].bitcast(F32),
                                  ALU.subtract).then_inc(gv.lo, 1)
            dve.wait_ge(tab_in, 32)

            def grouped_sum(n):
                r = GROUPED_ORDER[n]
                dve.wait_ge(gx.rot, n + 1)
                dve.tensor_tensor(g_x[:, r, :], bank[n % 2][:], tab[:, 1, :], ALU.mult).then_inc(gx.sin, 1)
                dve.wait_ge(gx.sin, n + 1)
                dve.tensor_tensor(wb[:, n % 2, :], wb[:, n % 2, :], g_x[:, r, :], ALU.add).then_inc(gx.sum, 1)

            def grouped_lo(n):
                r = GROUPED_ORDER[n]
                a, b, s = (gq_l[:, r, :], gq_h[:, r, :], HD ** -0.5) if r < 4 else (gk_l[:, r - 4, :], gk_h[:, r - 4, :], 1.0)
                dve.wait_ge(gx.out.hi, n + 1)
                dve.scalar_tensor_tensor(a, wb[:, n % 2, :], s, b.bitcast(F32), ALU.mult, ALU.subtract).then_inc(gx.out.lo, 1)

            def gate(g, source):
                dve.wait_ge(unit_used, done(gate_unit(g)))
                if g:
                    dve.wait_ge(gate_out, 16 * g)
                dve.tensor_tensor(gate_stage[:], bank[source][:], scale[:], ALU.mult).then_inc(gate_scaled, 1)

            for n, r in enumerate(GROUPED_ORDER):
                if n >= 2:
                    grouped_lo(n - 2)
                dve.wait_ge(norm.spread, n_heads.spread0 + n + 1)
                if n + 1 < 6:
                    lay_out_heads(n + 1)
                dve.scalar_tensor_tensor(g_x[:, r, :], g_x[:, r, :], gain_row(G_QN_ROW if r < 4 else G_KN_ROW),
                                         bank[4 + n % 2][:], ALU.mult, ALU.mult).then_inc(gx_normed, 1)
                dve.wait_ge(gx_normed, n + 1)
                dve.tensor_tensor(wb[:, n % 2, :], g_x[:, r, :], tab[:, 0, :], ALU.mult).then_inc(gx.cos, 1)
                gate(n, 2 + n % 2)
                if n < 4:
                    grouped_value_lo(n)
                if n >= 1:
                    grouped_sum(n - 1)
            grouped_lo(4)
            grouped_sum(5)
            grouped_lo(5)
            attention(a_grp, (0, HB), plain_top(T), lambda n: TB, g_pt_h, g_pt_l, paired(go_h, go_l),
                      lambda n: gate({1: 6, 6: 7}[n], 7) if n in (1, 6) else None)

            u = FIRST["latent"]
            for r in range(3):
                dve.wait_ge(unit_used, done(u + r))
                dve.tensor_tensor(l_x[:, r, :], bank[r][:], scale[:], ALU.mult).then_inc(lx, 1)
            dve.wait_ge(unit_used, done(u + 3))
            dve.tensor_tensor(l_x[:, 3, :], bank[3][:], scale[:], ALU.mult).then_inc(kpe.x, 1)
            add_squares(n_cq, 0)
            newton(n_cq, LAT_Q)
            dve.wait_ge(lx, 3)
            dve.wait_ge(norm.spread, n_cq.spread0 + 1)
            for k in range(2):
                dve.scalar_tensor_tensor(wb[:, k, :], l_x[:, k, :], gain_row(G_QA_ROW + k), bank[SPREAD][:],
                                         ALU.mult, ALU.mult).then_inc(l_normed, 1)
            newton(n_ckv, LAT_KV, slice(8, 8 + TB))
            dve.wait_ge(norm.spread, n_ckv.spread0 + 1)
            dve.scalar_tensor_tensor(wa[:, 0, :], l_x[:, 2, :], gain_row(G_KVA_ROW), bank[5][:],
                                     ALU.mult, ALU.mult).then_inc(l_normed, 1)
            dve.wait_ge(tab_in, 48)
            dve.wait_ge(kpe.x, 1)
            dve.tensor_tensor(wa[:, 1, :], l_x[:, 3, :], tab[:, 0, :], ALU.mult).then_inc(kpe.cos, 1)
            dve.wait_ge(kpe.rot, 1)
            dve.wait_ge(kpe.cos, 1)
            dve.tensor_tensor(l_x[:, 3, :], bank[4][:], tab[:, 1, :], ALU.mult).then_inc(kpe.sin, 1)
            dve.wait_ge(kpe.sin, 1)
            dve.tensor_tensor(wa[:, 1, :], wa[:, 1, :], l_x[:, 3, :], ALU.add).then_inc(kpe.sum, 1)
            gate(8, 2)
            for k in range(3):
                a, b, s = ((cq_l[:, 0, :], cq_h[:, 0, :], wb[:, 0, :]), (cq_l[:, 1, :], cq_h[:, 1, :], wb[:, 1, :]),
                           (ck_l[:], ck_h[:], wa[:, 0, :]))[k]
                dve.wait_ge(l_lat.hi, k + 1)
                dve.tensor_tensor(a, s, b.bitcast(F32), ALU.subtract).then_inc(l_lat.lo, 1)
            for q in range(2):
                dve.wait_ge(kpe.out.hi, q + 1)
                dve.tensor_tensor(lk_l[NOPE:QW, q, :], wa[NOPE:QW, 1, :], lk_h[NOPE:QW, q, :].bitcast(F32),
                                  ALU.subtract).then_inc(kpe.out.lo, 1)
            zero(lv_h[:, :, HD:P])
            zero(lv_l[:, :, HD:P]).then_inc(v_zero, 1)
            gate(9, 3)

            def pair_gates(c, n):
                if n == 1:
                    gate(PAIR_GATE[c], 7)
                if c in PAIR_GATE_2 and n == 6:
                    gate(PAIR_GATE_2[c], 7)
                if n == 2 * TB + 4 and c < 3:
                    pair_cos(c + 1)

            def pair_key(c, q):
                dve.wait_ge(lk.hi, 2 * c + q + 1)
                dve.tensor_tensor(lk_l[0:NOPE, q, :], bank[2 + q][0:NOPE, :], lk_h[0:NOPE, q, :].bitcast(F32),
                                  ALU.subtract).then_inc(lk.lo, 1)

            def pair_cos(c):
                for q in range(2):
                    dve.wait_ge(lq.x, 2 * c + q + 1)
                    dve.tensor_tensor(wb[0:QW, q, :], l_q[0:QW, q, :], tab[0:QW, 0, :], ALU.mult).then_inc(lq.cos, 1)
                pair_key(c, 0)

            pair_cos(0)
            for c in range(4):
                for q in range(2):
                    dve.wait_ge(lq.rot, 2 * c + q + 1)
                    dve.wait_ge(lq.cos, 2 * c + q + 1)
                    dve.tensor_tensor(l_q[0:QW, q, :], bank[q][0:QW, :], tab[0:QW, 1, :], ALU.mult).then_inc(lq.sin, 1)
                    dve.wait_ge(lq.sin, 2 * c + q + 1)
                    dve.tensor_tensor(wb[0:QW, q, :], wb[0:QW, q, :], l_q[0:QW, q, :], ALU.add).then_inc(lq.sum, 1)
                pair_key(c, 1)
                for q in range(2):
                    part = (slice(None), slice(None), slice(q * P, q * P + HD))
                    dve.wait_ge(lv.hi, 2 * c + 2)
                    dve.tensor_tensor(lv_l[part], bank[6][:].rearrange("p (s c) -> p s c", c=P)[:, :, q * HD:(q + 1) * HD],
                                      lv_h[part].bitcast(F32), ALU.subtract).then_inc(lv.lo, 1)
                for q in range(2):
                    dve.wait_ge(lq.out.hi, 2 * c + q + 1)
                    dve.scalar_tensor_tensor(lq_l[0:QW, q, :], wb[0:QW, q, :], QW ** -0.5, lq_h[0:QW, q, :].bitcast(F32),
                                             ALU.mult, ALU.subtract).then_inc(lq.out.lo, 1)
                attention(a_lat, (2 * TB * c, 2 * TB * (c + 1)), plain_top(T), lambda n: TB, l_pt_h, l_pt_l, paired(lo_h, lo_l),
                          lambda n: pair_gates(c, n - 2 * TB * c))

            def merged_lo(m):
                dve.wait_ge(merged.hi, KC + m + 1)
                dve.tensor_tensor(mg_l[:, m, :], wa[:, m % 2, :], mg_h[:, m, :].bitcast(F32), ALU.subtract).then_inc(merged.lo, 1)

            for m in range(KC):
                c, b0 = m % 2, 4 * (m // 2 % 2)
                dve.wait_ge(unit_used, done(FIRST["merge"] + m // 2 * 2 + 1))
                dve.wait_ge(gate_sig, m + 1)
                if m >= 2:
                    dve.wait_ge(merged.lo, KC + m - 1)
                for n, t in enumerate((wa, wb)):
                    dve.tensor_tensor(t[:, c, :], bank[b0 + 2 * n + c][:], gates_back[:, m % 4, n, :], ALU.mult).then_inc(me_term, 1)
                dve.wait_ge(me_term, 2 * m + 2)
                dve.tensor_tensor(wa[:, c, :], wa[:, c, :], wb[:, c, :], ALU.add).then_inc(me_sum, 1)
                if m >= 1:
                    merged_lo(m - 1)
            merged_lo(KC - 1)
            for m in range(KC):
                dve.wait_ge(unit_used, done(FIRST["out"] + m))
                dve.tensor_tensor(h[:, m, :], bank[1 + m % 3][:], h[:, m, :], ALU.add).then_inc(h_out, 1)
                if m >= 1:
                    remainder(x_mlp, m - 1, "g_mlp_2")
                    add_squares(n_mlp, m - 1)
            remainder(x_mlp, KC - 1, "g_mlp_2")
            add_squares(n_mlp, KC - 1)
            for k in range(2):
                dve.wait_ge(p_split.hi, k + 1)
                dve.tensor_tensor(pt_l[:, k, :], bank[4 + k][:], pt_h[:, k, :].bitcast(F32), ALU.subtract).then_inc(p_split.lo, 1)
            newton(n_mlp, D)
            dve.wait_ge(norm.scale, n_mlp.scale0 + 1)

            def mlp_up(first, j0, i):
                for q in range(RING):
                    c = q % 2
                    dve.wait_ge(unit_used, done(first + q, i))
                    dve.tensor_tensor(wa[:, c, :], bank[q][:], scale[:], ALU.mult).then_inc(ml_x, 1)
                    dve.wait_ge(ml_x, 4 * i + (j0 + q + 1))
                    dve.scalar_tensor_tensor(wb[:, c, :], wa[:, c, :], 0.0, wa[:, c, :], ALU.max, ALU.mult).then_inc(ml_sq, 1)
                    dve.wait_ge(ml_hid.hi, 4 * i + (j0 + q + 1))
                    dve.tensor_tensor(hid_l[:, 4 * i + q, :], wb[:, c, :], hid_h[:, 4 * i + q, :].bitcast(F32),
                                      ALU.subtract).then_inc(ml_hid.lo, 1)

            def mlp_down(first, kept, i, split, opening=False):
                for m in range(2):
                    dve.wait_ge(unit_used, done(first + 2 * m + 1, i))
                    x = h[:, 2 * i + m, :]
                    dve.tensor_tensor(x, bank[4 + m][:], x, ALU.add).then_inc(kept, 1)
                    if split:
                        row = GAINS.index("g_ple_2") * KC + m
                        dve.wait_ge(x_ple.hi, 2 * i + (x_ple.first + m + 1))
                        dve.scalar_tensor_tensor(xl[:, 2 * i + m, :], x, gains[:, bass.ds(2 * i + row, 1)],
                                                 xh[:, 2 * i + m, :].bitcast(F32), ALU.mult, ALU.subtract).then_inc(x_ple.lo, 1)
                        add_squares(n_ple, m, None if opening else i)

            with dve.Fori(0, FF2_HALF // RING) as i:
                mlp_up(FIRST["mlp_up_a"], 0, i)
            with dve.Fori(0, KC // 2) as i:
                mlp_down(FIRST["mlp_down_a"], ml_part, i, False)
            with dve.Fori(0, FF2_HALF // RING) as i:
                mlp_up(FIRST["mlp_up_b"], FF2_HALF, i)
            dve.wait_ge(ml_part, KC)
            mlp_down(FIRST["mlp_down_b"], h_mlp, 0, True, opening=True)
            with dve.Fori(1, KC // 2) as i:
                mlp_down(FIRST["mlp_down_b"], h_mlp, i, True)

            newton(n_ple, D)
            dve.wait_ge(norm.scale, n_ple.scale0 + 1)
            for m in range(KC):
                c = m % 2
                dve.wait_ge(unit_used, done(FIRST["ple_gate"] + m))
                dve.tensor_tensor(wa[:, c, :], bank[2 + c][:], scale[:], ALU.mult).then_inc(pg_x, 1)
                dve.wait_ge(pg_sig, m + 1)
                dve.wait_ge(ple_kept, m + 1)
                dve.tensor_tensor(wb[:, c, :], wa[:, c, :], ple[:, m, :], ALU.mult).then_inc(pg_term, 1)
                dve.wait_ge(pg_term, m + 1)
                dve.tensor_tensor(h[:, m, :], h[:, m, :], wb[:, c, :], ALU.add).then_inc(h_end, 1)
                if m >= 1:
                    add_squares(n_end, m - 1)
            newton(n_end, D)
            dve.wait_ge(end_kept, KC)
            for b in range(0, TB, 2):
                dve.tensor_scalar(out_rows[:, b, :], out_rows[:, b, :], n_y[:, b:b + 1], None, ALU.mult).then_inc(end_scaled, 1)


INPUTS = ["x", "mem", "ffn1_pre_g", "ffn1_post_g", "ffn1_w1", "ffn1_w3", "ffn1_w2", "mix_pre_g", "mix_post_g", "w_in",
          "conv_w", "w_a_out", "w_b_out", "w_out", "mem_g", "xattn_pre_g", "xattn_post_g", "xattn_w_q", "xattn_w_kv",
          "xattn_w_o", "ffn2_pre_g", "ffn2_post_g", "ffn2_w1", "ffn2_w3", "ffn2_w2", "p_2", "g_mix_2", "w_in_2", "g_qa_2",
          "w_qb_2", "g_kva_2", "w_kvb_2", "g_qn_2", "g_kn_2", "w_oa_2", "w_ob_2", "w_o_2", "g_mlp_2", "w_up_2", "w_down_2",
          "g_ple_2", "w_ple_gate_2", "w_ple_2", "g_final_2"]


def kernel(**inputs):
    import concourse.bacc as bacc
    from concourse.bass_utils import run_bass_kernel_spmd

    nc = bacc.Bacc("TRN2", target_bir_lowering=False, num_devices=1)
    arrays = {f"in_{name}": np.ascontiguousarray(inputs[name]) for name in INPUTS}
    vectors = [inputs[name] for name in GAINS] + [inputs["g_qa_2"], inputs["g_kva_2"], inputs["conv_w"]]
    vectors += [inputs[name] for name in ("g_qn_2", "g_kn_2") for _ in range(2)]
    columns = np.concatenate([np.ravel(v) for v in vectors]).reshape(GAIN_ROWS, P).T
    arrays["in_gain_columns"] = np.ascontiguousarray(columns)
    mats, tabs = shape_constants()
    arrays["in_shape_mats"] = np.ascontiguousarray(mats.reshape(P, -1))
    arrays["in_shape_tabs"] = np.ascontiguousarray(tabs.reshape(P, -1))
    dram = {name[3:]: nc.dram_tensor(name, a.shape, mybir.dt.from_np(a.dtype), kind="ExternalInput").ap()
            for name, a in arrays.items()}
    out = nc.dram_tensor("out_0", (1, T, D), F32, kind="ExternalOutput").ap()
    build(nc, dram, out)
    result = run_bass_kernel_spmd(nc, [arrays], core_ids=[0])
    return result.results[0]["out_0"]
```
